# Optimizing a Trainium2 kernel written in Bass

```python
import math
import jax
import jax.numpy as jnp
from jax import lax
import numpy as np
import jax, jax.numpy as jnp

D_MODEL = 2048
BATCH = 1
SEQ = 256
DEPTH = 1

HEAD_DIM = 128
NSA_HEADS = 8
NSA_KV_HEADS = 2
CMP_LEN = 32
CMP_STRIDE = 16
CMP_HIDDEN = 2 * HEAD_DIM
SEL_BLOCK = 64
SEL_TOP_N = 16
NSA_WINDOW = 512
NSA_Q_CHUNK = 64
SWA_HEADS = 8
SWA_KV_HEADS = 2
SWA_WINDOW = 128
MOBA_HEADS = 8
MOBA_KV_HEADS = 2
MOBA_BLOCK = 256
MOBA_TOP_K = 3
MOBA_Q_CHUNK = 16
BAND_BLOCK = 128
N_BUCKETS = 32
BUCKET_MAX_DIST = 128
TOTAL_HEADS = NSA_HEADS + SWA_HEADS + MOBA_HEADS
N_BRANCHES = 3
MIX_WIDTH = NSA_HEADS * HEAD_DIM
D_FF = 4 * D_MODEL
RMS_EPS = 1e-6
NEG_INF = -1e30
FORCE_SCORE = 1e30
TINY = 1e-30

SPLIT_SIZES = (
    NSA_HEADS * HEAD_DIM,
    NSA_KV_HEADS * HEAD_DIM,
    NSA_KV_HEADS * HEAD_DIM,
    NSA_KV_HEADS * HEAD_DIM,
    NSA_KV_HEADS * HEAD_DIM,
    NSA_KV_HEADS * HEAD_DIM,
    NSA_KV_HEADS * HEAD_DIM,
    NSA_HEADS * 3,
    SWA_HEADS * HEAD_DIM,
    SWA_KV_HEADS * HEAD_DIM,
    SWA_KV_HEADS * HEAD_DIM,
    MOBA_HEADS * HEAD_DIM,
    MOBA_KV_HEADS * HEAD_DIM,
    MOBA_KV_HEADS * HEAD_DIM,
    N_BRANCHES * D_MODEL,
)
SPLIT_POINTS = tuple(int(v) for v in np.cumsum(SPLIT_SIZES)[:-1])
D_IN = sum(SPLIT_SIZES)


def rms_norm(x, gain):
    x32 = x.astype(jnp.float32)
    y = x32 * lax.rsqrt(jnp.mean(x32 * x32, axis=-1, keepdims=True) + RMS_EPS)
    return (y * gain.astype(jnp.float32)).astype(x.dtype)

def t5_bucket(dist):
    n = jnp.maximum(dist, 0)
    exact = N_BUCKETS // 2
    log_ratio = jnp.log(jnp.maximum(n, 1).astype(jnp.float32) / exact) / math.log(BUCKET_MAX_DIST / exact)
    large = jnp.minimum(exact + (log_ratio * (N_BUCKETS - exact)).astype(jnp.int32), N_BUCKETS - 1)
    return jnp.where(n < exact, n, large)

def masked_softmax(logits, mask, sink=None):
    logits = jnp.where(mask, logits, NEG_INF)
    m = jnp.max(logits, axis=-1, keepdims=True)
    if sink is not None:
        m = jnp.maximum(m, sink)
    p = jnp.where(mask, jnp.exp(logits - m), 0.0)
    denom = jnp.sum(p, axis=-1, keepdims=True)
    if sink is not None:
        denom = denom + jnp.exp(sink - m)
    return p / jnp.maximum(denom, TINY)

def split_heads(t, n_heads):
    return t.reshape(t.shape[0], t.shape[1], n_heads, HEAD_DIM)

def banded_attention(q, k, v, bias_tbl, window, sinks=None):
    b, s, h, d = q.shape
    n_kv = k.shape[2]
    g = h // n_kv
    nb = s // BAND_BLOCK
    pad = -(-(window - 1) // BAND_BLOCK) * BAND_BLOCK
    span = BAND_BLOCK + pad
    key_idx = jnp.arange(nb)[:, None] * BAND_BLOCK + jnp.arange(span)[None, :]
    padding = ((0, 0), (pad, 0), (0, 0), (0, 0))
    kp = jnp.pad(k, padding)[:, key_idx]
    vp = jnp.pad(v, padding)[:, key_idx]
    qb = q.reshape(b, nb, BAND_BLOCK, n_kv, g, d)
    logits = jnp.einsum('bnqkgd,bnlkd->bnkgql', qb, kp, preferred_element_type=jnp.float32) * (d ** -0.5)
    dist = (jnp.arange(BAND_BLOCK)[:, None] + pad) - jnp.arange(span)[None, :]
    bias = jnp.transpose(bias_tbl[t5_bucket(dist)], (2, 0, 1)).reshape(n_kv, g, BAND_BLOCK, span)
    logits = logits + bias.astype(jnp.float32)
    mask = ((dist >= 0) & (dist < window))[None] & (key_idx >= pad)[:, None, :]
    mask = mask[None, :, None, None]
    sink = None
    if sinks is not None:
        sink = sinks.astype(jnp.float32).reshape(n_kv, g, 1, 1)
    p = masked_softmax(logits, mask, sink)
    out = jnp.einsum('bnkgql,bnlkd->bnqkgd', p.astype(v.dtype), vp)
    return out.reshape(b, s, h, d)

def nsa_compress(kv, pos_emb, w1, w2):
    b, s, n_kv, d = kv.shape
    n_cmp = (s - CMP_LEN) // CMP_STRIDE + 1
    idx = jnp.arange(n_cmp)[:, None] * CMP_STRIDE + jnp.arange(CMP_LEN)[None, :]
    blocks = kv[:, idx] + pos_emb[None, None, :, None, :]
    blocks = jnp.moveaxis(blocks, 3, 2).reshape(b, n_cmp, n_kv, CMP_LEN * d)
    return jax.nn.gelu(blocks @ w1) @ w2

def selection_weights(n_cmp, n_sel):
    starts = np.arange(n_cmp)[:, None] * CMP_STRIDE
    blk = np.arange(n_sel)[None, :] * SEL_BLOCK
    shared = np.clip(np.minimum(starts + CMP_LEN, blk + SEL_BLOCK) - np.maximum(starts, blk), 0, None)
    return (shared / CMP_STRIDE).astype(np.float32)

def nsa_selected_attention(qg, k_sel, v_sel, sel_idx, bias_tbl):
    b, s, n_kv, g, d = qg.shape
    n_top = sel_idx.shape[-1]
    n_sel = s // SEL_BLOCK
    n_keys = n_top * SEL_BLOCK
    scale = d ** -0.5
    kb = jnp.moveaxis(k_sel.reshape(b, n_sel, SEL_BLOCK, n_kv, d), 3, 1)
    vb = jnp.moveaxis(v_sel.reshape(b, n_sel, SEL_BLOCK, n_kv, d), 3, 1)
    tbl = jnp.moveaxis(bias_tbl.reshape(N_BUCKETS, n_kv, g), 0, 1)
    n_chunk = s // NSA_Q_CHUNK
    q_chunks = jnp.moveaxis(qg.reshape(b, n_chunk, NSA_Q_CHUNK, n_kv, g, d), 1, 0)
    idx_chunks = jnp.moveaxis(sel_idx.reshape(b, n_kv, n_chunk, NSA_Q_CHUNK, n_top), 2, 0)
    starts = jnp.arange(n_chunk) * NSA_Q_CHUNK
    bi = jnp.arange(b)[:, None, None, None]
    kvi = jnp.arange(n_kv)[None, :, None, None]
    pos_in_blk = jnp.arange(SEL_BLOCK)

    def chunk(xs):
        q_c, idx_c, start = xs
        t_c = start + jnp.arange(NSA_Q_CHUNK)
        k_c = kb[bi, kvi, idx_c]
        v_c = vb[bi, kvi, idx_c]
        dist = t_c[:, None, None] - (idx_c[..., None] * SEL_BLOCK + pos_in_blk)
        bias = jnp.moveaxis(tbl[kvi[..., None], t5_bucket(dist)], -1, 2)
        logits = jnp.einsum('bqkgd,bkqnld->bkgqnl', q_c, k_c, preferred_element_type=jnp.float32) * scale + bias
        mask = (dist >= 0)[:, :, None]
        p = masked_softmax(logits.reshape(b, n_kv, g, NSA_Q_CHUNK, n_keys),
                           mask.reshape(b, n_kv, 1, NSA_Q_CHUNK, n_keys))
        return jnp.einsum('bkgqm,bkqmd->bqkgd', p.astype(v_sel.dtype),
                          v_c.reshape(b, n_kv, NSA_Q_CHUNK, n_keys, d))

    out = lax.map(chunk, (q_chunks, idx_chunks, starts))
    return jnp.moveaxis(out, 0, 1).reshape(b, s, n_kv * g, d)

def nsa_attention(q, k_cmp, v_cmp, k_sel, v_sel, k_win, v_win, gate_logits, cmp_pos, cmp_w1, cmp_w2, bias_tbl):
    b, s, h, d = q.shape
    n_kv = k_cmp.shape[2]
    g = h // n_kv
    scale = d ** -0.5
    qg = q.reshape(b, s, n_kv, g, d)
    t = jnp.arange(s)
    kc = nsa_compress(k_cmp, cmp_pos[0], cmp_w1[0], cmp_w2[0])
    vc = nsa_compress(v_cmp, cmp_pos[1], cmp_w1[1], cmp_w2[1])
    n_cmp = kc.shape[1]
    dist_c = t[:, None] - (jnp.arange(n_cmp) * CMP_STRIDE + CMP_LEN - 1)[None, :]
    bias_c = jnp.moveaxis(bias_tbl[t5_bucket(dist_c)], -1, 0).reshape(n_kv, g, s, n_cmp)
    logits_c = jnp.einsum('bskgd,bckd->bkgsc', qg, kc, preferred_element_type=jnp.float32) * scale + bias_c
    p_cmp = masked_softmax(logits_c, dist_c >= 0)
    o_cmp = jnp.einsum('bkgsc,bckd->bskgd', p_cmp.astype(vc.dtype), vc).reshape(b, s, h, d)
    n_sel = s // SEL_BLOCK
    n_top = min(SEL_TOP_N, n_sel)
    share = jnp.asarray(selection_weights(n_cmp, n_sel))
    importance = jnp.einsum('bkgsc,cj->bksj', p_cmp, share)
    blk = jnp.arange(n_sel)[None, :]
    cur = (t // SEL_BLOCK)[:, None]
    forced = (blk == 0) | (blk == cur) | (blk == cur - 1)
    score = jnp.where(forced, FORCE_SCORE, jnp.where(blk <= cur, importance, NEG_INF))
    _, sel_idx = lax.top_k(score, n_top)
    o_sel = nsa_selected_attention(qg, k_sel, v_sel, sel_idx, bias_tbl)
    o_win = banded_attention(q, k_win, v_win, bias_tbl, NSA_WINDOW)
    gate = jax.nn.sigmoid(gate_logits.astype(jnp.float32)).reshape(b, s, h, 3).astype(q.dtype)
    out = gate[..., 0:1] * o_cmp + gate[..., 1:2] * o_sel + gate[..., 2:3] * o_win
    return out.reshape(b, s, h * d)

def moba_attention(q, k, v, bias_tbl):
    b, s, h, d = q.shape
    n_kv = k.shape[2]
    g = h // n_kv
    scale = d ** -0.5
    n_blk = -(-s // MOBA_BLOCK)
    padding = ((0, 0), (0, n_blk * MOBA_BLOCK - s), (0, 0), (0, 0))
    kb = jnp.moveaxis(jnp.pad(k, padding).reshape(b, n_blk, MOBA_BLOCK, n_kv, d), 3, 1)
    vb = jnp.moveaxis(jnp.pad(v, padding).reshape(b, n_blk, MOBA_BLOCK, n_kv, d), 3, 1)
    qg = q.reshape(b, s, n_kv, g, d)
    tbl = jnp.transpose(bias_tbl.reshape(N_BUCKETS, n_kv, g), (1, 2, 0))
    n_top = min(MOBA_TOP_K, n_blk - 1)
    n_chunk = s // MOBA_Q_CHUNK
    q_chunks = jnp.moveaxis(qg.reshape(b, n_chunk, MOBA_Q_CHUNK, n_kv, g, d), 1, 0)
    starts = jnp.arange(n_chunk) * MOBA_Q_CHUNK
    pos_in_blk = jnp.arange(MOBA_BLOCK)
    bi = jnp.arange(b)[:, None, None, None, None]
    kvi = jnp.arange(n_kv)[None, :, None, None, None]
    gi = jnp.arange(g)[None, None, :, None, None]

    def own_block(q_c, start):
        t_c = start + jnp.arange(MOBA_Q_CHUNK)
        blk = start // MOBA_BLOCK
        k_own = lax.dynamic_index_in_dim(kb, blk, axis=2, keepdims=False)
        v_own = lax.dynamic_index_in_dim(vb, blk, axis=2, keepdims=False)
        dist = t_c[:, None] - (blk * MOBA_BLOCK + pos_in_blk)[None, :]
        logits = jnp.einsum('bqkgd,bkld->bkgql', q_c, k_own, preferred_element_type=jnp.float32) * scale
        logits = logits + tbl[:, :, t5_bucket(dist)]
        mask = jnp.broadcast_to(dist >= 0, logits.shape)
        return logits, mask, v_own, t_c

    if n_top > 0:
        t = jnp.arange(s)
        q_blk = t // MOBA_BLOCK
        k_mean = jnp.mean(kb, axis=3)
        gate = jnp.einsum('bskgd,bknd->bkgsn', qg, k_mean, preferred_element_type=jnp.float32)
        gate = jnp.where(jnp.arange(n_blk)[None, :] < q_blk[:, None], gate, NEG_INF)
        _, sel_idx = lax.top_k(gate, n_top)
        valid = sel_idx < q_blk[:, None]
        idx_chunks = jnp.moveaxis(sel_idx.reshape(b, n_kv, g, n_chunk, MOBA_Q_CHUNK, n_top), 3, 0)
        valid_chunks = jnp.moveaxis(valid.reshape(b, n_kv, g, n_chunk, MOBA_Q_CHUNK, n_top), 3, 0)
        n_sel_keys = n_top * MOBA_BLOCK

        def chunk(xs):
            q_c, start, idx_c, valid_c = xs
            logits_own, mask_own, v_own, t_c = own_block(q_c, start)
            k_sel = kb[bi, kvi, idx_c]
            v_sel = vb[bi, kvi, idx_c]
            dist = t_c[:, None, None] - (idx_c[..., None] * MOBA_BLOCK + pos_in_blk)
            bias = tbl[kvi[..., None], gi[..., None], t5_bucket(dist)]
            logits_sel = jnp.einsum('bqkgd,bkgqnld->bkgqnl', q_c, k_sel, preferred_element_type=jnp.float32) * scale + bias
            logits_sel = logits_sel.reshape(b, n_kv, g, MOBA_Q_CHUNK, n_sel_keys)
            mask_sel = jnp.broadcast_to(valid_c[..., None], dist.shape).reshape(logits_sel.shape)
            p = masked_softmax(jnp.concatenate([logits_sel, logits_own], axis=-1),
                               jnp.concatenate([mask_sel, mask_own], axis=-1)).astype(v.dtype)
            o_sel = jnp.einsum('bkgqm,bkgqmd->bqkgd', p[..., :n_sel_keys],
                               v_sel.reshape(b, n_kv, g, MOBA_Q_CHUNK, n_sel_keys, d))
            o_own = jnp.einsum('bkgql,bkld->bqkgd', p[..., n_sel_keys:], v_own)
            return o_sel + o_own

        out = lax.map(chunk, (q_chunks, starts, idx_chunks, valid_chunks))
    else:
        def chunk(xs):
            q_c, start = xs
            logits_own, mask_own, v_own, _ = own_block(q_c, start)
            p = masked_softmax(logits_own, mask_own).astype(v.dtype)
            return jnp.einsum('bkgql,bkld->bqkgd', p, v_own)

        out = lax.map(chunk, (q_chunks, starts))
    return jnp.moveaxis(out, 0, 1).reshape(b, s, h, d)

def first_inputs(seed: int = 0) -> dict:
    key = jax.random.key(seed)
    ks = jax.random.split(key, 14)

    def nrm(k, shape, scale):
        return jax.random.normal(k, shape, jnp.float32) * scale

    out_scale = (2 * DEPTH) ** -0.5
    return {
        'x': nrm(ks[0], (BATCH, SEQ, D_MODEL), 1.0),
        'w_in': nrm(ks[1], (DEPTH, D_MODEL, D_IN), D_MODEL ** -0.5),
        'cmp_pos': nrm(ks[2], (DEPTH, 2, CMP_LEN, HEAD_DIM), 0.1),
        'cmp_w1': nrm(ks[3], (DEPTH, 2, CMP_LEN * HEAD_DIM, CMP_HIDDEN), (CMP_LEN * HEAD_DIM) ** -0.5),
        'cmp_w2': nrm(ks[4], (DEPTH, 2, CMP_HIDDEN, HEAD_DIM), CMP_HIDDEN ** -0.5),
        'swa_sinks': nrm(ks[5], (DEPTH, SWA_HEADS), 1.0),
        'w_branch': nrm(ks[6], (DEPTH, N_BRANCHES, MIX_WIDTH, D_MODEL), MIX_WIDTH ** -0.5),
        'w_out': nrm(ks[7], (DEPTH, D_MODEL, D_MODEL), D_MODEL ** -0.5 * out_scale),
        'w_mlp_in': nrm(ks[8], (DEPTH, D_MODEL, D_FF), D_MODEL ** -0.5),
        'w_mlp_out': nrm(ks[9], (DEPTH, D_FF, D_MODEL), D_FF ** -0.5 * out_scale),
        'norm_mix': 1.0 + nrm(ks[10], (DEPTH, D_MODEL), 0.02),
        'norm_mlp': 1.0 + nrm(ks[11], (DEPTH, D_MODEL), 0.02),
        'norm_final': 1.0 + nrm(ks[12], (D_MODEL,), 0.02),
        'rel_bias': nrm(ks[13], (N_BUCKETS, TOTAL_HEADS), 0.5),
    }

def first_block(x, w_in, cmp_pos, cmp_w1, cmp_w2, swa_sinks, w_branch, w_out, w_mlp_in, w_mlp_out,
              norm_mix, norm_mlp, norm_final, rel_bias):
    b, s, _ = x.shape
    bias_a = rel_bias[:, :NSA_HEADS]
    bias_b = rel_bias[:, NSA_HEADS:NSA_HEADS + SWA_HEADS]
    bias_c = rel_bias[:, NSA_HEADS + SWA_HEADS:]
    for layer in range(DEPTH):
        h = rms_norm(x, norm_mix[layer])
        (a_q, a_kc, a_vc, a_ks, a_vs, a_kw, a_vw, a_gate,
         b_q, b_k, b_v, c_q, c_k, c_v, merge_gate) = jnp.split(h @ w_in[layer], SPLIT_POINTS, axis=-1)
        o_a = nsa_attention(split_heads(a_q, NSA_HEADS),
                            split_heads(a_kc, NSA_KV_HEADS), split_heads(a_vc, NSA_KV_HEADS),
                            split_heads(a_ks, NSA_KV_HEADS), split_heads(a_vs, NSA_KV_HEADS),
                            split_heads(a_kw, NSA_KV_HEADS), split_heads(a_vw, NSA_KV_HEADS),
                            a_gate, cmp_pos[layer], cmp_w1[layer], cmp_w2[layer], bias_a)
        o_b = banded_attention(split_heads(b_q, SWA_HEADS), split_heads(b_k, SWA_KV_HEADS),
                               split_heads(b_v, SWA_KV_HEADS), bias_b, SWA_WINDOW,
                               swa_sinks[layer]).reshape(b, s, MIX_WIDTH)
        o_c = moba_attention(split_heads(c_q, MOBA_HEADS), split_heads(c_k, MOBA_KV_HEADS),
                             split_heads(c_v, MOBA_KV_HEADS), bias_c).reshape(b, s, MIX_WIDTH)
        branches = jnp.stack([o_a, o_b, o_c], axis=2)
        y = jnp.einsum('bsmc,mcd->bsmd', branches, w_branch[layer])
        gate = jax.nn.sigmoid(merge_gate.reshape(b, s, N_BRANCHES, D_MODEL))
        x = x + jnp.sum(gate * y, axis=2) @ w_out[layer]
        h = rms_norm(x, norm_mlp[layer])
        x = x + jnp.square(jax.nn.relu(h @ w_mlp_in[layer])) @ w_mlp_out[layer]
    return rms_norm(x, norm_final)


MEM_LEN = 256
EPS = 1e-6
POOL_WINDOWS = (2, 4, 8, 16)
POOL_GROUP_DIM = D_MODEL // 8
POOL_DIM = POOL_GROUP_DIM * len(POOL_WINDOWS)
HGRN_DK = 128
HGRN_DV = 128
HGRN_HEADS = D_MODEL // 256
HGRN_DIM = HGRN_HEADS * HGRN_DK
MIX_DIM = POOL_DIM + HGRN_DIM
IN_DIM = POOL_DIM + 4 * HGRN_DIM
CHUNK = 64
XATTN_HEADS = 4
XATTN_HEAD_DIM = D_MODEL // XATTN_HEADS
N_GROUPS = 4
EXPERTS_PER_GROUP = 4
N_EXPERTS = N_GROUPS * EXPERTS_PER_GROUP
TOP_K_INNER = 2
D_EXPERT = D_MODEL // 4


def rmsnorm(x, gain):
    xf = x.astype(jnp.float32)
    y = xf * lax.rsqrt(jnp.mean(xf * xf, axis=-1, keepdims=True) + EPS)
    return (y * gain.astype(jnp.float32)).astype(x.dtype)

def causal_pool_mixer(u, pool_w, pool_scale):
    b, s, _ = u.shape
    uf = u.astype(jnp.float32)
    cs = jnp.concatenate([jnp.zeros((b, 1, POOL_DIM), jnp.float32), jnp.cumsum(uf, axis=1)], axis=1)
    t_plus_1 = jnp.arange(1, s + 1, dtype=jnp.int32)
    outs = []
    for g, w in enumerate(POOL_WINDOWS):
        sl = slice(g * POOL_GROUP_DIM, (g + 1) * POOL_GROUP_DIM)
        c = cs[:, :, sl]
        upper = c[:, 1:]
        lower = jnp.pad(c[:, : s + 1 - w], ((0, 0), (w - 1, 0), (0, 0)))
        count = jnp.minimum(t_plus_1, w).astype(jnp.float32)[None, :, None]
        pooled = (upper - lower) / count - uf[:, :, sl]
        outs.append(jnp.einsum('bsc,cd->bsd', pooled.astype(u.dtype), pool_w[g]))
    return (jnp.concatenate(outs, axis=-1) * pool_scale).astype(u.dtype)

def hgrn2_mixer(q_in, f_in, i_in, g_in, lb, norm_gain):
    b, s, _ = q_in.shape
    n_chunks = s // CHUNK
    q = jax.nn.silu(q_in.astype(jnp.float32))
    lb = lb.astype(jnp.float32)
    log_f = jnp.logaddexp(jnp.log(lb), jnp.log1p(-lb) + jax.nn.log_sigmoid(f_in.astype(jnp.float32)))
    k = -jnp.expm1(log_f)
    v = i_in.astype(jnp.float32)

    def to_chunks(t, d):
        return t.reshape(b, n_chunks, CHUNK, HGRN_HEADS, d).transpose(1, 0, 3, 2, 4)

    causal = jnp.tril(jnp.ones((CHUNK, CHUNK), dtype=bool))[None, None, :, :, None]

    def step(state, xs):
        qc, lfc, kc, vc = xs
        a = jnp.cumsum(lfc, axis=2)
        rel = a[:, :, :, None, :] - a[:, :, None, :, :]
        decay = jnp.exp(jnp.where(causal, rel, -jnp.inf))
        scores = jnp.einsum('bhtd,bhtsd,bhsd->bhts', qc, decay, kc)
        o = jnp.einsum('bhts,bhsv->bhtv', scores, vc) + jnp.einsum('bhtd,bhdv->bhtv', qc * jnp.exp(a), state)
        a_last = a[:, :, -1:, :]
        new_state = jnp.exp(a_last[:, :, 0, :])[..., None] * state + jnp.einsum(
            'bhsd,bhsv->bhdv', kc * jnp.exp(a_last - a), vc)
        return new_state, o

    s0 = jnp.zeros((b, HGRN_HEADS, HGRN_DK, HGRN_DV), jnp.float32)
    _, o = lax.scan(step, s0, (to_chunks(q, HGRN_DK), to_chunks(log_f, HGRN_DK),
                               to_chunks(k, HGRN_DK), to_chunks(v, HGRN_DV)))
    o = o.transpose(1, 0, 3, 2, 4).reshape(b, s, HGRN_HEADS, HGRN_DV)
    o = rmsnorm(o, norm_gain)
    gate = jax.nn.silu(g_in.astype(jnp.float32)).reshape(b, s, HGRN_HEADS, HGRN_DV)
    return (o * gate).reshape(b, s, HGRN_HEADS * HGRN_DV).astype(q_in.dtype)

def memory_cross_attention(h, mem_n, wq, wk, wv, wo):
    b, s, _ = h.shape
    m = mem_n.shape[1]
    q = (h @ wq).reshape(b, s, XATTN_HEADS, XATTN_HEAD_DIM)
    k = (mem_n @ wk).reshape(b, m, XATTN_HEADS, XATTN_HEAD_DIM)
    v = (mem_n @ wv).reshape(b, m, XATTN_HEADS, XATTN_HEAD_DIM)
    scores = jnp.einsum('bshd,bmhd->bhsm', q, k).astype(jnp.float32) * (XATTN_HEAD_DIM ** -0.5)
    p = jax.nn.softmax(scores, axis=-1).astype(v.dtype)
    o = jnp.einsum('bhsm,bmhd->bshd', p, v).reshape(b, s, D_MODEL)
    return o @ wo

def hierarchical_moe(h, router_group, router_expert, w_gate, w_up, w_down):
    b, s, _ = h.shape
    p_group = jax.nn.softmax(jnp.einsum('bsd,dg->bsg', h, router_group).astype(jnp.float32), axis=-1)
    pg_top, g_idx = lax.top_k(p_group, 1)
    logits_e = jnp.einsum('bsd,de->bse', h, router_expert).astype(jnp.float32)
    logits_e = logits_e.reshape(b, s, N_GROUPS, EXPERTS_PER_GROUP)
    g_onehot = jax.nn.one_hot(g_idx[..., 0], N_GROUPS, dtype=jnp.float32)
    sel = jnp.einsum('bsg,bsge->bse', g_onehot, logits_e)
    top_vals, top_idx = lax.top_k(sel, TOP_K_INNER)
    w_inner = jax.nn.softmax(top_vals, axis=-1)
    expert_id = g_idx * EXPERTS_PER_GROUP + top_idx
    combine = jnp.sum(jax.nn.one_hot(expert_id, N_EXPERTS, dtype=jnp.float32)
                      * (pg_top * w_inner)[..., None], axis=2).astype(h.dtype)
    y = jnp.zeros_like(h)
    for e in range(N_EXPERTS):
        hid = jax.nn.silu(h @ w_gate[e]) * (h @ w_up[e])
        y = y + combine[..., e:e + 1] * (hid @ w_down[e])
    return y

def second_inputs(seed: int = 0) -> dict:
    key = jax.random.key(seed)
    ks = jax.random.split(key, 24)
    f32 = jnp.float32

    def nrm(k, shape, scale):
        return jax.random.normal(k, shape, f32) * scale

    def gain(k, shape):
        return 1.0 + 0.02 * jax.random.normal(k, shape, f32)

    return {
        "x": nrm(ks[0], (BATCH, SEQ, D_MODEL), 1.0),
        "mem": nrm(ks[1], (BATCH, MEM_LEN, D_MODEL), 1.0),
        "norm_mix": gain(ks[2], (DEPTH, D_MODEL)),
        "w_in": nrm(ks[3], (DEPTH, D_MODEL, IN_DIM), D_MODEL ** -0.5),
        "pool_w": nrm(ks[4], (DEPTH, len(POOL_WINDOWS), POOL_GROUP_DIM, POOL_GROUP_DIM), POOL_GROUP_DIM ** -0.5),
        "pool_scale": gain(ks[5], (DEPTH, POOL_DIM)),
        "hgrn_lb_logits": nrm(ks[6], (DEPTH + 1, HGRN_DIM), 0.5),
        "hgrn_norm": gain(ks[7], (DEPTH, HGRN_DV)),
        "w_out": nrm(ks[8], (DEPTH, MIX_DIM, D_MODEL), MIX_DIM ** -0.5),
        "norm_xattn": gain(ks[9], (DEPTH, D_MODEL)),
        "norm_mem": gain(ks[10], (DEPTH, D_MODEL)),
        "xattn_wq": nrm(ks[11], (DEPTH, D_MODEL, D_MODEL), D_MODEL ** -0.5),
        "xattn_wk": nrm(ks[12], (DEPTH, D_MODEL, D_MODEL), D_MODEL ** -0.5),
        "xattn_wv": nrm(ks[13], (DEPTH, D_MODEL, D_MODEL), D_MODEL ** -0.5),
        "xattn_wo": nrm(ks[14], (DEPTH, D_MODEL, D_MODEL), D_MODEL ** -0.5),
        "norm_ffn": gain(ks[15], (DEPTH, D_MODEL)),
        "router_group": nrm(ks[16], (DEPTH, D_MODEL, N_GROUPS), D_MODEL ** -0.5),
        "router_expert": nrm(ks[17], (DEPTH, D_MODEL, N_EXPERTS), D_MODEL ** -0.5),
        "w_gate": nrm(ks[18], (DEPTH, N_EXPERTS, D_MODEL, D_EXPERT), D_MODEL ** -0.5),
        "w_up": nrm(ks[19], (DEPTH, N_EXPERTS, D_MODEL, D_EXPERT), D_MODEL ** -0.5),
        "w_down": nrm(ks[20], (DEPTH, N_EXPERTS, D_EXPERT, D_MODEL), D_EXPERT ** -0.5),
        "norm_final": gain(ks[21], (D_MODEL,)),
    }

def second_block(x, mem, norm_mix, w_in, pool_w, pool_scale, hgrn_lb_logits, hgrn_norm, w_out,
              norm_xattn, norm_mem, xattn_wq, xattn_wk, xattn_wv, xattn_wo, norm_ffn,
              router_group, router_expert, w_gate, w_up, w_down, norm_final):
    lower_bounds = jnp.cumsum(jax.nn.softmax(hgrn_lb_logits.astype(jnp.float32), axis=0), axis=0)
    splits = [POOL_DIM, POOL_DIM + HGRN_DIM, POOL_DIM + 2 * HGRN_DIM, POOL_DIM + 3 * HGRN_DIM]
    for l in range(DEPTH):
        h = rmsnorm(x, norm_mix[l])
        proj = h @ w_in[l]
        u, q_in, f_in, i_in, g_in = jnp.split(proj, splits, axis=-1)
        pool_out = causal_pool_mixer(u, pool_w[l], pool_scale[l])
        hgrn_out = hgrn2_mixer(q_in, f_in, i_in, g_in, lower_bounds[l], hgrn_norm[l])
        x = x + jnp.concatenate([pool_out, hgrn_out], axis=-1) @ w_out[l]
        h = rmsnorm(x, norm_xattn[l])
        m = rmsnorm(mem, norm_mem[l])
        x = x + memory_cross_attention(h, m, xattn_wq[l], xattn_wk[l], xattn_wv[l], xattn_wo[l])
        h = rmsnorm(x, norm_ffn[l])
        x = x + hierarchical_moe(h, router_group[l], router_expert[l], w_gate[l], w_up[l], w_down[l])
    return rmsnorm(x, norm_final)


def setup_inputs(seed=0):
    out = dict(first_inputs(seed))
    for name, value in second_inputs(seed + 1).items():
        if name != "x":
            out[name + "_2"] = value
    return out


def reference(
    x, w_in, cmp_pos, cmp_w1, cmp_w2, swa_sinks, w_branch, w_out, w_mlp_in, w_mlp_out, norm_mix,
    norm_mlp, norm_final, rel_bias, mem_2, norm_mix_2, w_in_2, pool_w_2, pool_scale_2,
    hgrn_lb_logits_2, hgrn_norm_2, w_out_2, norm_xattn_2, norm_mem_2, xattn_wq_2, xattn_wk_2,
    xattn_wv_2, xattn_wo_2, norm_ffn_2, router_group_2, router_expert_2, w_gate_2, w_up_2,
    w_down_2, norm_final_2,
):
    x = first_block(
        x, w_in, cmp_pos, cmp_w1, cmp_w2, swa_sinks, w_branch, w_out, w_mlp_in, w_mlp_out,
        norm_mix, norm_mlp, norm_final, rel_bias,
    )
    return second_block(
        x, mem_2, norm_mix_2, w_in_2, pool_w_2, pool_scale_2, hgrn_lb_logits_2, hgrn_norm_2,
        w_out_2, norm_xattn_2, norm_mem_2, xattn_wq_2, xattn_wk_2, xattn_wv_2, xattn_wo_2,
        norm_ffn_2, router_group_2, router_expert_2, w_gate_2, w_up_2, w_down_2, norm_final_2,
    )


_drawn_inputs = setup_inputs


def setup_inputs(seed=0):
    import zlib

    import numpy as np

    out = dict(_drawn_inputs(seed))
    spreads = {}
    factors = {'cmp_pos': 2.849,
     'swa_sinks': 8.0,
     'norm_mix': 7.232,
     'pool_scale_2': 3.863,
     'hgrn_norm_2': 8.0,
     'norm_xattn_2': 6.613,
     'norm_mem_2': 4.675,
     'norm_final_2': 7.973,
     'norm_mlp': 3.277,
     'norm_ffn_2': 8.0}
    for name, (base, spread) in spreads.items():
        noise = np.random.default_rng([zlib.crc32(name.encode()), seed]).standard_normal(out[name].shape)
        drawn = base * np.exp(spread * noise) if base else spread * noise
        out[name] = jnp.asarray(drawn.astype(out[name].dtype))
    for name, factor in factors.items():
        out[name] = (out[name] * factor).astype(out[name].dtype)
    return out
```

```python
from contextlib import ExitStack, contextmanager
import math

import numpy as np
import concourse.bass as bass
from concourse import mybir
from concourse.alu_op_type import AluOpType as ALU

F32 = mybir.dt.float32
F32R = mybir.dt.float32r
U32 = mybir.dt.uint32
ACT = mybir.ActivationFunctionType
AX = mybir.AxisListType
ENG = mybir.EngineType

P = 128
D = 2048
S = 256
NH = S // P
DK = D // P
HD = 128
HEADS = 8
KVH = 2
GRP = HEADS // KVH
W512 = 512
EPS = 1e-6
NEG = -1e30
TINY = 1e-30
N_CMP = (S - 32) // 16 + 1
CMP_LEN = 32
N_EXP = 16
RAW_SLOTS = 8
HL_SLOTS = 4
LEAD = 3
BLK = 1024


class Count:

    loop = None

    def __init__(self, ctx, nc, name):
        self.h, self.name, self.n, self.used = ctx.enter_context(nc.semaphore(name)), name, 0, 0
        nc.gpsimd.sem_inc(self.h, 1)
        self.n = 1

    def now(self):
        if Count.loop and Count.loop[1].get(self.name):
            it, per = Count.loop
            return it * per[self.name] + (self.n + self.used)
        return self.n + self.used

    def inc(self, instruction, by=1):
        instruction.then_inc(self.h, by)
        if Count.loop:
            assert self.name in Count.loop[1], self.name
            self.used += by
        else:
            self.n += by
        return self.now()


def build(nc, a, out):
    ctx = ExitStack()
    with ctx:
        def sb(name, shape, dt=F32):
            return ctx.enter_context(nc.sbuf_tensor(name, shape, dt))

        def count(name):
            c = Count(ctx, nc, name)
            counts.append(c)
            return c

        counts = []
        pe, act, dve, pool, sp = nc.tensor, nc.scalar, nc.vector, nc.gpsimd, nc.sync
        MAIN = [ENG.PE, ENG.Activation, ENG.DVE, ENG.Pool]

        RAW = sb("RAW", [P, RAW_SLOTS, BLK])
        HI = sb("HI", [P, HL_SLOTS, BLK], F32R)
        LO = sb("LO", [P, HL_SLOTS, BLK], F32R)
        XH = sb("XH", [P, 32, S], F32R)
        XL = sb("XL", [P, 32, S], F32R)
        X = sb("X", [P, NH, D])
        Y = sb("Y", [P, NH * D])
        WORK = sb("WORK", [P, 10240])
        IDENT = sb("IDENT", [P, P])
        SWH = sb("SWH", [P, DK * 24], F32R)
        SWL = sb("SWL", [P, DK * 24], F32R)
        GATE = sb("GATE", [P, NH, 24])
        GAIN = sb("GAIN", [P, 7, DK])
        SMALL = sb("SMALL", [P, 512])
        PS = ctx.enter_context(nc.psum_tensor("PS", [P, 8, 512], F32))
        Y3 = Y[:, :].rearrange("p (h n) -> p h n", h=NH)

        used = {}

        def work(name, at, n, *dims):
            assert at + n <= 10240, name
            v = WORK[:, at:at + n]
            return v.rearrange("p (a b) -> p a b", a=dims[0]) if dims else v

        def dram(name, cols):
            return nc.dram_tensor(name, (NH, P, cols), F32, kind="Internal").ap()

        PROJ, SGATE, PROJ2 = dram("proj", 5632), dram("sgate", 3 * D), dram("proj2", 5120)
        XQ, XK, XV = dram("xq", D), dram("xk", D), dram("xv", D)

        raw_in = [ctx.enter_context(nc.semaphore(f"raw_in{k}")) for k in range(RAW_SLOTS)]
        hi_done = ctx.enter_context(nc.semaphore("hi_done"))
        lo_done = ctx.enter_context(nc.semaphore("lo_done"))
        pe_done = ctx.enter_context(nc.semaphore("pe_done"))
        ld = [count(f"ld{i}") for i in range(4)]
        ev = [count(f"ev{i}") for i in range(3)]
        st = [count(f"st{i}") for i in range(2)]
        s_stage = count("s_stage")
        s_act = count("s_act")
        s_dve = count("s_dve")
        s_pe = count("s_pe")
        s_tp = count("s_tp")
        s_hi = count("s_hi")
        s_lo = count("s_lo")

        @contextmanager
        def loop(n, per):
            names = {c.name: c for c in counts}
            before = {c.name: c.n for c in counts}
            with nc.Fori(0, n, engines=MAIN) as it:
                Count.loop = (it, per)
                yield it
                Count.loop = None
            bad = {c.name: c.used for c in counts if c.used != per.get(c.name, 0)}
            assert not bad, bad
            for c in counts:
                c.n = before[c.name] + n * c.used
                c.used = 0

        def A(i):
            return s_act.inc(i)

        def V(i):
            return s_dve.inc(i)

        def T(i):
            return s_pe.inc(i)

        def seq(i):
            dve.drain()
            return i

        sources = []

        def stream_load():
            b = 0
            for passes, blocks in sources:
                def body(it, base):
                    for k, src in enumerate(blocks):
                        n = base + k
                        sp.wait_ge(lo_done, it * len(blocks) + (n + 1))
                        dst = RAW[:, n % RAW_SLOTS, :]
                        s = src(it)
                        sp.dma_start(dst.rearrange("p (k n) -> p k n", k=s.shape[1]), s).then_inc(raw_in[n % RAW_SLOTS], 16)
                assert len(blocks) % RAW_SLOTS == 0 or passes == 1
                if passes == 1:
                    body(0, b)
                else:
                    with nc.Fori(0, passes, engines=[ENG.SP]) as it:
                        body(it, b)
                b += passes * len(blocks)
            assert b == total

        plan = make_plan(a)
        total = sum(p * len(bl) for p, bl in plan)
        sources.extend(plan)
        at = {"b": 0, "stage": 0}

        def split(b, it=0, per=0):
            if isinstance(it, int) and b >= total:
                return
            raw, hl = b % RAW_SLOTS, b % HL_SLOTS
            act.wait_ge(raw_in[raw], it * (16 * per // RAW_SLOTS) + 16 * (b // RAW_SLOTS + 1))
            act.wait_ge(pe_done, it * per + (b + 1))
            act.activation(HI[:, hl, :], RAW[:, raw, :], ACT.Copy).then_inc(hi_done, 1)
            dve.wait_ge(hi_done, it * per + (b + 1))
            dve.tensor_tensor(LO[:, hl, :], RAW[:, raw, :], HI[:, hl, :].bitcast(F32), ALU.subtract).then_inc(lo_done, 1)

        class Stage:

            def __init__(self, it=0):
                self.passes, blocks = plan[at["stage"]]
                self.per = len(blocks) if self.passes > 1 else 0
                self.base, self.k, self.n, self.it = at["b"], 0, len(blocks), it

            def end(self):
                assert self.k == self.n, (self.k, self.n)
                at["b"] += self.passes * self.n
                at["stage"] += 1

            def gemm(self, blocks, kt0, pair, cols=W512, m=P, lhs=None):
                ktb = BLK // cols
                halves = NH if lhs is None else 1
                for j in range(blocks):
                    b = self.base + self.k
                    split(b + LEAD, self.it, self.per)
                    pe.wait_ge(lo_done, self.it * self.per + (b + 1 + RAW_SLOTS))
                    if j == 0:
                        pe.wait_ge(ev[pair].h, ev[pair].now())
                    for q in range(ktb):
                        kt = j * ktb + q
                        for h in range(halves):
                            o = PS[0:m, 2 * pair + h, 0:cols]
                            if lhs is None:
                                xh, xl = (t[:, kt0 + kt, h * P:h * P + P] for t in (XH, XL))
                            else:
                                xh, xl = lhs(kt)
                            wh, wl = (t[:, b % HL_SLOTS, q * cols:(q + 1) * cols] for t in (HI, LO))
                            pe.matmul(o, xh, wh, start=kt == 0, stop=False)
                            pe.matmul(o, xh, wl, start=False, stop=False)
                            mm = pe.matmul(o, xl, wh, start=False, stop=kt == blocks * ktb - 1)
                    mm.then_inc(pe_done, 1)
                    self.k += 1
                return self.it * self.per + (self.base + self.k + HL_SLOTS)

        def pair_ap(pair):
            return PS[:, 2 * pair:2 * pair + 2, :]

        bank_free = [1, 1, 1, 1]

        def transpose_split(src, nk, kt0, gain=None, banks=(4, 5, 6, 7)):
            for j in range(0, nk, 2):
                i = banks[(j // 2) % len(banks)]
                if bank_free[i - 4] is not None:
                    pe.wait_ge(s_lo.h, bank_free[i - 4])
                for q in range(2):
                    for h in range(NH):
                        mm = pe.transpose(PS[:, i, q * S + h * P:q * S + h * P + P],
                                          src[:, h, (j + q) * P:(j + q + 1) * P], IDENT[:, :])
                t = s_tp.inc(mm)
                act.wait_ge(s_tp.h, t)
                dve.wait_ge(s_tp.h, t)
                if gain is None:
                    dh, dl = (v[:, kt0 + j:kt0 + j + 2, :].rearrange("p a b -> p (a b)") for v in (XH, XL))
                    hi = s_hi.inc(act.activation(dh, PS[:, i, :], ACT.Copy))
                    dve.wait_ge(s_hi.h, hi)
                    lo = s_lo.inc(dve.tensor_tensor(dl, PS[:, i, :], dh.bitcast(F32), ALU.subtract))
                else:
                    for q in range(2):
                        g = gain[:, j + q:j + q + 1]
                        ins = act.activation(XH[:, kt0 + j + q, :], PS[:, i, q * S:(q + 1) * S], ACT.Copy, scale=g)
                    dve.wait_ge(s_hi.h, s_hi.inc(ins))
                    for q in range(2):
                        g = gain[:, j + q:j + q + 1]
                        ins = dve.scalar_tensor_tensor(
                            out=XL[:, kt0 + j + q, :], in0=PS[:, i, q * S:(q + 1) * S], scalar=g,
                            in1=XH[:, kt0 + j + q, :].bitcast(F32), op0=ALU.mult, op1=ALU.subtract)
                    lo = s_lo.inc(ins)
                bank_free[i - 4] = lo
            return lo

        def rstd(sums, out_, v, n, width):
            dve.tensor_scalar(v, sums, 1.0 / n, EPS, ALU.mult, ALU.add)
            dve.drain()
            t = V(dve.reciprocal(out_, v))
            act.wait_ge(s_dve.h, t)
            t = A(act.activation(out_, out_, ACT.Sqrt))
            dve.wait_ge(s_act.h, t)
            sq = SMALL[:, 480:480 + width]
            dve.tensor_tensor(sq, out_, out_, ALU.mult)
            dve.drain()
            dve.tensor_tensor(sq, sq, v, ALU.mult)
            dve.drain()
            dve.tensor_scalar(sq, sq, -0.5, 1.5, ALU.mult, ALU.add)
            dve.drain()
            dve.tensor_tensor(out_, out_, sq, ALU.mult)
            dve.drain()

        def normalize(src, dst, ready=None):
            ss, v, r = SMALL[:, 464:466], SMALL[:, 466:468], SMALL[:, 468:470]
            t = V(dve.drain())
            act.wait_ge(s_dve.h, t)
            if ready:
                act.wait_ge(*ready)
            for h in range(NH):
                t = A(act.activation(dst[:, h, :], src[:, h, :], ACT.Square, accum_out=ss[:, h:h + 1]))
            dve.wait_ge(s_act.h, t)
            rstd(ss, r, v, D, 2)
            t = V(dve.drain())
            act.wait_ge(s_dve.h, t)
            dve.tensor_scalar(dst[:, 0, :], src[:, 0, :], r[:, 0:1], None, ALU.mult)
            t2 = A(act.activation(dst[:, 1, :], src[:, 1, :], ACT.Copy, scale=r[:, 1:2]))
            t = V(dve.drain())
            pe.wait_ge(s_dve.h, t)
            pe.wait_ge(s_act.h, t2)

        STAGE = work("stage", 0, 2048, 2)

        def store(pair, ready, slot, dst, func=ACT.Copy):
            act.wait_ge(pe_done, ready)
            act.wait_ge(st[slot].h, st[slot].now())
            t = ev[pair].inc(act.activation(STAGE[:, slot, :], pair_ap(pair).rearrange("p h n -> p (h n)"), func))
            act.wait_ge(ev[pair].h, t)
            st[slot].inc(act.dma_start(dst, STAGE[:, slot, :].rearrange("p (h n) -> p h n", h=NH)), 16)

        def add_to_x(pair, ready, cols):
            dve.wait_ge(pe_done, ready)
            ev[pair].inc(dve.tensor_tensor(X[:, :, cols], pair_ap(pair), X[:, :, cols], ALU.add))

        def cols_of(t, c, n=W512):
            return t[:, :, bass.ds(c, n)].rearrange("h p n -> p h n")

        def all_stored():
            for s in st:
                act.wait_ge(s.h, s.now())

        def small_gemm(srcs, n, done_with):
            raw = SMALL[:, 0:DK * n]
            t = V(dve.drain())
            act.wait_ge(s_dve.h, t)
            c = 0
            for s in srcs:
                w = s.shape[1]
                l = ld[0].inc(act.dma_start(raw.rearrange("p (k n) -> p k n", n=n)[:, :, c:c + w],
                                            s.rearrange("(k p) n -> p k n", p=P)), 16)
                c += w
            act.wait_ge(ld[0].h, l)
            act.wait_ge(s_pe.h, s_pe.now())
            t = A(act.activation(SWH[:, 0:DK * n], raw, ACT.Copy))
            dve.wait_ge(s_act.h, t)
            t = V(dve.tensor_tensor(SWL[:, 0:DK * n], raw, SWH[:, 0:DK * n].bitcast(F32), ALU.subtract))
            pe.wait_ge(s_dve.h, t)
            for i in range(4):
                pe.wait_ge(s_lo.h, bank_free[i])
            for h in range(NH):
                o = PS[:, 7, h * n:(h + 1) * n]
                for k in range(DK):
                    wh, wl = (s[:, k * n:(k + 1) * n] for s in (SWH, SWL))
                    xh, xl = (s[:, k, h * P:(h + 1) * P] for s in (XH, XL))
                    pe.matmul(o, xh, wh, start=k == 0, stop=False)
                    pe.matmul(o, xh, wl, start=False, stop=False)
                    mm = pe.matmul(o, xl, wh, start=False, stop=k == DK - 1)
            return T(mm)

        def fence():
            marks = [A(act.drain()), V(dve.drain()), T(pe.drain())]
            for e in (act, dve, pe):
                for s, t in zip((s_act, s_dve, s_pe), marks):
                    e.wait_ge(s.h, t)

        sp.dma_start(X[:, :, :], a["x"][0].rearrange("(h p) n -> p h n", p=P)).then_inc(ld[1].h, 16)
        ld[1].n += 16
        lo_start = dve.sem_inc(lo_done, RAW_SLOTS)
        pe.sem_inc(pe_done, HL_SLOTS)
        stream_load()
        ld[2].inc(act.dma_start(IDENT[:, :], a["ident"]), 16)
        for i, g in enumerate(["norm_mix", "norm_mlp", "norm_mix_2", "norm_xattn_2", "norm_mem_2", "norm_ffn_2"]):
            ld[2].inc(act.dma_start(GAIN[:, i, :], a[g]), 16)
        for e in (act, dve, pe):
            e.wait_ge(ld[2].h, ld[2].now())
        dve.wait_ge(ld[1].h, ld[1].now())
        for b in range(LEAD):
            split(b)
        normalize(X, Y3, (ld[1].h, ld[1].now()))
        x_ready = transpose_split(Y3, DK, 0, GAIN[:, 0, :])
        pe.wait_ge(s_lo.h, x_ready)

        g0 = 2560
        t = small_gemm([a["w_in"][0, :, g0:g0 + 24]], 24, None)
        act.wait_ge(s_pe.h, t)
        A(act.activation(GATE[:, :, :].rearrange("p h n -> p (h n)"), PS[:, 7, 0:48], ACT.Sigmoid))
        for passes, dst, c0, func in ((2, PROJ, 0, ACT.Copy), (1, PROJ, 2048, ACT.Copy),
                                      (3, PROJ, 2560, ACT.Copy), (6, SGATE, 0, ACT.Sigmoid)):
            if passes == 1:
                s = Stage()
                store(0, s.gemm(8, 0, 0), 0, cols_of(dst, c0), func)
                s.end()
                continue
            with loop(passes, {"ev0": 1, "ev1": 1, "st0": 16, "st1": 16}) as it:
                s = Stage(it)
                for u in range(2):
                    store(u, s.gemm(8, 0, u), u, cols_of(dst, it * 1024 + (c0 + u * 512)), func)
            s.end()
        fence()
        all_stored()

        BIAS = work("bias", 0, 24 * 256, 24)
        KT = work("kT", 6144, 256)
        AQ = work("aq", 6400, 1024, 2)
        AK = work("ak", 7424, 256, 2)
        AV = work("av", 7680, 256, 2)
        OA = work("oa", 7936, 2048, 2)
        LG = Y[:, 0:1536].rearrange("p (i n) -> p i n", i=4)
        PT = Y[:, 1536:3072].rearrange("p (i n) -> p i n", i=4)
        QT = Y[:, 3072:4096].rearrange("p (i n) -> p i n", i=4)
        SINK, MX, NM, RS, RI, ES = (SMALL[:, 8 * i:8 * i + 8] for i in range(6))

        OH = Y[0:34, 0:512]
        REL = Y[0:34, 512:536]
        ld[0].inc(act.dma_start(OH, a["onehot"]), 16)
        ld[0].inc(act.dma_start(REL[0:32, :], a["rel_bias"]), 16)
        ld[0].inc(act.dma_start(REL[32:34, :], a["maskrows"]), 16)
        ld[0].inc(act.dma_start(SINK, a["swa_sinks"].rearrange("a n -> (a n)").partition_broadcast(P)), 16)
        l = ld[0].now()
        pe.wait_ge(ld[0].h, l)
        dve.wait_ge(ld[0].h, l)
        free = {}
        n = 0
        for part, shift in ((0, P), (1, 0)):
            for s0 in range(0, P, 21):
                m = min(21, P - s0)
                bank = n % 4
                if bank in free:
                    pe.wait_ge(s_dve.h, free[bank])
                for j in range(m):
                    w = 256 + shift - (s0 + j)
                    mm = pe.matmul(PS[:, bank, j * 24:j * 24 + 24], OH[:, w:w + P] if w + P <= 512 else None,
                                   REL, start=True, stop=True)
                t = T(mm)
                dve.wait_ge(s_pe.h, t)
                free[bank] = V(dve.tensor_copy(BIAS[:, :, part * P + s0:part * P + s0 + m],
                                               PS[:, bank, 0:m * 24].rearrange("p (s h) -> p h s", h=24)))
                n += 1
        CB = SMALL[:, 64:304].rearrange("p (h c k) -> p h c k", h=2, k=8)
        for h in range(NH):
            for c in range(N_CMP):
                w = 256 + h * P - (16 * c + 31)
                mm = pe.matmul(PS[:, 4, (h * N_CMP + c) * 8:(h * N_CMP + c) * 8 + 8], OH[:, w:w + P],
                               REL[:, 0:8], start=True, stop=True)
        t = T(mm)
        dve.wait_ge(s_pe.h, t)
        V(dve.tensor_copy(SMALL[:, 64:304], PS[:, 4, 0:240]))
        fence()

        POS = Y[:, 0:64].rearrange("p (w l) -> p w l", w=2)
        W2 = Y[:, 64:576].rearrange("p (w k n) -> p w k n", w=2, k=2)
        KC = Y[:, 576:576 + 32].rearrange("p (g c) -> p g c", g=2)
        VC = Y[:, 608:608 + 256].rearrange("p (g d) -> p g d", g=2)
        HC = Y[:, 864:864 + 256]
        HCT = Y[:, 1120:1120 + 64].rearrange("p (k c) -> p k c", k=2)
        for w in range(2):
            ld[0].inc(act.dma_start(POS[:, w, :], a["cmp_pos"][w]), 16)
            ld[0].inc(act.dma_start(W2[:, w, :, :], a["cmp_w2"][0, w].rearrange("(k p) n -> p k n", p=P)), 16)
        NC2 = 2 * N_CMP
        for w in range(2):
            ld[1].inc(act.dma_start(AQ[:, :, 0:256], cols_of(PROJ, 1024 + 256 * w, 256)), 16)
            pe.wait_ge(ld[1].h, ld[1].now())
            for g in range(KVH):
                for h in range(NH):
                    mm = pe.transpose(PS[:, 7, g * S + h * P:g * S + h * P + P], AQ[:, h, g * P:g * P + P], IDENT[:, :])
            t = T(mm)
            act.wait_ge(s_pe.h, t)
            t = A(act.activation(KTC := work("ktc", 7936, 512), PS[:, 7, :], ACT.Copy))
            dve.wait_ge(s_act.h, t)
            dve.wait_ge(ld[0].h, ld[0].now())
            xc = work("xc", 8448, 960, 32)
            for g in range(KVH):
                for q in range(2):
                    src = KTC[:, g * S + 16 * q:g * S + 16 * q + 240].rearrange("p (c r) -> p r c", r=16)
                    V(dve.tensor_tensor(xc[:, 16 * q:16 * q + 16, g * N_CMP:(g + 1) * N_CMP], src,
                                        POS[:, w, 16 * q:16 * q + 16].unsqueeze(2).to_broadcast([P, 16, N_CMP]), ALU.add))
            t = V(dve.drain())
            act.wait_ge(s_dve.h, t)
            xcf = work("xc", 8448, 960)
            xch, xcl = (v[:, 24 + 4 * w:28 + 4 * w, :].rearrange("p a b -> p (a b)")[:, 0:960] for v in (XH, XL))
            t = A(act.activation(xch, xcf, ACT.Copy))
            dve.wait_ge(s_act.h, t)
            t = V(dve.tensor_tensor(xcl, xcf, xch.bitcast(F32), ALU.subtract))
            pe.wait_ge(s_dve.h, t)
            s = Stage()
            r = s.gemm(8, 0, 0, cols=256, m=NC2,
                       lhs=lambda kt: (xch[:, kt * NC2:(kt + 1) * NC2], xcl[:, kt * NC2:(kt + 1) * NC2]))
            s.end()
            act.wait_ge(pe_done, r)
            t = ev[0].inc(act.activation(HC[0:NC2, :], PS[0:NC2, 0, 0:256], ACT.Gelu_apprx_tanh))
            pe.wait_ge(ev[0].h, t)
            for k in range(2):
                mm = pe.transpose(PS[:, 7, k * 32:k * 32 + NC2], HC[0:NC2, k * P:(k + 1) * P], IDENT[0:NC2, 0:NC2])
            t = T(mm)
            dve.wait_ge(s_pe.h, t)
            t = V(dve.tensor_copy(HCT[:, :, 0:NC2], PS[:, 7, 0:64].rearrange("p (k c) -> p k c", k=2)[:, :, 0:NC2]))
            pe.wait_ge(s_dve.h, t)
            if w == 0:
                for k in range(2):
                    mm = pe.matmul(PS[:, 6, 0:NC2], W2[:, 0, k, :], HCT[:, k, 0:NC2], start=k == 0, stop=k == 1)
                t = T(mm)
                dve.wait_ge(s_pe.h, t)
                V(dve.tensor_copy(KC[:, :, 0:N_CMP], PS[:, 6, 0:NC2].rearrange("p (g c) -> p g c", g=2)))
            else:
                for g in range(KVH):
                    for k in range(2):
                        mm = pe.matmul(PS[0:N_CMP, 6, g * P:(g + 1) * P], HCT[:, k, g * N_CMP:(g + 1) * N_CMP],
                                       W2[:, 1, k, :], start=k == 0, stop=k == 1)
                t = T(mm)
                dve.wait_ge(s_pe.h, t)
                V(dve.tensor_copy(VC[0:N_CMP, :, :], PS[0:N_CMP, 6, 0:256].rearrange("p (g c) -> p g c", g=2)))
        fence()

        CQT = Y[:, 2048:4096].rearrange("p (i n) -> p i n", i=8)
        CL = Y[:, 1184:1184 + 240]
        CM = Y[:, 1424:1424 + 240]
        CPT = Y[:, 1664:1664 + 256].rearrange("p (i n) -> p i n", i=1)
        CR = SMALL[:, 304:320]
        for g in range(KVH):
            act.wait_ge(s_pe.h, s_pe.now())
            l = ld[1].inc(act.dma_start(AQ, cols_of(PROJ, 512 * g)), 16)
            pe.wait_ge(ld[1].h, l)
            pe.wait_ge(s_act.h, s_act.now())
            for i in range(4):
                for h in range(NH):
                    mm = pe.transpose(PS[:, 4 + i // 2, (i % 2) * S + h * P:(i % 2) * S + h * P + P],
                                      AQ[:, h, i * P:(i + 1) * P], IDENT[:, :])
            t = T(mm)
            act.wait_ge(s_pe.h, t)
            A(act.activation(CQT[:, 4 * g:4 * g + 4, :].rearrange("p i n -> p (i n)"),
                             PS[:, 4:6, :].rearrange("p a n -> p (a n)"), ACT.Copy))
        pe.wait_ge(s_act.h, s_act.now())
        for h in range(NH):
            for i in range(HEADS):
                o = (h * HEADS + i) * N_CMP
                mm = pe.matmul(PS[:, 0, o:o + N_CMP], CQT[:, i, h * P:h * P + P], KC[:, i // GRP, 0:N_CMP],
                               start=True, stop=True)
        t = T(mm)
        dve.wait_ge(s_pe.h, t)
        cl4, cm4 = (v.rearrange("p (h i c) -> p h i c", h=2, i=8) for v in (CL, CM))
        for h in range(NH):
            cb = CB[:, h, :, :].rearrange("p c k -> p k c")
            dve.scalar_tensor_tensor(out=cl4[:, h], in0=PS[:, 0, h * 120:h * 120 + 120].rearrange("p (i c) -> p i c", i=8),
                                     scalar=HD ** -0.5, in1=cb, op0=ALU.mult, op1=ALU.add)
            dve.tensor_scalar(cm4[:, h], cb, NEG / 2, None, ALU.is_gt)
        dve.drain()
        cl3, cm3 = (v.rearrange("p (i c) -> p i c", i=16) for v in (CL, CM))
        dve.tensor_reduce(CR, cl3, AX.X, ALU.max)
        dve.drain()
        t = V(dve.tensor_tensor(cl3, cl3, CR.unsqueeze(2).to_broadcast([P, 16, N_CMP]), ALU.subtract))
        act.wait_ge(s_dve.h, t)
        t = A(act.activation(CL, CL, ACT.Exp))
        dve.wait_ge(s_act.h, t)
        dve.tensor_tensor(CL, CL, CM, ALU.mult)
        dve.drain()
        dve.tensor_reduce(CR, cl3, AX.X, ALU.add)
        dve.drain()
        dve.tensor_scalar(CR, CR, TINY, None, ALU.max)
        dve.drain()
        dve.reciprocal(CR, CR)
        dve.drain()
        gates = GATE[:, :, :].rearrange("p h (i b) -> p h i b", b=3)
        dve.tensor_tensor(CR.rearrange("p (h i) -> p h i", h=2), CR.rearrange("p (h i) -> p h i", h=2), gates[:, :, :, 0], ALU.mult)
        dve.drain()
        t = V(dve.tensor_tensor(cl3, cl3, CR.unsqueeze(2).to_broadcast([P, 16, N_CMP]), ALU.mult))
        pe.wait_ge(s_dve.h, t)
        for i in range(HEADS):
            pe.wait_ge(s_act.h, s_act.now())
            for h in range(NH):
                o = (h * HEADS + i) * N_CMP
                mm = pe.transpose(PS[0:N_CMP, 4, h * P:h * P + P], CL[:, o:o + N_CMP], IDENT[:, :])
            t = T(mm)
            act.wait_ge(s_pe.h, t)
            t = A(act.activation(CPT[0:N_CMP, 0, :], PS[0:N_CMP, 4, 0:256], ACT.Copy))
            pe.wait_ge(s_act.h, t)
            for h in range(NH):
                mm = pe.matmul(PS[:, 2 * h + i // GRP, (i % GRP) * P:(i % GRP) * P + P], CPT[0:N_CMP, 0, h * P:h * P + P],
                               VC[0:N_CMP, i // GRP, :], start=True, stop=True)
            t = T(mm)
        dve.wait_ge(s_pe.h, t)
        V(dve.tensor_copy(OA[:, :, :], PS[:, 0:4, :].rearrange("p (h a) n -> p h (a n)", h=2)))
        fence()

        def attention(q0, k0, v0, head0, sink, gate, accumulate):
            with loop(KVH, {"ld1": 48, "s_pe": 4, "s_act": 5, "s_dve": 6}) as g:
                act.wait_ge(s_pe.h, s_pe.now())
                act.wait_ge(s_dve.h, s_dve.now())
                ld[1].inc(act.dma_start(AQ, cols_of(PROJ, g * 512 + q0)), 16)
                ld[1].inc(act.dma_start(AK, cols_of(PROJ, g * P + k0, P)), 16)
                l = ld[1].inc(act.dma_start(AV, cols_of(PROJ, g * P + v0, P)), 16)
                pe.wait_ge(s_dve.h, s_dve.now())
                pe.wait_ge(ld[1].h, l)
                for i in range(GRP):
                    for h in range(NH):
                        pe.transpose(PS[:, 4 + i // 2, (i % 2) * S + h * P:(i % 2) * S + h * P + P],
                                     AQ[:, h, i * P:(i + 1) * P], IDENT[:, :])
                for h in range(NH):
                    mm = pe.transpose(PS[:, 6, h * P:h * P + P], AK[:, h, :], IDENT[:, :])
                t = T(mm)
                act.wait_ge(s_pe.h, t)
                dve.wait_ge(s_pe.h, t)
                ta = A(act.activation(QT.rearrange("p i n -> p (i n)"), PS[:, 4:6, :].rearrange("p a n -> p (a n)"), ACT.Copy))
                tv = V(dve.tensor_copy(KT, PS[:, 6, 0:S]))
                pe.wait_ge(s_act.h, ta)
                pe.wait_ge(s_dve.h, tv)
                for i in range(GRP):
                    pe.matmul(PS[:, i, 0:P], QT[:, i, 0:P], KT[:, 0:P], start=True, stop=True)
                    mm = pe.matmul(PS[:, i, P:3 * P], QT[:, i, P:S], KT, start=True, stop=True)
                t = T(mm)
                dve.wait_ge(s_pe.h, t)
                hb = BIAS[:, bass.ds(g * GRP + head0, GRP), :]
                dve.scalar_tensor_tensor(out=LG[:, :, P:3 * P], in0=PS[:, 0:4, P:3 * P], scalar=HD ** -0.5,
                                         in1=hb, op0=ALU.mult, op1=ALU.add)
                dve.scalar_tensor_tensor(out=LG[:, :, 0:P], in0=PS[:, 0:4, 0:P], scalar=HD ** -0.5,
                                         in1=hb[:, :, P:S], op0=ALU.mult, op1=ALU.add)
                dve.drain()
                dve.tensor_reduce(MX[:, 4:8], LG[:, :, P:3 * P], AX.X, ALU.max)
                dve.tensor_reduce(MX[:, 0:4], LG[:, :, 0:P], AX.X, ALU.max)
                dve.drain()
                if sink:
                    sk = SINK[:, bass.ds(g * GRP, GRP)].unsqueeze(1).to_broadcast([P, 2, 4])
                    mx2, es2 = (v.rearrange("p (h i) -> p h i", h=2) for v in (MX, ES))
                    dve.tensor_tensor(mx2, mx2, sk, ALU.max)
                    dve.drain()
                    dve.tensor_tensor(es2, sk, mx2, ALU.subtract)
                t = V(dve.tensor_scalar(NM, MX, -1.0, None, ALU.mult))
                act.wait_ge(s_dve.h, t)
                for h in range(NH):
                    for i in range(GRP):
                        v = LG[:, i, 0:P] if h == 0 else LG[:, i, P:3 * P]
                        c = h * GRP + i
                        ins = act.activation(v, v, ACT.Exp, bias=NM[:, c:c + 1], accum_out=RS[:, c:c + 1])
                if sink:
                    dve.wait_ge(s_act.h, A(ins))
                    t = A(act.activation(ES, ES, ACT.Exp))
                    pe.wait_ge(s_act.h, t)
                    dve.wait_ge(s_act.h, t)
                    dve.tensor_tensor(RS, RS, ES, ALU.add)
                    dve.drain()
                else:
                    t = A(ins)
                    A(act.drain())
                    pe.wait_ge(s_act.h, t)
                    dve.wait_ge(s_act.h, t)
                for i in range(GRP):
                    for j in range(3):
                        mm = pe.transpose(PS[:, 4 + i, j * P:(j + 1) * P], LG[:, i, j * P:(j + 1) * P], IDENT[:, :])
                t = T(mm)
                dve.tensor_scalar(RS, RS, TINY, None, ALU.max)
                dve.drain()
                dve.reciprocal(RI, RS)
                dve.drain()
                ri2 = RI.rearrange("p (h i) -> p h i", h=2)
                if gate:
                    dve.tensor_tensor(ri2, ri2, GATE[:, :, :].rearrange("p h (i b) -> p h i b", b=3)[:, :, bass.ds(g * GRP, GRP), gate], ALU.mult)
                    dve.drain()
                act.wait_ge(s_pe.h, t)
                dve.wait_ge(s_pe.h, t)
                ta = A(act.activation(PT[:, 0:2, :], PS[:, 4:6, 0:3 * P], ACT.Copy))
                tv = V(dve.tensor_copy(PT[:, 2:4, :], PS[:, 6:8, 0:3 * P]))
                pe.wait_ge(s_act.h, ta)
                pe.wait_ge(s_dve.h, tv)
                for i in range(GRP):
                    c = slice(i * P, (i + 1) * P)
                    pe.matmul(PS[:, 0, c], PT[:, i, 0:P], AV[:, 0, :], start=True, stop=True)
                    pe.matmul(PS[:, 1, c], PT[:, i, P:2 * P], AV[:, 0, :], start=True, stop=False)
                    mm = pe.matmul(PS[:, 1, c], PT[:, i, 2 * P:3 * P], AV[:, 1, :], start=False, stop=True)
                t = T(mm)
                dve.wait_ge(s_pe.h, t)
                for h in range(NH):
                    dst = OA[:, h, bass.ds(g * 512, 512)].rearrange("p (i n) -> p i n", i=GRP)
                    src = PS[:, h, :].rearrange("p (i n) -> p i n", i=GRP)
                    r = RI[:, h * GRP:h * GRP + GRP].unsqueeze(2).to_broadcast([P, GRP, P])
                    if accumulate:
                        tmp = LG[:, h, 0:384]
                        lg = Y[:, h * 512:h * 512 + 512].rearrange("p (i n) -> p i n", i=GRP)
                        dve.tensor_tensor(lg, src, r, ALU.mult)
                        dve.drain()
                        last = dve.tensor_tensor(dst, dst, lg, ALU.add)
                    else:
                        last = dve.tensor_tensor(dst, src, r, ALU.mult)
                V(last)
                V(dve.drain())
                V(dve.drain())
                A(act.drain())
                A(act.drain()) if False else None
            fence()

        bank_free[:] = [1] * 4
        attention(0, 1536, 1792, 0, False, 1, True)
        attention(0, 2048, 2304, 0, False, 2, True)
        transpose_split(OA, 8, 0)
        fence()
        attention(2560, 3584, 3840, 8, True, 0, False)
        transpose_split(OA, 8, 8)
        fence()
        attention(4096, 5120, 5376, 16, False, 0, False)
        transpose_split(OA, 8, 16)
        fence()

        GS = work("gs", 0, 3072, 3)
        TM = work("tm", 3072, 3072, 3)
        with loop(2, {"ld2": 96, "ev0": 2, "ev1": 2, "ev2": 2, "s_dve": 6}) as it:
            s = Stage(it)
            for cc in range(2):
                act.wait_ge(s_dve.h, s_dve.now())
                for m in range(3):
                    ld[2].inc(act.dma_start(GS[:, m, :].rearrange("p (h n) -> p h n", h=2),
                                            cols_of(SGATE, it * 1024 + (m * D + cc * 512))), 16)
                gl = ld[2].now()
                for m in range(3):
                    r = s.gemm(4, 8 * m, m)
                    dve.wait_ge(pe_done, r)
                    dve.wait_ge(ld[2].h, gl)
                    y = Y3[:, :, bass.ds(it * 1024 + cc * 512, 512)]
                    g3, t3 = (v[:, m, :].rearrange("p (h n) -> p h n", h=2) for v in (GS, TM))
                    if m == 0:
                        ev[m].inc(dve.tensor_tensor(y, pair_ap(m), g3, ALU.mult))
                        dve.drain()
                    else:
                        ev[m].inc(dve.tensor_tensor(t3, pair_ap(m), g3, ALU.mult))
                        dve.drain()
                        dve.tensor_tensor(y, y, t3, ALU.add)
                    V(dve.drain())
        s.end()

        def project_add():
            with loop(2, {"ev0": 1, "ev1": 1}) as it:
                s = Stage(it)
                for u in range(2):
                    add_to_x(u, s.gemm(8, 0, u), bass.ds(it * 1024 + u * 512, 512))
            s.end()

        fence()
        pe.wait_ge(s_lo.h, transpose_split(Y3, DK, 0))
        project_add()

        def down(s, pairs=(1, 2, 1, 2)):
            for c in range(4):
                add_to_x(pairs[c], s.gemm(2, 16, pairs[c]), slice(c * 512, (c + 1) * 512))

        HB = work("hb", 0, 1024, 2)
        SG = work("sg", 1024, 1024)

        def relu_square(r):
            act.wait_ge(pe_done, r)
            act.wait_ge(s_tp.h, s_tp.now())
            t = ev[0].inc(act.activation(SG, pair_ap(0).rearrange("p h n -> p (h n)"), ACT.Relu))
            act.wait_ge(ev[0].h, t)
            return A(act.activation(HB[:, :, :].rearrange("p h n -> p (h n)"), SG, ACT.Square))

        def hidden_T(t):
            pe.wait_ge(s_act.h, t)
            bank_free[2] = bank_free[3] = s_lo.now()
            act.wait_ge(pe_done, down_done())
            pe.wait_ge(s_lo.h, transpose_split(HB, 4, 16, banks=(6, 7)))

        state = {}

        def down_done():
            return state["down"]

        fence()
        normalize(X, Y3)
        pe.wait_ge(s_lo.h, transpose_split(Y3, DK, 0, GAIN[:, 1, :]))
        fence()
        s = Stage()
        relu_square(s.gemm(8, 0, 0))
        s.end()
        with loop(15, {"ev0": 1, "ev1": 2, "ev2": 2, "s_act": 1, "s_tp": 2, "s_hi": 2, "s_lo": 2}) as it:
            s = Stage(it)
            state["down"] = it * s.per + (s.base + HL_SLOTS)
            before = s_act.now()
            r = s.gemm(8, 0, 0)
            hidden_T(before)
            relu_square(r)
            down(s)
        s.end()
        state["down"] = at["b"] + HL_SLOTS
        hidden_T(s_act.now())
        s = Stage()
        down(s)
        s.end()

        fence()
        FG = work("fg", 2048, 2048)

        def norm_in_place(gain):
            l = ld[0].inc(act.dma_start(FG, gain.partition_broadcast(P)), 16)
            normalize(X, Y3)
            dve.wait_ge(ld[0].h, l)
            dve.wait_ge(s_act.h, s_act.now())
            for h in range(NH):
                dve.tensor_tensor(X[:, h, :], Y3[:, h, :], FG, ALU.mult)

        norm_in_place(a["norm_final"])

        fence()
        normalize(X, Y3)
        pe.wait_ge(s_lo.h, transpose_split(Y3, DK, 0, GAIN[:, 2, :]))
        fence()

        def project_store(passes, dst, kt0=0):
            with loop(passes, {"ev0": 1, "ev1": 1, "st0": 16, "st1": 16}) as it:
                s = Stage(it)
                for u in range(2):
                    store(u, s.gemm(8, kt0, u), u, cols_of(dst, it * 1024 + u * 512))
            s.end()

        project_store(5, PROJ2)
        fence()
        all_stored()

        PU = Y[:, 0:2048].rearrange("p (h n) -> p h n", h=2)
        BAND = work("band", 0, 2048).rearrange("p (g h n) -> p g h n", g=4, h=2)
        PW = work("pw", 2048, 2048).rearrange("p (g k n) -> p g k n", g=4, k=2)
        PP = work("pp", 4096, 2048, 8)
        PSC = SMALL[:, 0:8]
        act.wait_ge(s_dve.h, s_dve.now())
        ld[0].inc(act.dma_start(PU, cols_of(PROJ2, 0, 1024)), 16)
        ld[0].inc(act.dma_start(BAND, a["band"].rearrange("g (h p) n -> p g h n", p=P)), 16)
        ld[0].inc(act.dma_start(PW, a["pool_w_2"][0].rearrange("g (k p) n -> p g k n", p=P)), 16)
        ld[0].inc(act.dma_start(PSC, a["pool_scale_2"]), 16)
        for e in (pe, act, dve):
            e.wait_ge(ld[0].h, ld[0].now())
        for g in range(4):
            for k in range(2):
                c = 2 * g + k
                if c >= 4:
                    pe.wait_ge(s_act.h, s_act.now())
                for h in range(NH):
                    mm = pe.matmul(PS[:, c % 4, 0:S], PU[:, h, c * P:(c + 1) * P], BAND[:, g, h, :], start=h == 0, stop=h == 1)
                t = T(mm)
                act.wait_ge(s_pe.h, t)
                A(act.activation(PP[:, c, :], PS[:, c % 4, 0:S], ACT.Copy))
        pe.wait_ge(s_act.h, s_act.now())
        for g in range(4):
            for k in range(2):
                c = 2 * g + k
                if c >= 4:
                    pe.wait_ge(s_dve.h, s_dve.now())
                for j in range(2):
                    mm = pe.matmul(PS[:, c % 4, 0:S], PW[:, g, j, k * P:(k + 1) * P], PP[:, 2 * g + j, :], start=j == 0, stop=j == 1)
                t = T(mm)
                act.wait_ge(s_pe.h, t)
                t = A(act.activation(XH[:, c, :], PS[:, c % 4, 0:S], ACT.Copy, scale=PSC[:, c:c + 1]))
                dve.wait_ge(s_act.h, t)
                V(dve.scalar_tensor_tensor(out=XL[:, c, :], in0=PS[:, c % 4, 0:S], scalar=PSC[:, c:c + 1],
                                           in1=XH[:, c, :].bitcast(F32), op0=ALU.mult, op1=ALU.subtract))
        fence()

        QF = Y[:, 0:1024].rearrange("p (h n) -> p h n", h=2)
        FF = Y[:, 1024:2048].rearrange("p (h n) -> p h n", h=2)
        AA = Y[:, 2048:3072]
        XX = Y[:, 3072:4096]
        VV = work("vv", 0, 1024, 2)
        QQ = work("qq", 1024, 1024)
        KK = work("kk", 2048, 1024)
        SC = work("sc", 3072, 1536, 4)
        MASK = work("mask", 4608, 1024, 8)
        ONE = work("one", 5632, 1024)
        TMP = work("tmp", 6656, 1024)
        HO = work("ho", 7680, 2048, 2)
        LB = SMALL[:, 16:24]
        LB1 = SMALL[:, 24:32]
        HG = SMALL[:, 32:160]
        L2 = SMALL[:, 160:176]
        HS, HV, HR = SMALL[:, 176:184], SMALL[:, 184:192], SMALL[:, 192:200]
        ld[0].inc(act.dma_start(MASK, a["levels"].rearrange("l p n -> p l n")), 16)
        ld[0].inc(act.dma_start(HG, a["hgrn_norm_2"][0].partition_broadcast(P)), 16)
        ld[0].inc(act.dma_start(L2, a["hgrn_lb_logits_2"]), 16)
        dve.memset(ONE, 1.0)
        dve.drain()
        dve.memset(ONE.rearrange("p (c t) -> p c t", t=64)[:, :, 0:1], 0.0)
        dve.wait_ge(ld[0].h, ld[0].now())
        t = V(dve.tensor_tensor(L2[:, 0:8], L2[:, 0:8], L2[:, 8:16], ALU.subtract))
        act.wait_ge(s_dve.h, t)
        A(act.activation(LB, L2[:, 0:8], ACT.Sigmoid))
        A(act.activation(LB1, L2[:, 0:8], ACT.Sigmoid, scale=-1.0))
        fence()
        with loop(2, {"ld1": 64, "s_pe": 11, "s_act": 16, "s_dve": 34}) as g:
            act.wait_ge(s_pe.h, s_pe.now())
            act.wait_ge(s_dve.h, s_dve.now())
            ld[1].inc(act.dma_start(QF, cols_of(PROJ2, g * 512 + 1024)), 16)
            ld[1].inc(act.dma_start(FF, cols_of(PROJ2, g * 512 + 2048)), 16)
            l = ld[1].inc(act.dma_start(VV, cols_of(PROJ2, g * 512 + 3072)), 16)
            pe.wait_ge(ld[1].h, l)
            pe.wait_ge(s_dve.h, s_dve.now())
            for src, bank in ((QF, 4), (FF, 6)):
                for i in range(4):
                    for h in range(NH):
                        mm = pe.transpose(PS[:, bank + i // 2, (i % 2) * S + h * P:(i % 2) * S + h * P + P],
                                          src[:, h, i * P:(i + 1) * P], IDENT[:, :])
            tt = T(mm)
            act.wait_ge(s_pe.h, tt)
            l2 = ld[1].inc(act.dma_start(QF, cols_of(PROJ2, g * 512 + 4096)), 16)
            q_ps, f_ps = (PS[:, b:b + 2, :].rearrange("p a n -> p (a n)") for b in (4, 6))
            A(act.activation(XX, q_ps, ACT.Sigmoid))
            A(act.activation(KK, f_ps, ACT.Sigmoid, scale=-1.0))
            t = A(act.activation(AA, f_ps, ACT.Sigmoid))
            dve.wait_ge(s_act.h, t)
            V(dve.tensor_tensor(QQ, q_ps, XX, ALU.mult))
            for i in range(4):
                c = slice(i * S, (i + 1) * S)
                lb, lb1 = (v[:, bass.ds(g * 4 + i, 1)] for v in (LB, LB1))
                dve.tensor_scalar(KK[:, c], KK[:, c], lb1, None, ALU.mult)
                V(dve.tensor_scalar(AA[:, c], AA[:, c], lb1, lb, ALU.mult, ALU.add))
            dve.drain()
            t = V(dve.tensor_scalar(AA, AA, 1e-19, None, ALU.max))
            act.wait_ge(s_dve.h, t)
            t = A(act.activation(TMP, AA, ACT.Ln))
            dve.wait_ge(s_act.h, t)
            dve.tensor_tensor_scan(AA, ONE, TMP, 0.0, ALU.mult, ALU.add)
            dve.drain()
            free_sc = s_dve.now()
            levels = [32, 16, 8, 4, 2, 1, 0, 64, 128]
            for n, H in enumerate(levels):
                if H >= 64:
                    av = AA.rearrange("p (b n) -> p b n", n=2 * H)
                    dve.tensor_tensor(av[:, :, H:2 * H], av[:, :, H:2 * H],
                                      av[:, :, H - 1:H].to_broadcast([P, 1024 // (2 * H), H]), ALU.add)
                    dve.drain()
                if H:
                    nb = 1024 // (2 * H)
                    av, xv, qv, kv, tv = (v.rearrange("p (b n) -> p b n", n=2 * H) for v in (AA, XX, QQ, KK, TMP))
                    ref = av[:, :, H - 1:H].to_broadcast([P, nb, H])
                    dve.tensor_tensor(tv[:, :, H:2 * H], av[:, :, H:2 * H], ref, ALU.subtract)
                    t = V(dve.tensor_tensor(tv[:, :, 0:H], ref, av[:, :, 0:H], ALU.subtract))
                    act.wait_ge(s_dve.h, t)
                    t = A(act.activation(TMP, TMP, ACT.Exp))
                    dve.wait_ge(s_act.h, t)
                    dve.wait_ge(s_pe.h, s_pe.now())
                    dve.tensor_tensor(xv[:, :, H:2 * H], tv[:, :, H:2 * H], qv[:, :, H:2 * H], ALU.mult)
                    t = V(dve.tensor_tensor(xv[:, :, 0:H], tv[:, :, 0:H], kv[:, :, 0:H], ALU.mult))
                    pe.wait_ge(s_dve.h, t)
                lft, rgt = (XX, XX) if H else (KK, QQ)
                if H == 128:
                    for i in range(4):
                        mm = pe.matmul(PS[:, 2, i * P:(i + 1) * P], lft[:, i * S:i * S + P], rgt[:, i * S + P:(i + 1) * S],
                                       start=True, stop=True)
                    t = T(mm)
                    dve.wait_ge(s_pe.h, t)
                    V(dve.tensor_copy(SC[:, :, P:2 * P], PS[:, 2, :].rearrange("p (i n) -> p i n", i=4)))
                    continue
                b = 0 if n % 2 == 0 else 2
                for i in range(4):
                    for h in range(NH):
                        c = slice(i * S + h * P, i * S + h * P + P)
                        mm = pe.matmul(PS[:, b + h, i * P:(i + 1) * P], lft[:, c], rgt[:, c], start=True, stop=True)
                t = T(mm)
                dve.wait_ge(s_pe.h, t)
                mk = MASK[:, {64: 0, 32: 1, 16: 2, 8: 3, 4: 4, 2: 5, 1: 6, 0: 7}[H], :].unsqueeze(1).to_broadcast([P, 4, P])
                for h in range(NH):
                    dst = SC[:, :, 2 * h * P:(2 * h + 1) * P]
                    src = PS[:, b + h, :].rearrange("p (i n) -> p i n", i=4)
                    if n == 0:
                        last = dve.tensor_tensor(dst, src, mk, ALU.mult)
                    else:
                        t4 = TMP[:, h * 512:(h + 1) * 512].rearrange("p (i n) -> p i n", i=4)
                        dve.tensor_tensor(t4, src, mk, ALU.mult)
                        dve.drain()
                        last = dve.tensor_tensor(dst, dst, t4, ALU.add)
                V(last)
                dve.drain()
            pe.wait_ge(s_dve.h, s_dve.now())
            for i in range(4):
                c = slice(i * P, (i + 1) * P)
                pe.matmul(PS[:, 0, c], SC[:, i, 0:P], VV[:, 0, c], start=True, stop=True)
                pe.matmul(PS[:, 1, c], SC[:, i, P:2 * P], VV[:, 0, c], start=True, stop=False)
                mm = pe.matmul(PS[:, 1, c], SC[:, i, 2 * P:3 * P], VV[:, 1, c], start=False, stop=True)
            t = T(mm)
            act.wait_ge(s_pe.h, t)
            t = A(act.activation(TMP, PS[:, 0:2, :].rearrange("p a n -> p (a n)"), ACT.Square))
            act.wait_ge(ld[1].h, l2)
            qff = QF.rearrange("p h n -> p (h n)")
            t = A(act.activation(XX, qff, ACT.Sigmoid))
            dve.wait_ge(s_act.h, t)
            dve.wait_ge(ld[1].h, l2)
            dve.tensor_reduce(HS, TMP.rearrange("p (i n) -> p i n", i=8), AX.X, ALU.add)
            dve.drain()
            rstd(HS, HR, HV, P, 8)
            dve.tensor_tensor(XX, XX, qff, ALU.mult)
            dve.drain()
            dve.tensor_tensor(XX.rearrange("p (i n) -> p i n", i=8), XX.rearrange("p (i n) -> p i n", i=8),
                              HR.unsqueeze(2).to_broadcast([P, 8, P]), ALU.mult)
            dve.drain()
            dve.tensor_tensor(XX.rearrange("p (i n) -> p i n", i=8), XX.rearrange("p (i n) -> p i n", i=8),
                              HG.unsqueeze(1).to_broadcast([P, 8, P]), ALU.mult)
            dve.drain()
            V(dve.tensor_tensor(HO[:, :, bass.ds(g * 512, 512)], PS[:, 0:2, :], XX.rearrange("p (h n) -> p h n", h=2), ALU.mult))
            V(dve.drain())
            A(act.drain())
        fence()
        bank_free[:] = [1] * 4
        pe.wait_ge(s_lo.h, transpose_split(HO, 8, 8))
        project_add()

        fence()
        act.wait_ge(s_dve.h, s_dve.now())
        l = ld[1].inc(act.dma_start(MEM := work("mem", 2048, 4096, 2), a["mem_2"][0].rearrange("(h p) n -> p h n", p=P)), 16)
        dve.wait_ge(ld[1].h, l)
        normalize(MEM, Y3, (ld[1].h, l))
        pe.wait_ge(s_lo.h, transpose_split(Y3, DK, 0, GAIN[:, 4, :]))
        fence()
        project_store(2, XK)
        project_store(2, XV)
        fence()
        normalize(X, Y3)
        pe.wait_ge(s_lo.h, transpose_split(Y3, DK, 0, GAIN[:, 3, :]))
        fence()
        project_store(2, XQ)
        fence()
        all_stored()
        MQ = work("mq", 0, 1024, 2)
        MK = work("mk", 1024, 1024, 2)
        MV = work("mv", 2048, 1024, 2)
        MQT = work("mqt", 3072, 1024, 4)
        MKT = work("mkt", 4096, 1024, 4)
        MP = work("mp", 5120, 512, 2)
        MPT = work("mpt", 5632, 512, 2)
        M1, M2, M3 = SMALL[:, 0:2], SMALL[:, 2:4], SMALL[:, 4:6]
        XD = float(W512) ** -0.5
        with loop(4, {"ld1": 48, "s_pe": 4, "s_act": 4, "s_dve": 4}) as g:
            act.wait_ge(s_pe.h, s_pe.now())
            for dst, src in ((MQ, XQ), (MK, XK), (MV, XV)):
                l = ld[1].inc(act.dma_start(dst, cols_of(src, g * 512)), 16)
            pe.wait_ge(ld[1].h, l)
            pe.wait_ge(s_dve.h, s_dve.now())
            for src, bank in ((MQ, 4), (MK, 6)):
                for i in range(4):
                    for h in range(NH):
                        mm = pe.transpose(PS[:, bank + i // 2, (i % 2) * S + h * P:(i % 2) * S + h * P + P],
                                          src[:, h, i * P:(i + 1) * P], IDENT[:, :])
            t = T(mm)
            act.wait_ge(s_pe.h, t)
            dve.wait_ge(s_pe.h, t)
            ta = A(act.activation(MQT.rearrange("p i n -> p (i n)"), PS[:, 4:6, :].rearrange("p a n -> p (a n)"), ACT.Copy))
            tv = V(dve.tensor_copy(MKT.rearrange("p i n -> p (i n)"), PS[:, 6:8, :].rearrange("p a n -> p (a n)")))
            pe.wait_ge(s_act.h, ta)
            pe.wait_ge(s_dve.h, tv)
            for h in range(NH):
                for k in range(4):
                    mm = pe.matmul(PS[:, h, 0:S], MQT[:, k, h * P:(h + 1) * P], MKT[:, k, :], start=k == 0, stop=k == 3)
            t = T(mm)
            dve.wait_ge(s_pe.h, t)
            dve.tensor_reduce(M1, PS[:, 0:2, 0:S], AX.X, ALU.max)
            dve.drain()
            t = V(dve.tensor_scalar(M1, M1, -XD, None, ALU.mult))
            act.wait_ge(s_dve.h, t)
            for h in range(NH):
                ins = act.activation(MP[:, h, :], PS[:, h, 0:S], ACT.Exp, scale=XD, bias=M1[:, h:h + 1], accum_out=M2[:, h:h + 1])
            A(ins)
            t = A(act.drain())
            pe.wait_ge(s_act.h, t)
            dve.wait_ge(s_act.h, t)
            V(dve.reciprocal(M3, M2))
            for k in range(2):
                for h in range(NH):
                    mm = pe.transpose(PS[:, 4, k * S + h * P:k * S + h * P + P], MP[:, h, k * P:(k + 1) * P], IDENT[:, :])
            t = T(mm)
            act.wait_ge(s_pe.h, t)
            t = A(act.activation(MPT.rearrange("p k n -> p (k n)"), PS[:, 4, :], ACT.Copy))
            pe.wait_ge(s_act.h, t)
            for h in range(NH):
                for k in range(2):
                    mm = pe.matmul(PS[:, 2 + h, :], MPT[:, k, h * P:(h + 1) * P], MV[:, k, :], start=k == 0, stop=k == 1)
            t = T(mm)
            dve.drain()
            dve.wait_ge(s_pe.h, t)
            for h in range(NH):
                last = dve.tensor_scalar(Y3[:, h, bass.ds(g * 512, 512)], PS[:, 2 + h, :], M3[:, h:h + 1], None, ALU.mult)
            V(last)
        fence()
        bank_free[:] = [1] * 4
        pe.wait_ge(s_lo.h, transpose_split(Y3, DK, 0))
        project_add()

        fence()
        normalize(X, Y3)
        pe.wait_ge(s_lo.h, transpose_split(Y3, DK, 0, GAIN[:, 5, :]))
        fence()
        t = small_gemm([a["router_group_2"][0], a["router_expert_2"][0]], 20, None)
        COMB = GATE[:, :, 0:16]
        act.wait_ge(s_pe.h, t)
        LGT = SMALL[:, 0:40].rearrange("p (h n) -> p h n", h=2)
        t = A(act.activation(SMALL[:, 0:40], PS[:, 7, 0:40], ACT.Copy))
        RANK = SMALL[:, 40:44]
        l = ld[0].inc(act.dma_start(RANK, a["rank"][0].partition_broadcast(P)), 16)
        dve.wait_ge(s_act.h, t)
        dve.wait_ge(ld[0].h, l)
        rank2 = RANK.unsqueeze(1).to_broadcast([P, 2, 4])
        R1 = SMALL[:, 48:50]
        E4, OHG, SEL, O1, O2, WG = (SMALL[:, 56 + 8 * i:64 + 8 * i].rearrange("p (h n) -> p h n", h=2) for i in range(6))
        T1, T2, PG, WB = (SMALL[:, 112 + 2 * i:114 + 2 * i] for i in range(4))
        BIG = SMALL[:, 128:160].rearrange("p (h n) -> p h n", h=2)

        def b4(v):
            return v.unsqueeze(2).to_broadcast([P, 2, 4])

        def first_max(x, top, onehot):
            dve.tensor_reduce(top, x, AX.X, ALU.max)
            dve.drain()
            dve.tensor_tensor(onehot, x, b4(top), ALU.is_equal)
            dve.drain()
            dve.tensor_tensor(onehot, onehot, rank2, ALU.mult)
            dve.drain()
            dve.tensor_reduce(R1, onehot, AX.X, ALU.max)
            dve.drain()
            dve.tensor_tensor(onehot, onehot, b4(R1), ALU.is_equal)
            dve.drain()

        grp = LGT[:, :, 0:4]
        first_max(grp, T1, OHG)
        t = V(dve.tensor_tensor(E4, grp, b4(T1), ALU.subtract))
        act.wait_ge(s_dve.h, t)
        t = A(act.activation(E4, E4, ACT.Exp))
        dve.wait_ge(s_act.h, t)
        dve.tensor_reduce(PG, E4, AX.X, ALU.add)
        dve.drain()
        dve.reciprocal(PG, PG)
        for j in range(4):
            o = OHG[:, :, j:j + 1].to_broadcast([P, 2, 4])
            x = LGT[:, :, 4 + 4 * j:8 + 4 * j]
            dve.tensor_tensor(E4 if j else SEL, x, o, ALU.mult)
            dve.drain()
            if j:
                dve.tensor_tensor(SEL, SEL, E4, ALU.add)
                dve.drain()
        first_max(SEL, T1, O1)
        dve.scalar_tensor_tensor(out=E4, in0=O1, scalar=-3e38, in1=SEL, op0=ALU.mult, op1=ALU.add)
        dve.drain()
        first_max(E4, T2, O2)
        t = V(dve.tensor_tensor(WB, T2, T1, ALU.subtract))
        act.wait_ge(s_dve.h, t)
        t = A(act.activation(WB, WB, ACT.Exp))
        dve.wait_ge(s_act.h, t)
        dve.tensor_scalar(T1, WB, 1.0, None, ALU.add)
        dve.drain()
        dve.reciprocal(T1, T1)
        dve.drain()
        dve.tensor_tensor(T2, WB, T1, ALU.mult)
        dve.drain()
        dve.tensor_tensor(O1, O1, b4(T1), ALU.mult)
        dve.tensor_tensor(O2, O2, b4(T2), ALU.mult)
        dve.drain()
        dve.tensor_tensor(O1, O1, O2, ALU.add)
        dve.drain()
        dve.tensor_tensor(O1, O1, b4(PG), ALU.mult)
        dve.drain()
        for j in range(4):
            o = OHG[:, :, j:j + 1].to_broadcast([P, 2, 4])
            dve.tensor_tensor(COMB[:, :, 4 * j:4 * j + 4], O1, o, ALU.mult)
        dve.drain()

        def expert_hidden(e, r):
            act.wait_ge(pe_done, r[0])
            act.wait_ge(s_dve.h, s_dve.now())
            t = A(act.activation(SG, pair_ap(0).rearrange("p h n -> p (h n)"), ACT.Sigmoid))
            dve.wait_ge(s_act.h, t)
            sg3 = SG.rearrange("p (h n) -> p h n", h=2)
            ev[0].inc(dve.tensor_tensor(sg3, sg3, pair_ap(0), ALU.mult))
            dve.drain()
            dve.wait_ge(pe_done, r[1])
            dve.wait_ge(s_tp.h, s_tp.now())
            for h in range(NH):
                ins = dve.scalar_tensor_tensor(out=HB[:, h, :], in0=pair_ap(1)[:, h, :], scalar=COMB[:, h, bass.ds(e, 1)],
                                               in1=sg3[:, h, :], op0=ALU.mult, op1=ALU.mult)
            ev[1].inc(ins)
            return V(dve.drain())

        def expert_T(t):
            pe.wait_ge(s_dve.h, t)
            bank_free[2] = bank_free[3] = s_lo.now()
            act.wait_ge(pe_done, down_done())
            pe.wait_ge(s_lo.h, transpose_split(HB, 4, 16, banks=(6, 7)))

        fence()
        s = Stage()
        r = (s.gemm(8, 0, 0), s.gemm(8, 0, 1))
        expert_hidden(0, r)
        s.end()
        with loop(N_EXP - 1, {"ev0": 2, "ev1": 2, "ev2": 2, "s_act": 1, "s_dve": 1, "s_tp": 2, "s_hi": 2, "s_lo": 2}) as it:
            s = Stage(it)
            state["down"] = it * s.per + (s.base + HL_SLOTS)
            before = s_dve.now()
            r0 = s.gemm(8, 0, 0)
            expert_T(before)
            r1 = s.gemm(8, 0, 1)
            expert_hidden(it + 1, (r0, r1))
            down(s, (2, 0, 1, 2))
        s.end()
        state["down"] = at["b"] + HL_SLOTS
        expert_T(s_dve.now())
        s = Stage()
        down(s, (2, 0, 1, 2))
        s.end()
        assert at["b"] == total and at["stage"] == len(plan)

        fence()
        norm_in_place(a["norm_final_2"])
        t = V(dve.drain())
        act.wait_ge(s_dve.h, t)
        st[0].inc(act.dma_start(out[0].rearrange("(h p) n -> p h n", p=P), X[:, :, :]), 16)
        act.wait_ge(st[0].h, st[0].now())
        act.wait_ge(st[1].h, st[1].now())


def make_plan(a):
    plan = []

    def rows(w, r0, kt, c, n):
        return w[r0:r0 + kt * P, bass.ds(c, n)].rearrange("(k p) n -> p k n", p=P)

    def unit(w, per, c0, r0=0, blocks=8):
        return [lambda it, j=j: rows(w, r0 + j * 2 * P, 2, it * per + c0, 512) for j in range(blocks)]

    w_in = a["w_in"][0]
    for passes, c0 in ((2, 0), (1, 2048), (3, 2584), (6, 5656)):
        n = 1 if passes == 1 else 2
        plan.append((passes, sum((unit(w_in, 1024, c0 + 512 * u) for u in range(n)), [])))
    for w in range(2):
        w1 = a["cmp_w1"][0, w]
        plan.append((1, [lambda it, w1=w1, j=j: rows(w1, j * 4 * P, 4, 0, 256) for j in range(8)]))
    plan.append((2, sum((unit(a["w_branch"][0, m], 1024, 512 * u, 0, 4) for u in range(2) for m in range(3)), [])))

    def square(w, passes=2):
        plan.append((passes, unit(w, 1024, 0) + unit(w, 1024, 512)))

    def down_blocks(w, row):
        return [lambda it, c=c, j=j: w(it)[bass.ds(row(it) + j * 2 * P, 2 * P), c * 512:(c + 1) * 512]
                .rearrange("(k p) n -> p k n", p=P) for c in range(4) for j in range(2)]

    square(a["w_out"][0])
    w1, w2 = a["w_mlp_in"][0], a["w_mlp_out"][0]
    plan.append((1, unit(w1, 0, 0)))
    plan.append((15, unit(w1, 512, 512) + down_blocks(lambda it: w2, lambda it: it * 512)))
    plan.append((1, down_blocks(lambda it: w2, lambda it: 15 * 512)))
    square(a["w_in_2"][0], 5)
    square(a["w_out_2"][0])
    square(a["xattn_wk_2"][0])
    square(a["xattn_wv_2"][0])
    square(a["xattn_wq_2"][0])
    square(a["xattn_wo_2"][0])

    wg, wu = (a[n][0].rearrange("e k n -> (e k) n") for n in ("w_gate_2", "w_up_2"))
    wd = a["w_down_2"][0].rearrange("e k n -> (e k) n")

    def expert(w, e0):
        return [lambda it, j=j: w[bass.ds(it * D + (e0 * D + j * 2 * P), 2 * P), :].rearrange("(k p) n -> p k n", p=P)
                for j in range(8)]

    plan.append((1, expert(wg, 0) + expert(wu, 0)))
    plan.append((N_EXP - 1, expert(wg, 1) + expert(wu, 1) + down_blocks(lambda it: wd, lambda it: it * 512)))
    plan.append((1, down_blocks(lambda it: wd, lambda it: (N_EXP - 1) * 512)))
    return plan


def constants():
    dist = np.arange(512) - 256
    n = np.maximum(dist, 0)
    ratio = np.log(np.maximum(n, 1).astype(np.float32) / np.float32(16)) / np.float32(math.log(128 / 16))
    large = np.minimum(16 + (ratio * 16).astype(np.int32), 31)
    bucket = np.where(n < 16, n, large)
    onehot = np.zeros((34, 512), np.float32)
    onehot[bucket, np.arange(512)] = 1.0
    onehot[:32, dist < 0] = 0.0
    onehot[32] = dist < 0
    onehot[33] = dist >= 128
    maskrows = np.zeros((2, 24), np.float32)
    maskrows[0] = NEG
    maskrows[1, 8:16] = NEG
    t, s = np.arange(S)[None, :], np.arange(S)[:, None]
    band = np.stack([((t - s >= 0) & (t - s < w)) / np.minimum(t + 1, w) - (t == s) for w in (2, 4, 8, 16)]).astype(np.float32)
    q, k = np.arange(P)[None, :], np.arange(P)[:, None]
    levels = [(q // (2 * h) == k // (2 * h)) & (k % (2 * h) < h) & (q % (2 * h) >= h) for h in (64, 32, 16, 8, 4, 2, 1)]
    levels = np.stack(levels + [q == k]).astype(np.float32)
    return {"ident": np.eye(P, dtype=np.float32), "onehot": onehot, "maskrows": maskrows, "band": band,
            "levels": levels, "rank": np.array([[4, 3, 2, 1]], np.float32)}


def by_feature(v):
    v = np.asarray(v)
    return v.reshape(-1, P).T


LAYOUT = {g: by_feature for g in ("norm_mix", "norm_mlp", "norm_mix_2", "norm_xattn_2", "norm_mem_2", "norm_ffn_2",
                                  "pool_scale_2", "hgrn_lb_logits_2")}
LAYOUT["cmp_pos"] = lambda v: np.asarray(v)[0].transpose(0, 2, 1)


def kernel(**inputs):
    from concourse import bacc
    from concourse.bass_utils import run_bass_kernel_spmd

    nc = bacc.Bacc("TRN2", target_bir_lowering=False, num_devices=1)
    arrays, aps = {}, {}
    for name, value in {**inputs, **constants()}.items():
        v = np.ascontiguousarray(LAYOUT.get(name, np.asarray)(value))
        arrays[f"in_{name}"] = v
        aps[name] = nc.dram_tensor(f"in_{name}", v.shape, mybir.dt.from_np(v.dtype), kind="ExternalInput").ap()
    out = nc.dram_tensor("out", (1, S, D), F32, kind="ExternalOutput").ap()
    build(nc, aps, out)
    r = run_bass_kernel_spmd(nc, [arrays], core_ids=[0])
    return r.results[0]["out"]
```

```python
from contextlib import ExitStack, contextmanager
import math

import numpy as np
import concourse.bass as bass
from concourse import mybir
from concourse.alu_op_type import AluOpType as ALU

F32 = mybir.dt.float32
F32R = mybir.dt.float32r
U32 = mybir.dt.uint32
ACT = mybir.ActivationFunctionType
AX = mybir.AxisListType
ENG = mybir.EngineType

P = 128
D = 2048
S = 256
NH = S // P
DK = D // P
HD = 128
HEADS = 8
KVH = 2
GRP = HEADS // KVH
W512 = 512
EPS = 1e-6
NEG = -1e30
TINY = 1e-30
N_CMP = (S - 32) // 16 + 1
CMP_LEN = 32
N_EXP = 16
RAW_SLOTS = 8
HL_SLOTS = 4
LEAD = 3
BLK = 1024


class Count:

    loop = None

    def __init__(self, ctx, nc, name, start=1):
        self.h, self.name, self.n, self.used = ctx.enter_context(nc.semaphore(name)), name, start, 0
        if start:
            nc.gpsimd.sem_inc(self.h, start)

    def now(self):
        if Count.loop and Count.loop[1].get(self.name):
            it, per = Count.loop
            return it * per[self.name] + (self.n + self.used)
        return self.n + self.used

    def inc(self, instruction, by=1):
        instruction.then_inc(self.h, by)
        if Count.loop:
            assert self.name in Count.loop[1], self.name
            self.used += by
        else:
            self.n += by
        return self.now()


def build(nc, a, out):
    ctx = ExitStack()
    with ctx:
        def sb(name, shape, dt=F32):
            return ctx.enter_context(nc.sbuf_tensor(name, shape, dt))

        def count(name, start=1):
            c = Count(ctx, nc, name, start)
            counts.append(c)
            return c

        counts = []
        pe, act, dve, pool, sp = nc.tensor, nc.scalar, nc.vector, nc.gpsimd, nc.sync
        MAIN = [ENG.PE, ENG.Activation, ENG.DVE, ENG.Pool]

        RAW = sb("RAW", [P, RAW_SLOTS, BLK])
        HI = sb("HI", [P, HL_SLOTS, BLK], F32R)
        LO = sb("LO", [P, HL_SLOTS, BLK], F32R)
        XH = sb("XH", [P, 32, S], F32R)
        XL = sb("XL", [P, 32, S], F32R)
        X = sb("X", [P, NH, D])
        Y = sb("Y", [P, NH * D])
        WORK = sb("WORK", [P, 10240])
        IDENT = sb("IDENT", [P, P])
        SWH = sb("SWH", [P, DK * 24], F32R)
        SWL = sb("SWL", [P, DK * 24], F32R)
        GATE = sb("GATE", [P, NH, 24])
        GAIN = sb("GAIN", [P, 7, DK])
        SMALL = sb("SMALL", [P, 512])
        PS = ctx.enter_context(nc.psum_tensor("PS", [P, 8, 512], F32))
        Y3 = Y[:, :].rearrange("p (h n) -> p h n", h=NH)

        used = {}

        def work(name, at, n, *dims):
            assert at + n <= 10240, name
            v = WORK[:, at:at + n]
            return v.rearrange("p (a b) -> p a b", a=dims[0]) if dims else v

        def dram(name, cols):
            return nc.dram_tensor(name, (NH, P, cols), F32, kind="Internal").ap()

        BROUT = dram("branches", 3072)
        BTAB = nc.dram_tensor("btab", (24, 384), F32, kind="Internal").ap()
        BROWS = nc.dram_tensor("brows", (P, 24, 384), F32, kind="Internal").ap()
        PROJ, SGATE, PROJ2 = dram("proj", 5632), dram("sgate", 3 * D), dram("proj2", 5120)
        XQ, XKV = dram("xq", D), dram("xkv", 2 * D)

        raw_in = [ctx.enter_context(nc.semaphore(f"raw_in{k}")) for k in range(RAW_SLOTS)]
        hi_done = ctx.enter_context(nc.semaphore("hi_done"))
        lo_done = ctx.enter_context(nc.semaphore("lo_done"))
        pe_done = ctx.enter_context(nc.semaphore("pe_done"))
        ld = [count(f"ld{i}") for i in range(6)]
        ev = [count(f"ev{i}") for i in range(3)]
        st = [count(f"st{i}") for i in range(2)]
        s_stage = count("s_stage")
        sw = [count(f"sw{i}", 0) for i in range(3)]
        s_act = count("s_act")
        s_dve = count("s_dve")
        s_pe = count("s_pe")
        s_tp = count("s_tp")
        s_hi = count("s_hi")
        s_lo = count("s_lo")

        @contextmanager
        def loop(n, per):
            names = {c.name: c for c in counts}
            before = {c.name: c.n for c in counts}
            with nc.Fori(0, n, engines=MAIN) as it:
                Count.loop = (it, per)
                yield it
                Count.loop = None
            bad = {c.name: c.used for c in counts if c.used != per.get(c.name, 0)}
            assert not bad, bad
            for c in counts:
                c.n = before[c.name] + n * c.used
                c.used = 0

        def A(i):
            return s_act.inc(i)

        def V(i):
            return s_dve.inc(i)

        def T(i):
            return s_pe.inc(i)

        def seq(i):
            dve.drain()
            return i

        sources = []

        def stream_load():
            b = 0
            for passes, blocks in sources:
                def body(it, base):
                    for k, src in enumerate(blocks):
                        n = base + k
                        sp.wait_ge(lo_done, it * len(blocks) + (n + 1))
                        dst = RAW[:, n % RAW_SLOTS, :]
                        s = src(it)
                        sp.dma_start(dst.rearrange("p (k n) -> p k n", k=s.shape[1]), s).then_inc(raw_in[n % RAW_SLOTS], 16)
                assert len(blocks) % RAW_SLOTS == 0 or passes == 1
                if passes == 1:
                    body(0, b)
                else:
                    with nc.Fori(0, passes, engines=[ENG.SP]) as it:
                        body(it, b)
                b += passes * len(blocks)
            assert b == total

        plan = make_plan(a)
        total = sum(p * len(bl) for p, bl in plan)
        sources.extend(plan)
        at = {"b": 0, "stage": 0}

        def split(b, it=0, per=0):
            if isinstance(it, int) and b >= total:
                return
            raw, hl = b % RAW_SLOTS, b % HL_SLOTS
            act.wait_ge(raw_in[raw], it * (16 * per // RAW_SLOTS) + 16 * (b // RAW_SLOTS + 1))
            act.wait_ge(pe_done, it * per + (b + 1))
            act.activation(HI[:, hl, :], RAW[:, raw, :], ACT.Copy).then_inc(hi_done, 1)
            dve.wait_ge(hi_done, it * per + (b + 1))
            dve.tensor_tensor(LO[:, hl, :], RAW[:, raw, :], HI[:, hl, :].bitcast(F32), ALU.subtract).then_inc(lo_done, 1)

        class Stage:

            def __init__(self, it=0):
                self.passes, blocks = plan[at["stage"]]
                self.per = len(blocks) if self.passes > 1 else 0
                self.base, self.k, self.n, self.it = at["b"], 0, len(blocks), it

            def end(self):
                assert self.k == self.n, (self.k, self.n)
                at["b"] += self.passes * self.n
                at["stage"] += 1

            def gemm(self, blocks, kt0, pair, cols=W512, m=P, lhs=None, hooks={}, ready=None):
                ktb = BLK // cols
                halves = NH if lhs is None else 1
                for j in range(blocks):
                    b = self.base + self.k
                    split(b + LEAD, self.it, self.per)
                    pe.wait_ge(lo_done, self.it * self.per + (b + 1 + RAW_SLOTS))
                    if ready is not None:
                        pe.wait_ge(s_lo.h, ready[j])
                    if j == 0:
                        pe.wait_ge(ev[pair].h, ev[pair].now())
                    for q in range(ktb):
                        kt = j * ktb + q
                        for h in range(halves):
                            o = PS[0:m, 2 * pair + h, 0:cols]
                            if lhs is None:
                                xh, xl = (t[:, kt0 + kt, h * P:h * P + P] for t in (XH, XL))
                            else:
                                xh, xl = lhs(kt)
                            wh, wl = (t[:, b % HL_SLOTS, q * cols:(q + 1) * cols] for t in (HI, LO))
                            pe.matmul(o, xh, wh, start=kt == 0, stop=False)
                            pe.matmul(o, xh, wl, start=False, stop=False)
                            mm = pe.matmul(o, xl, wh, start=False, stop=kt == blocks * ktb - 1)
                    mm.then_inc(pe_done, 1)
                    self.k += 1
                    if j in hooks:
                        hooks[j]()
                return self.it * self.per + (self.base + self.k + HL_SLOTS)

        def pair_ap(pair):
            return PS[:, 2 * pair:2 * pair + 2, :]

        bank_free = [1, 1, 1, 1]

        def transpose_split(src, nk, kt0, gain=None, banks=(4, 5, 6, 7), j0=0):
            for j in range(j0, nk, 2):
                i = banks[(j // 2) % len(banks)]
                if bank_free[i - 4] is not None:
                    pe.wait_ge(s_lo.h, bank_free[i - 4])
                for q in range(2):
                    for h in range(NH):
                        mm = pe.transpose(PS[:, i, q * S + h * P:q * S + h * P + P],
                                          src[:, h, (j + q) * P:(j + q + 1) * P], IDENT[:, :])
                t = s_tp.inc(mm)
                act.wait_ge(s_tp.h, t)
                dve.wait_ge(s_tp.h, t)
                if gain is None:
                    dh, dl = (v[:, bass.ds(kt0 + j, 2), :].rearrange("p a b -> p (a b)") for v in (XH, XL))
                    hi = s_hi.inc(act.activation(dh, PS[:, i, :], ACT.Copy))
                    dve.wait_ge(s_hi.h, hi)
                    lo = s_lo.inc(dve.tensor_tensor(dl, PS[:, i, :], dh.bitcast(F32), ALU.subtract))
                else:
                    for q in range(2):
                        g = gain[:, j + q:j + q + 1]
                        ins = act.activation(XH[:, kt0 + j + q, :], PS[:, i, q * S:(q + 1) * S], ACT.Copy, scale=g)
                    dve.wait_ge(s_hi.h, s_hi.inc(ins))
                    for q in range(2):
                        g = gain[:, j + q:j + q + 1]
                        ins = dve.scalar_tensor_tensor(
                            out=XL[:, kt0 + j + q, :], in0=PS[:, i, q * S:(q + 1) * S], scalar=g,
                            in1=XH[:, kt0 + j + q, :].bitcast(F32), op0=ALU.mult, op1=ALU.subtract)
                    lo = s_lo.inc(ins)
                bank_free[i - 4] = lo
            return lo

        def first_unit(src, gain, kt0=0, then={}, hooks_at=4):
            ready = {}

            def group(j):
                ready[j] = transpose_split(src, 2 * j + 2, kt0, gain, j0=2 * j)

            def lead():
                for j in range(hooks_at):
                    group(j)

            hooks = {j: (lambda j=j: (group(j + hooks_at) if j + hooks_at < 8 else None, then[j]() if j in then else None))
                     for j in range(8)}
            return lead, hooks, ready

        def rstd(sums, out_, v, n, width):
            dve.tensor_scalar(v, sums, 1.0 / n, EPS, ALU.mult, ALU.add)
            dve.drain()
            t = V(dve.reciprocal(out_, v))
            act.wait_ge(s_dve.h, t)
            t = A(act.activation(out_, out_, ACT.Sqrt))
            dve.wait_ge(s_act.h, t)
            sq = SMALL[:, 480:480 + width]
            dve.tensor_tensor(sq, out_, out_, ALU.mult)
            dve.drain()
            dve.tensor_tensor(sq, sq, v, ALU.mult)
            dve.drain()
            dve.tensor_scalar(sq, sq, -0.5, 1.5, ALU.mult, ALU.add)
            dve.drain()
            dve.tensor_tensor(out_, out_, sq, ALU.mult)
            dve.drain()

        def normalize(src, dst, ready=None):
            ss, v, r = SMALL[:, 464:466], SMALL[:, 466:468], SMALL[:, 468:470]
            t = V(dve.drain())
            act.wait_ge(s_dve.h, t)
            if ready:
                for e in (act, dve):
                    e.wait_ge(*ready)
            t = A(act.activation(dst[:, 0, :], src[:, 0, :], ACT.Square, accum_out=ss[:, 0:1]))
            dve.tensor_tensor_reduce(dst[:, 1, :], src[:, 1, :], src[:, 1, :], 1.0, 0.0, ALU.mult, ALU.add, ss[:, 1:2])
            dve.drain()
            dve.wait_ge(s_act.h, t)
            rstd(ss, r, v, D, 2)
            t = V(dve.drain())
            act.wait_ge(s_dve.h, t)
            A(act.activation(dst[:, 0, :], src[:, 0, :], ACT.Copy, scale=r[:, 0:1]))
            dve.tensor_scalar(dst[:, 1, :], src[:, 1, :], r[:, 1:2], None, ALU.mult)
            V(dve.drain())

        def pe_after_both():
            pe.wait_ge(s_dve.h, s_dve.now())
            pe.wait_ge(s_act.h, s_act.now())

        STAGE = work("stage", 0, 2048, 2)

        def store(pair, ready, slot, dst, func=ACT.Copy):
            act.wait_ge(pe_done, ready)
            act.wait_ge(st[slot].h, st[slot].now())
            t = ev[pair].inc(act.activation(STAGE[:, slot, :], pair_ap(pair).rearrange("p h n -> p (h n)"), func))
            act.wait_ge(ev[pair].h, t)
            st[slot].inc(act.dma_start(dst, STAGE[:, slot, :].rearrange("p (h n) -> p h n", h=NH)), 16)

        def add_to_x(pair, ready, cols):
            dve.wait_ge(pe_done, ready)
            ev[pair].inc(dve.tensor_tensor(X[:, :, cols], pair_ap(pair), X[:, :, cols], ALU.add))

        def cols_of(t, c, n=W512):
            return t[:, :, bass.ds(c, n)].rearrange("h p n -> p h n")

        def all_stored():
            for s in st:
                act.wait_ge(s.h, s.now())

        SW = work("sw", 9856, DK * 24)

        def small_load(srcs, n):
            for x in (s_act, s_dve):
                pool.wait_ge(x.h, x.now())
            c = 0
            for x in srcs:
                w = x.shape[1]
                sw[2].inc(pool.dma_start(SW[:, 0:DK * n].rearrange("p (k n) -> p k n", n=n)[:, :, c:c + w],
                                         x.rearrange("(k p) n -> p k n", p=P)), 16)
                c += w

        def small_gemm(n):
            act.wait_ge(sw[2].h, sw[2].now())
            act.wait_ge(s_pe.h, s_pe.now())
            t = A(act.activation(SWH[:, 0:DK * n], SW[:, 0:DK * n], ACT.Copy))
            dve.wait_ge(s_act.h, t)
            t = V(dve.tensor_tensor(SWL[:, 0:DK * n], SW[:, 0:DK * n], SWH[:, 0:DK * n].bitcast(F32), ALU.subtract))
            pe.wait_ge(s_dve.h, t)
            for i in range(4):
                pe.wait_ge(s_lo.h, bank_free[i])
            for h in range(NH):
                o = PS[:, 7, h * n:(h + 1) * n]
                for k in range(DK):
                    wh, wl = (s[:, k * n:(k + 1) * n] for s in (SWH, SWL))
                    xh, xl = (s[:, k, h * P:(h + 1) * P] for s in (XH, XL))
                    pe.matmul(o, xh, wh, start=k == 0, stop=False)
                    pe.matmul(o, xh, wl, start=False, stop=False)
                    mm = pe.matmul(o, xl, wh, start=False, stop=k == DK - 1)
            return T(mm)

        def fence():
            marks = [A(act.drain()), V(dve.drain()), T(pe.drain())]
            for e in (act, dve, pe):
                for s, t in zip((s_act, s_dve, s_pe), marks):
                    e.wait_ge(s.h, t)

        small_load([a["w_in"][0, :, 2560:2584]], 24)
        sp.dma_start(X[:, :, :], a["x"][0].rearrange("(h p) n -> p h n", p=P)).then_inc(ld[1].h, 16)
        ld[1].n += 16
        lo_start = dve.sem_inc(lo_done, RAW_SLOTS)
        pe.sem_inc(pe_done, HL_SLOTS)
        stream_load()
        ld[2].inc(act.dma_start(IDENT[:, :], a["ident"]), 16)
        for i, g in enumerate(["norm_mix", "norm_mlp", "norm_mix_2", "norm_xattn_2", "norm_mem_2", "norm_ffn_2"]):
            ld[2].inc(act.dma_start(GAIN[:, i, :], a[g]), 16)
        for e in (act, dve, pe):
            e.wait_ge(ld[2].h, ld[2].now())
        OH, REL = WORK[0:34, 8192:8704], WORK[0:34, 8704:8728]
        BIAS = work("bias", 2048, 24 * 256, 24)
        sw[0].inc(pool.dma_start(OH, a["onehot"]), 16)
        sw[0].inc(pool.dma_start(REL[0:32, :], a["rel_bias"]), 16)
        sw[0].inc(pool.dma_start(REL[32:34, :], a["maskrows"]), 16)
        pe.wait_ge(sw[0].h, sw[0].now())
        t = T(pe.matmul(PS[0:24, 3, :], REL, OH, start=True, stop=True))
        dve.wait_ge(s_pe.h, t)
        t = V(dve.tensor_copy(WORK[0:24, 8960:9344], PS[0:24, 3, 0:384]))
        pool.wait_ge(s_dve.h, t)
        sw[1].inc(pool.dma_start(BTAB, WORK[0:24, 8960:9344]), 16)
        pool.wait_ge(sw[1].h, sw[1].now())
        sw[1].inc(pool.dma_start(BROWS, BTAB.partition_broadcast(P)), 16)
        pool.wait_ge(sw[1].h, sw[1].now())
        sw[1].inc(pool.dma_start(BIAS, bass.AP(BROWS.tensor, 127, [[24 * 384 - 1, P], [384, 24], [1, 256]])), 16)
        dve.wait_ge(ld[1].h, ld[1].now())
        for b in range(LEAD):
            split(b)
        normalize(X, Y3, (ld[1].h, ld[1].now()))
        pe_after_both()
        lead, hooks1, ready1 = first_unit(Y3, GAIN[:, 0, :])
        lead()

        s = Stage()
        store(0, s.gemm(8, 0, 0, hooks=hooks1, ready=ready1), 0, cols_of(PROJ, 0))
        s.end()
        t = small_gemm(24)
        act.wait_ge(s_pe.h, t)
        A(act.activation(GATE[:, :, :].rearrange("p h n -> p (h n)"), PS[:, 7, 0:48], ACT.Sigmoid))
        for passes, c0 in ((2, 512), (3, 2560)):
            with loop(passes, {"ev0": 1, "ev1": 1, "st0": 16, "st1": 16}) as it:
                s = Stage(it)
                for u in range(2):
                    store(u, s.gemm(8, 0, u), u, cols_of(PROJ, it * 1024 + (c0 + u * 512)))
            s.end()
        all_stored()

        KT = work("kT", 8192, 256)
        AQ = work("aq", 8448, 1024, 2)
        AK = work("ak", 9472, 256, 2)
        AV = work("av", 9728, 256, 2)
        OA = AQ
        LG = Y[:, 0:1536].rearrange("p (i n) -> p i n", i=4)
        PT = Y[:, 1536:3072].rearrange("p (i n) -> p i n", i=4)
        QT = Y[:, 3072:4096].rearrange("p (i n) -> p i n", i=4)
        SINK, MX, NM, RS, RI, ES = (SMALL[:, 8 * i:8 * i + 8] for i in range(6))
        ld[0].inc(act.dma_start(SINK, a["swa_sinks"].rearrange("a n -> (a n)").partition_broadcast(P)), 16)
        dve.wait_ge(ld[0].h, ld[0].now())
        dve.wait_ge(sw[1].h, sw[1].now())
        gate_cols = [0]

        def gate_unit(pair, hooks, base=0, it=None):
            s = Stage(0 if it is None else it)
            r = s.gemm(8, 0, pair, hooks=hooks)
            store(pair, r, pair, cols_of(SGATE, gate_cols[0] if it is None else it * 512 + gate_cols[0]), ACT.Sigmoid)
            return s

        POS = Y[:, 0:64].rearrange("p (w l) -> p w l", w=2)
        W2 = Y[:, 64:576].rearrange("p (w k n) -> p w k n", w=2, k=2)
        KC = Y[:, 576:576 + 32].rearrange("p (g c) -> p g c", g=2)
        VC = Y[:, 608:608 + 256].rearrange("p (g d) -> p g d", g=2)
        HC = Y[:, 864:864 + 256]
        HCT = Y[:, 1120:1120 + 64].rearrange("p (k c) -> p k c", k=2)
        KTC = work("ktc", 8192, 256 + 256)
        NC2 = 2 * N_CMP
        pe_done_of = {}
        act.wait_ge(s_dve.h, s_dve.now())
        for w in range(2):
            ld[4].inc(act.dma_start(POS[:, w, :], a["cmp_pos"][w]), 16)
            ld[4].inc(act.dma_start(W2[:, w, :, :], a["cmp_w2"][0, w].rearrange("(k p) n -> p k n", p=P)), 16)
        CIN = Y[:, 2048:3072].rearrange("p (w h n) -> p w h n", w=2, h=2)
        for w in range(2):
            ld[1].inc(act.dma_start(CIN[:, w, :, :], cols_of(PROJ, 1024 + 256 * w, 256)), 16)
        ld_c = ld[1].now()

        def xc_parts(w):
            return (v[:, 24 + 4 * w:28 + 4 * w, :].rearrange("p a b -> p (a b)")[:, 0:960] for v in (XH, XL))

        def compress_in(w):
            pe.wait_ge(ld[1].h, ld_c)
            for g in range(KVH):
                for h in range(NH):
                    mm = pe.transpose(PS[:, 6 + w, g * S + h * P:g * S + h * P + P], CIN[:, w, h, g * P:g * P + P], IDENT[:, :])
            t = T(mm)
            dve.wait_ge(s_pe.h, t)
            dve.tensor_copy(KTC, PS[:, 6 + w, :])
            dve.drain()
            dve.wait_ge(ld[4].h, ld[4].now())
            xc = Y[:, 3072:4032].rearrange("p (l c) -> p l c", l=32)
            for g in range(KVH):
                for q in range(2):
                    src = KTC[:, g * S + 16 * q:g * S + 16 * q + 240].rearrange("p (c r) -> p r c", r=16)
                    dve.tensor_tensor(xc[:, 16 * q:16 * q + 16, g * N_CMP:(g + 1) * N_CMP], src,
                                      POS[:, w, 16 * q:16 * q + 16].unsqueeze(2).to_broadcast([P, 16, N_CMP]), ALU.add)
            t = V(dve.drain())
            xcf = Y[:, 3072:4032]
            xch, xcl = xc_parts(w)
            act.wait_ge(s_dve.h, t)
            t = A(act.activation(xch, xcf, ACT.Copy))
            dve.wait_ge(s_act.h, t)
            V(dve.tensor_tensor(xcl, xcf, xch.bitcast(F32), ALU.subtract))
            dve.drain()

        s = gate_unit(0, {1: lambda: compress_in(0), 4: lambda: compress_in(1)})
        s.end()
        gate_cols[0] += 512
        pe.wait_ge(s_dve.h, s_dve.now())
        for w in range(2):
            s = Stage()
            xch, xcl = xc_parts(w)
            pe_done_of[w] = s.gemm(8, 0, 2 + w - 1, cols=256, m=NC2,
                                   lhs=lambda kt: (xch[:, kt * NC2:(kt + 1) * NC2], xcl[:, kt * NC2:(kt + 1) * NC2]))
            s.end()
            act.wait_ge(pe_done, pe_done_of[w])
            ev[1 + w].inc(act.activation(HC[0:NC2, :] if w == 0 else Y[0:NC2, 1792:2048], PS[0:NC2, 2 + 2 * w, 0:256],
                                         ACT.Gelu_apprx_tanh))

        def compress_T(w):
            pe.wait_ge(ev[1 + w].h, ev[1 + w].now())
            hc = HC if w == 0 else Y[:, 1792:2048]
            for k in range(2):
                mm = pe.transpose(PS[:, 7, k * 32:k * 32 + NC2], hc[0:NC2, k * P:(k + 1) * P], IDENT[0:NC2, 0:NC2])
            t = T(mm)
            dve.wait_ge(s_pe.h, t)
            V(dve.tensor_copy(HCT[:, :, 0:NC2], PS[:, 7, 0:64].rearrange("p (k c) -> p k c", k=2)[:, :, 0:NC2]))

        def compress_out(w):
            pe.wait_ge(s_dve.h, s_dve.now())
            if w == 0:
                for k in range(2):
                    mm = pe.matmul(PS[:, 6, 0:NC2], W2[:, 0, k, :], HCT[:, k, 0:NC2], start=k == 0, stop=k == 1)
                t = T(mm)
                dve.wait_ge(s_pe.h, t)
                V(dve.tensor_copy(KC[:, :, 0:N_CMP], PS[:, 6, 0:NC2].rearrange("p (g c) -> p g c", g=2)))
            else:
                for g in range(KVH):
                    for k in range(2):
                        mm = pe.matmul(PS[0:N_CMP, 6, g * P:(g + 1) * P], HCT[:, k, g * N_CMP:(g + 1) * N_CMP],
                                       W2[:, 1, k, :], start=k == 0, stop=k == 1)
                t = T(mm)
                dve.wait_ge(s_pe.h, t)
                V(dve.tensor_copy(VC[0:N_CMP, :, :], PS[0:N_CMP, 6, 0:256].rearrange("p (g c) -> p g c", g=2)))

        CQT = Y[:, 2048:4096].rearrange("p (i n) -> p i n", i=8)
        CL = Y[:, 1184:1184 + 240]
        CM = Y[:, 1424:1424 + 240]
        CPT = work("cpt", 9472, 512, 2)
        CR = SMALL[:, 304:320]
        cl4, cm4, cb4 = (v.rearrange("p (h i c) -> p h i c", h=2, i=8) for v in (CL, CM, SMALL[:, 64:304]))
        cl3, cm3 = (v.rearrange("p (i c) -> p i c", i=16) for v in (CL, CM))

        def cmp_bias():
            dve.memset(SMALL[:, 64:304], NEG)
            dve.drain()
            n0 = 7
            dve.tensor_copy(cb4[:, 0, :, 0:n0], BIAS[:, 0:HEADS, P + 31:P + 31 + 16 * (n0 - 1) + 1:16])
            dve.tensor_copy(cb4[:, 1, :, :], BIAS[:, 0:HEADS, 31:31 + 16 * (N_CMP - 1) + 1:16])
            dve.drain()
            dve.tensor_scalar(CM, SMALL[:, 64:304], NEG / 2, None, ALU.is_gt)
            V(dve.drain())

        def cmp_load(g):
            act.wait_ge(s_pe.h, s_pe.now())
            ld[1].inc(act.dma_start(AQ, cols_of(PROJ, 512 * g)), 16)

        def cmp_q(g):
            pe.wait_ge(ld[1].h, ld[1].now())
            pe.wait_ge(s_act.h, s_act.now())
            for i in range(4):
                for h in range(NH):
                    mm = pe.transpose(PS[:, 4 + i // 2, (i % 2) * S + h * P:(i % 2) * S + h * P + P],
                                      AQ[:, h, i * P:(i + 1) * P], IDENT[:, :])
            t = T(mm)
            act.wait_ge(s_pe.h, t)
            A(act.activation(CQT[:, 4 * g:4 * g + 4, :].rearrange("p i n -> p (i n)"),
                             PS[:, 4:6, :].rearrange("p a n -> p (a n)"), ACT.Copy))

        def cmp_logits():
            pe.wait_ge(s_act.h, s_act.now())
            pe.wait_ge(s_dve.h, s_dve.now())
            for h in range(NH):
                for i in range(HEADS):
                    o = (h * HEADS + i) * N_CMP
                    mm = pe.matmul(PS[:, 6, o:o + N_CMP], CQT[:, i, h * P:h * P + P], KC[:, i // GRP, 0:N_CMP],
                                   start=True, stop=True)
            t = T(mm)
            dve.wait_ge(s_pe.h, t)
            for h in range(NH):
                dve.scalar_tensor_tensor(out=cl4[:, h], in0=PS[:, 6, h * 120:h * 120 + 120].rearrange("p (i c) -> p i c", i=8),
                                         scalar=HD ** -0.5, in1=cb4[:, h], op0=ALU.mult, op1=ALU.add)
            dve.drain()
            dve.tensor_reduce(CR, cl3, AX.X, ALU.max)
            dve.drain()
            V(dve.tensor_tensor(cl3, cl3, CR.unsqueeze(2).to_broadcast([P, 16, N_CMP]), ALU.subtract))

        def cmp_softmax():
            act.wait_ge(s_dve.h, s_dve.now())
            t = A(act.activation(CL, CL, ACT.Exp))
            dve.wait_ge(s_act.h, t)
            dve.tensor_tensor(CL, CL, CM, ALU.mult)
            dve.drain()
            dve.tensor_reduce(CR, cl3, AX.X, ALU.add)
            dve.drain()
            dve.tensor_scalar(CR, CR, TINY, None, ALU.max)
            dve.drain()
            dve.reciprocal(CR, CR)
            dve.drain()
            gates = GATE[:, :, :].rearrange("p h (i b) -> p h i b", b=3)
            dve.tensor_tensor(CR.rearrange("p (h i) -> p h i", h=2), CR.rearrange("p (h i) -> p h i", h=2), gates[:, :, :, 0], ALU.mult)
            dve.drain()
            V(dve.tensor_tensor(cl3, cl3, CR.unsqueeze(2).to_broadcast([P, 16, N_CMP]), ALU.mult))

        def cmp_pT(i0):
            pe.wait_ge(s_dve.h, s_dve.now())
            pe.wait_ge(s_act.h, s_act.now())
            for i in range(2):
                for h in range(NH):
                    o = (h * HEADS + i0 + i) * N_CMP
                    mm = pe.transpose(PS[0:N_CMP, 6, (i * 2 + h) * P:(i * 2 + h + 1) * P], CL[:, o:o + N_CMP], IDENT[:, :])
            t = T(mm)
            act.wait_ge(s_pe.h, t)
            A(act.activation(CPT[0:N_CMP, :, :].rearrange("p i n -> p (i n)"), PS[0:N_CMP, 6, :], ACT.Copy))

        def cmp_pv(i0):
            pe.wait_ge(s_act.h, s_act.now())
            for i in range(2):
                for h in range(NH):
                    c = (i0 + i) % GRP
                    mm = pe.matmul(PS[:, 4 + h, c * P:c * P + P], CPT[0:N_CMP, i, h * P:h * P + P],
                                   VC[0:N_CMP, i0 // GRP, :], start=True, stop=True)
            t = T(mm)
            if i0 % GRP == 2:
                dve.wait_ge(s_pe.h, t)
                t = V(dve.tensor_copy(OA[:, :, :], PS[:, 4:6, :]))
                act.wait_ge(s_dve.h, t)
                ld[2].inc(act.dma_start(cols_of(BROUT, 512 * (i0 // GRP)), OA), 16)
                act.wait_ge(ld[2].h, ld[2].now())

        hk = {0: [lambda: compress_T(0), lambda: cmp_load(0)], 1: [lambda: compress_out(0), cmp_bias], 2: [lambda: compress_T(1)],
              3: [lambda: compress_out(1), lambda: cmp_q(0)], 4: [lambda: cmp_load(1)], 6: [lambda: cmp_q(1)], 7: [cmp_logits]}
        def both(hk):
            return {k: (lambda v=v: [f() for f in v]) for k, v in hk.items()}
        gate_unit(0, both(hk)).end()
        gate_cols[0] += 512
        hk = {0: [cmp_softmax], 2: [lambda: cmp_pT(0)], 3: [lambda: cmp_pv(0)], 4: [lambda: cmp_pT(2)], 5: [lambda: cmp_pv(2)],
              6: [lambda: cmp_pT(4)], 7: [lambda: cmp_pv(4)]}
        gate_unit(1, both(hk)).end()
        gate_cols[0] += 512
        hk = {0: [lambda: cmp_pT(6)], 1: [lambda: cmp_pv(6)]}
        gate_unit(0, both(hk)).end()
        gate_cols[0] += 512

        def attention(q0, k0, v0, head0, sink, gate, out0, accumulate, slot):
            per = {"ld1": 48, "s_pe": 4, "s_act": 4, "s_dve": 5, "ev0": 1, "st0": 16, "ld2": 16 * (accumulate + (slot is None))}
            if slot is not None:
                per.update(s_tp=2, s_hi=2, s_lo=2)
            with loop(KVH, per) as g:
                def loads():
                    act.wait_ge(s_pe.h, s_pe.now())
                    act.wait_ge(s_dve.h, s_dve.now())
                    if slot is not None:
                        act.wait_ge(s_tp.h, s_tp.now())
                    act.wait_ge(ld[2].h, ld[2].now())
                    ld[1].inc(act.dma_start(AQ, cols_of(PROJ, g * 512 + q0)), 16)
                    ld[1].inc(act.dma_start(AK, cols_of(PROJ, g * P + k0, P)), 16)
                    ld[1].inc(act.dma_start(AV, cols_of(PROJ, g * P + v0, P)), 16)

                def transposes():
                    pe.wait_ge(s_dve.h, s_dve.now())
                    pe.wait_ge(ld[1].h, ld[1].now())
                    if slot is not None:
                        pe.wait_ge(s_lo.h, s_lo.now())
                    for i in range(GRP):
                        for h in range(NH):
                            pe.transpose(PS[:, 4 + i // 2, (i % 2) * S + h * P:(i % 2) * S + h * P + P],
                                         AQ[:, h, i * P:(i + 1) * P], IDENT[:, :])
                    for h in range(NH):
                        mm = pe.transpose(PS[:, 6, h * P:h * P + P], AK[:, h, :], IDENT[:, :])
                    t = T(mm)
                    act.wait_ge(s_pe.h, t)
                    dve.wait_ge(s_pe.h, t)
                    A(act.activation(QT.rearrange("p i n -> p (i n)"), PS[:, 4:6, :].rearrange("p a n -> p (a n)"), ACT.Copy))
                    V(dve.tensor_copy(KT[:, 0:S], PS[:, 6, 0:S]))
                    if accumulate:
                        ld[2].inc(act.dma_start(OA, cols_of(BROUT, g * 512 + out0)), 16)

                def logits():
                    pe.wait_ge(s_act.h, s_act.now())
                    pe.wait_ge(s_dve.h, s_dve.now())
                    for i in range(GRP):
                        pe.matmul(PS[:, 4 + i, 0:P], QT[:, i, 0:P], KT[:, 0:P], start=True, stop=True)
                        mm = pe.matmul(PS[:, 4 + i, P:3 * P], QT[:, i, P:S], KT[:, 0:S], start=True, stop=True)
                    t = T(mm)
                    dve.wait_ge(s_pe.h, t)
                    hb = BIAS[:, bass.ds(g * GRP + head0, GRP), :]
                    dve.scalar_tensor_tensor(out=LG[:, :, P:3 * P], in0=PS[:, 4:8, P:3 * P], scalar=HD ** -0.5,
                                             in1=hb, op0=ALU.mult, op1=ALU.add)
                    dve.scalar_tensor_tensor(out=LG[:, :, 0:P], in0=PS[:, 4:8, 0:P], scalar=HD ** -0.5,
                                             in1=hb[:, :, P:S], op0=ALU.mult, op1=ALU.add)
                    dve.drain()
                    dve.tensor_reduce(MX[:, 4:8], LG[:, :, P:3 * P], AX.X, ALU.max)
                    dve.tensor_reduce(MX[:, 0:4], LG[:, :, 0:P], AX.X, ALU.max)
                    dve.drain()
                    if sink:
                        sk = SINK[:, bass.ds(g * GRP, GRP)].unsqueeze(1).to_broadcast([P, 2, 4])
                        mx2, es2 = (v.rearrange("p (h i) -> p h i", h=2) for v in (MX, ES))
                        dve.tensor_tensor(mx2, mx2, sk, ALU.max)
                        dve.drain()
                        dve.tensor_tensor(es2, sk, mx2, ALU.subtract)
                    V(dve.tensor_scalar(NM, MX, -1.0, None, ALU.mult))

                def exps(h):
                    act.wait_ge(s_dve.h, s_dve.now())
                    for i in range(GRP):
                        v = LG[:, i, 0:P] if h == 0 else LG[:, i, P:3 * P]
                        c = h * GRP + i
                        act.activation(v, v, ACT.Exp, bias=NM[:, c:c + 1], accum_out=RS[:, c:c + 1])
                    if h == 0:
                        return
                    if sink:
                        act.activation(ES, ES, ACT.Exp)
                    A(act.drain())

                def probs_T():
                    pe.wait_ge(s_act.h, s_act.now())
                    dve.wait_ge(s_act.h, s_act.now())
                    for i in range(GRP):
                        for j in range(3):
                            mm = pe.transpose(PS[:, 4 + i, j * P:(j + 1) * P], LG[:, i, j * P:(j + 1) * P], IDENT[:, :])
                    t = T(mm)
                    if sink:
                        dve.tensor_tensor(RS, RS, ES, ALU.add)
                        dve.drain()
                    dve.tensor_scalar(RS, RS, TINY, None, ALU.max)
                    dve.drain()
                    dve.reciprocal(RI, RS)
                    dve.drain()
                    ri2 = RI.rearrange("p (h i) -> p h i", h=2)
                    if gate:
                        dve.tensor_tensor(ri2, ri2, GATE[:, :, :].rearrange("p h (i b) -> p h i b", b=3)[:, :, bass.ds(g * GRP, GRP), gate], ALU.mult)
                        dve.drain()
                    act.wait_ge(s_pe.h, t)
                    dve.wait_ge(s_pe.h, t)
                    A(act.activation(PT[:, 0:2, :], PS[:, 4:6, 0:3 * P], ACT.Copy))
                    V(dve.tensor_copy(PT[:, 2:4, :], PS[:, 6:8, 0:3 * P]))

                def values():
                    pe.wait_ge(s_act.h, s_act.now())
                    pe.wait_ge(s_dve.h, s_dve.now())
                    for i in range(GRP):
                        c = slice(i * P, (i + 1) * P)
                        pe.matmul(PS[:, 4, c], PT[:, i, 0:P], AV[:, 0, :], start=True, stop=True)
                        pe.matmul(PS[:, 5, c], PT[:, i, P:2 * P], AV[:, 0, :], start=True, stop=False)
                        mm = pe.matmul(PS[:, 5, c], PT[:, i, 2 * P:3 * P], AV[:, 1, :], start=False, stop=True)
                    t = T(mm)
                    dve.wait_ge(s_pe.h, t)
                    if accumulate:
                        dve.wait_ge(ld[2].h, ld[2].now())
                    for h in range(NH):
                        dst = OA[:, h, :].rearrange("p (i n) -> p i n", i=GRP)
                        src = PS[:, 4 + h, :].rearrange("p (i n) -> p i n", i=GRP)
                        r = RI[:, h * GRP:h * GRP + GRP].unsqueeze(2).to_broadcast([P, GRP, P])
                        if accumulate:
                            lg = Y[:, h * 512:h * 512 + 512].rearrange("p (i n) -> p i n", i=GRP)
                            dve.tensor_tensor(lg, src, r, ALU.mult)
                            dve.drain()
                            dve.tensor_tensor(dst, dst, lg, ALU.add)
                        else:
                            dve.tensor_tensor(dst, src, r, ALU.mult)
                    V(dve.drain())

                def result():
                    if slot is None:
                        act.wait_ge(s_dve.h, s_dve.now())
                        ld[2].inc(act.dma_start(cols_of(BROUT, g * 512 + out0), OA), 16)
                        A(act.drain())
                        V(dve.drain())
                        return
                    pe.wait_ge(s_dve.h, s_dve.now())
                    bank_free[:] = [s_lo.now()] * 4
                    transpose_split(OA, 4, g * 4 + slot, banks=(6, 7))
                    V(dve.drain())
                    A(act.drain())

                loads()
                s = gate_unit(0, {1: transposes, 2: logits, 4: lambda: exps(0), 5: lambda: exps(1), 6: probs_T, 7: values}, it=g)
                result()
            s.end()
            gate_cols[0] += 1024
            bank_free[:] = [s_lo.now()] * 4

        attention(0, 1536, 1792, 0, False, 1, 0, True, None)
        attention(0, 2048, 2304, 0, False, 2, 0, True, 16)
        attention(2560, 3584, 3840, 8, True, 0, 1024, False, 24)
        attention(4096, 5120, 5376, 16, False, 0, 2048, False, None)
        fence()
        act.wait_ge(ld[2].h, ld[2].now())
        l = ld[1].inc(act.dma_start(OB := work("ob", 4096, 2048, 2), cols_of(BROUT, 2048, 1024)), 16)
        pe.wait_ge(ld[1].h, l)
        pe.wait_ge(s_lo.h, transpose_split(OB, 8, 0))
        fence()
        all_stored()

        GS = work("gs", 0, 3072, 3)
        TM = work("tm", 3072, 3072, 3)
        with loop(2, {"ld2": 96, "ev0": 2, "ev1": 2, "ev2": 2, "s_dve": 6}) as it:
            s = Stage(it)
            for cc in range(2):
                act.wait_ge(s_dve.h, s_dve.now())
                for m in range(3):
                    ld[2].inc(act.dma_start(GS[:, m, :].rearrange("p (h n) -> p h n", h=2),
                                            cols_of(SGATE, it * 1024 + (m * D + cc * 512))), 16)
                gl = ld[2].now()
                for m in range(3):
                    r = s.gemm(4, (16, 24, 0)[m], m)
                    dve.wait_ge(pe_done, r)
                    dve.wait_ge(ld[2].h, gl)
                    y = Y3[:, :, bass.ds(it * 1024 + cc * 512, 512)]
                    g3, t3 = (v[:, m, :].rearrange("p (h n) -> p h n", h=2) for v in (GS, TM))
                    if m == 0:
                        ev[m].inc(dve.tensor_tensor(y, pair_ap(m), g3, ALU.mult))
                        dve.drain()
                    else:
                        ev[m].inc(dve.tensor_tensor(t3, pair_ap(m), g3, ALU.mult))
                        dve.drain()
                        dve.tensor_tensor(y, y, t3, ALU.add)
                    V(dve.drain())
        s.end()

        def project_add(src=None):
            s = Stage()
            hooks, ready = {}, None
            if src is not None:
                lead, hooks, ready = first_unit(src, None)
                lead()
            add_to_x(1, s.gemm(8, 0, 1, hooks=hooks, ready=ready), slice(0, 512))
            add_to_x(0, s.gemm(8, 0, 0), slice(512, 1024))
            s.end()
            s = Stage()
            for u in range(2):
                add_to_x(1 - u, s.gemm(8, 0, 1 - u), slice(1024 + u * 512, 1536 + u * 512))
            s.end()

        fence()
        project_add(Y3)

        def down(s, pairs=(1, 2, 1, 2)):
            pe.wait_ge(s_lo.h, state["hidden"])
            for c in range(4):
                add_to_x(pairs[c], s.gemm(2, 16, pairs[c]), slice(c * 512, (c + 1) * 512))

        HB = work("hb", 0, 1024, 2)
        SG = work("sg", 1024, 1024)

        def relu_square(r):
            act.wait_ge(pe_done, r)
            act.wait_ge(s_tp.h, s_tp.now())
            t = ev[0].inc(act.activation(SG, pair_ap(0).rearrange("p h n -> p (h n)"), ACT.Relu))
            act.wait_ge(ev[0].h, t)
            return A(act.activation(HB[:, :, :].rearrange("p h n -> p (h n)"), SG, ACT.Square))

        def hidden_T(t):
            pe.wait_ge(s_act.h, t)
            bank_free[2] = bank_free[3] = s_lo.now()
            act.wait_ge(pe_done, down_done())
            state["hidden"] = transpose_split(HB, 4, 16, banks=(6, 7))

        state = {}

        def down_done():
            return state["down"]

        def norm_first(gain):
            fence()
            normalize(X, Y3)
            pe_after_both()
            lead, hooks, ready = first_unit(Y3, gain)
            lead()
            return dict(hooks=hooks, ready=ready)

        first = norm_first(GAIN[:, 1, :])
        s = Stage()
        relu_square(s.gemm(8, 0, 0, **first))
        s.end()
        with loop(15, {"ev0": 1, "ev1": 2, "ev2": 2, "s_act": 1, "s_tp": 2, "s_hi": 2, "s_lo": 2}) as it:
            s = Stage(it)
            state["down"] = it * s.per + (s.base + HL_SLOTS)
            before = s_act.now()
            r = s.gemm(8, 0, 0, hooks={2: lambda: hidden_T(before)})
            relu_square(r)
            down(s)
        s.end()
        state["down"] = at["b"] + HL_SLOTS
        hidden_T(s_act.now())
        s = Stage()
        down(s)
        s.end()

        fence()
        FG = work("fg", 2048, 2048)

        def norm_in_place(gain):
            l = ld[0].inc(act.dma_start(FG, gain.partition_broadcast(P)), 16)
            normalize(X, Y3)
            dve.wait_ge(ld[0].h, l)
            dve.wait_ge(s_act.h, s_act.now())
            for h in range(NH):
                dve.tensor_tensor(X[:, h, :], Y3[:, h, :], FG, ALU.mult)

        norm_in_place(a["norm_final"])

        MEM = work("mem", 2048, 4096, 2)
        first = norm_first(GAIN[:, 2, :])

        def mem_load():
            act.wait_ge(s_dve.h, s_dve.now())
            ld[1].inc(act.dma_start(MEM, a["mem_2"][0].rearrange("(h p) n -> p h n", p=P)), 16)

        def mem_norm():
            pe_marks = s_tp.now()
            act.wait_ge(s_tp.h, pe_marks)
            dve.wait_ge(s_tp.h, pe_marks)
            normalize(MEM, Y3, (ld[1].h, ld[1].now()))

        def mem_T(j):
            if j == 0:
                pe_after_both()
            transpose_split(Y3, 4 * j + 4, 16, GAIN[:, 4, :], j0=4 * j)

        mem_load()
        s = Stage()
        h0 = dict(first["hooks"])
        store(0, s.gemm(8, 0, 0, hooks={**h0, 7: mem_norm}, ready=first["ready"]), 0, cols_of(PROJ2, 0))
        store(1, s.gemm(8, 0, 1, hooks={2 + j: (lambda j=j: mem_T(j)) for j in range(4)}), 1, cols_of(PROJ2, 512))
        s.end()
        with loop(4, {"ev0": 1, "ev1": 1, "st0": 16, "st1": 16}) as it:
            s = Stage(it)
            for u in range(2):
                store(u, s.gemm(8, 0, u), u, cols_of(PROJ2, it * 1024 + (1024 + u * 512)))
        s.end()
        fence()
        all_stored()

        PU = Y[:, 0:2048].rearrange("p (h n) -> p h n", h=2)
        BAND = work("band", 0, 2048).rearrange("p (g h n) -> p g h n", g=4, h=2)
        PW = work("pw", 2048, 2048).rearrange("p (g k n) -> p g k n", g=4, k=2)
        PP = work("pp", 4096, 2048, 8)
        PSC = SMALL[:, 0:8]
        act.wait_ge(s_dve.h, s_dve.now())
        ld[0].inc(act.dma_start(PU, cols_of(PROJ2, 0, 1024)), 16)
        ld[0].inc(act.dma_start(BAND, a["band"].rearrange("g (h p) n -> p g h n", p=P)), 16)
        ld[0].inc(act.dma_start(PW, a["pool_w_2"][0].rearrange("g (k p) n -> p g k n", p=P)), 16)
        ld[0].inc(act.dma_start(PSC, a["pool_scale_2"]), 16)
        for e in (pe, act, dve):
            e.wait_ge(ld[0].h, ld[0].now())
        for g in range(4):
            for k in range(2):
                c = 2 * g + k
                if c >= 4:
                    pe.wait_ge(s_act.h, s_act.now())
                for h in range(NH):
                    mm = pe.matmul(PS[:, c % 4, 0:S], PU[:, h, c * P:(c + 1) * P], BAND[:, g, h, :], start=h == 0, stop=h == 1)
                t = T(mm)
                act.wait_ge(s_pe.h, t)
                A(act.activation(PP[:, c, :], PS[:, c % 4, 0:S], ACT.Copy))
        pe.wait_ge(s_act.h, s_act.now())
        for g in range(4):
            for k in range(2):
                c = 2 * g + k
                if c >= 4:
                    pe.wait_ge(s_dve.h, s_dve.now())
                for j in range(2):
                    mm = pe.matmul(PS[:, c % 4, 0:S], PW[:, g, j, k * P:(k + 1) * P], PP[:, 2 * g + j, :], start=j == 0, stop=j == 1)
                t = T(mm)
                act.wait_ge(s_pe.h, t)
                t = A(act.activation(XH[:, c, :], PS[:, c % 4, 0:S], ACT.Copy, scale=PSC[:, c:c + 1]))
                dve.wait_ge(s_act.h, t)
                V(dve.scalar_tensor_tensor(out=XL[:, c, :], in0=PS[:, c % 4, 0:S], scalar=PSC[:, c:c + 1],
                                           in1=XH[:, c, :].bitcast(F32), op0=ALU.mult, op1=ALU.subtract))
        fence()

        QF = Y[:, 0:1024].rearrange("p (h n) -> p h n", h=2)
        FF = Y[:, 1024:2048].rearrange("p (h n) -> p h n", h=2)
        AA = Y[:, 2048:3072]
        EE = [Y[:, 3072:4096], Y[:, 1024:2048]]
        VV = work("vv", 2048, 1024, 2)
        QQ = work("qq", 3072, 1024)
        KK = work("kk", 4096, 1024)
        SC = work("sc", 5120, 1536, 4)
        MASK = work("mask", 6656, 1024, 8)
        ONE = work("one", 7680, 256)
        HO = work("ho", 7936, 1024, 2)
        LB = SMALL[:, 16:24]
        LB1 = SMALL[:, 24:32]
        HG = SMALL[:, 32:160]
        L2 = SMALL[:, 160:176]
        HS, HV, HR = SMALL[:, 176:184], SMALL[:, 184:192], SMALL[:, 192:200]
        ld[0].inc(act.dma_start(MASK, a["levels"].rearrange("l p n -> p l n")), 16)
        ld[0].inc(act.dma_start(HG, a["hgrn_norm_2"][0].partition_broadcast(P)), 16)
        ld[0].inc(act.dma_start(L2, a["hgrn_lb_logits_2"]), 16)
        dve.memset(WORK[:, 5120:6656], 0.0)
        dve.memset(ONE, 1.0)
        dve.drain()
        dve.memset(ONE.rearrange("p (c t) -> p c t", t=64)[:, :, 0:1], 0.0)
        dve.wait_ge(ld[0].h, ld[0].now())
        t = V(dve.tensor_tensor(L2[:, 0:8], L2[:, 0:8], L2[:, 8:16], ALU.subtract))
        act.wait_ge(s_dve.h, t)
        A(act.activation(LB, L2[:, 0:8], ACT.Sigmoid))
        A(act.activation(LB1, L2[:, 0:8], ACT.Sigmoid, scale=-1.0))
        fence()
        levels = [32, 16, 8, 4, 2, 1, 0, 64, 128]
        per = {"ld1": 48, "ld2": 16, "s_pe": 11, "s_act": 15, "s_dve": 30, "ev0": 2, "ev1": 2, "st0": 32, "st1": 32,
               "s_tp": 2, "s_hi": 2, "s_lo": 2}
        with loop(2, per) as g:
            q_ps, f_ps = (PS[:, b:b + 2, :].rearrange("p a n -> p (a n)") for b in (4, 6))

            def loads():
                act.wait_ge(s_pe.h, s_pe.now())
                act.wait_ge(s_dve.h, s_dve.now())
                ld[1].inc(act.dma_start(QF, cols_of(PROJ2, g * 512 + 1024)), 16)
                ld[1].inc(act.dma_start(FF, cols_of(PROJ2, g * 512 + 2048)), 16)
                ld[1].inc(act.dma_start(VV, cols_of(PROJ2, g * 512 + 3072)), 16)

            def transposes():
                pe.wait_ge(ld[1].h, ld[1].now())
                pe.wait_ge(s_dve.h, s_dve.now())
                pe.wait_ge(s_lo.h, s_lo.now())
                for src, bank in ((QF, 4), (FF, 6)):
                    for i in range(4):
                        for h in range(NH):
                            mm = pe.transpose(PS[:, bank + i // 2, (i % 2) * S + h * P:(i % 2) * S + h * P + P],
                                              src[:, h, i * P:(i + 1) * P], IDENT[:, :])
                act.wait_ge(s_pe.h, T(mm))
                ld[2].inc(act.dma_start(QF, cols_of(PROJ2, g * 512 + 4096)), 16)
                A(act.activation(EE[0], q_ps, ACT.Sigmoid))
                A(act.activation(KK, f_ps, ACT.Sigmoid, scale=-1.0))
                A(act.activation(AA, f_ps, ACT.Sigmoid))

            def forget():
                dve.wait_ge(s_act.h, s_act.now())
                V(dve.tensor_tensor(QQ, q_ps, EE[0], ALU.mult))
                for i in range(4):
                    c = slice(i * S, (i + 1) * S)
                    lb, lb1 = (v[:, bass.ds(g * 4 + i, 1)] for v in (LB, LB1))
                    dve.tensor_scalar(KK[:, c], KK[:, c], lb1, None, ALU.mult)
                    dve.tensor_scalar(AA[:, c], AA[:, c], lb1, lb, ALU.mult, ALU.add)
                dve.drain()
                V(dve.tensor_scalar(AA, AA, 1e-19, None, ALU.max))

            def log_sum():
                act.wait_ge(s_dve.h, s_dve.now())
                dve.wait_ge(s_act.h, A(act.activation(EE[0], AA, ACT.Ln)))
                for i in range(4):
                    c = slice(i * S, (i + 1) * S)
                    dve.tensor_tensor_scan(AA[:, c], ONE, EE[0][:, c], 0.0, ALU.mult, ALU.add)
                V(dve.drain())

            def blocks_of(H, *v):
                return [x.rearrange("p (b n) -> p b n", n=2 * H) for x in v]

            def exponents(n):
                H = levels[n]
                if not H:
                    return
                e = EE[n % 2]
                av, ev_ = blocks_of(H, AA, e)
                nb = 1024 // (2 * H)
                if H >= 64:
                    dve.tensor_tensor(av[:, :, H:2 * H], av[:, :, H:2 * H],
                                      av[:, :, H - 1:H].to_broadcast([P, nb, H]), ALU.add)
                    dve.drain()
                ref = av[:, :, H - 1:H].to_broadcast([P, nb, H])
                dve.wait_ge(s_pe.h, s_pe.now())
                dve.tensor_tensor(ev_[:, :, H:2 * H], av[:, :, H:2 * H], ref, ALU.subtract)
                act.wait_ge(s_dve.h, V(dve.tensor_tensor(ev_[:, :, 0:H], ref, av[:, :, 0:H], ALU.subtract)))
                A(act.activation(e, e, ACT.Exp))

            exp_done = {}

            def factors(n):
                H = levels[n]
                if not H:
                    return
                ev_, qv, kv = blocks_of(H, EE[n % 2], QQ, KK)
                dve.wait_ge(s_act.h, exp_done[n])
                dve.tensor_tensor(ev_[:, :, H:2 * H], ev_[:, :, H:2 * H], qv[:, :, H:2 * H], ALU.mult)
                exp_done[n, "f"] = V(dve.tensor_tensor(ev_[:, :, 0:H], ev_[:, :, 0:H], kv[:, :, 0:H], ALU.mult))

            def products(n):
                H = levels[n]
                lft, rgt = (EE[n % 2], EE[n % 2]) if H else (KK, QQ)
                if H:
                    pe.wait_ge(s_dve.h, exp_done[n, "f"])
                b = 4 if n % 2 == 0 else 6
                if n >= 2:
                    pe.wait_ge(s_dve.h, exp_done[n - 2, "m"])
                if H == 128:
                    for i in range(4):
                        mm = pe.matmul(PS[:, b, i * P:(i + 1) * P], lft[:, i * S:i * S + P], rgt[:, i * S + P:(i + 1) * S],
                                       start=True, stop=True)
                else:
                    for i in range(4):
                        for h in range(NH):
                            c = slice(i * S + h * P, i * S + h * P + P)
                            mm = pe.matmul(PS[:, b + h, i * P:(i + 1) * P], lft[:, c], rgt[:, c], start=True, stop=True)
                exp_done[n, "p"] = T(mm)

            def masked(n):
                H = levels[n]
                b = 4 if n % 2 == 0 else 6
                dve.wait_ge(s_pe.h, exp_done[n, "p"])
                if H == 128:
                    exp_done[n, "m"] = V(dve.tensor_copy(SC[:, :, P:2 * P], PS[:, b, :].rearrange("p (i n) -> p i n", i=4)))
                    return
                mk = MASK[:, {64: 0, 32: 1, 16: 2, 8: 3, 4: 4, 2: 5, 1: 6, 0: 7}[H], :].bitcast(U32).unsqueeze(1).to_broadcast([P, 4, P])
                dve.memset(SMALL[:, 500:501], 0.0)
                for h in range(NH):
                    ins = dve.copy_predicated(SC[:, :, 2 * h * P:(2 * h + 1) * P], mk,
                                              PS[:, b + h, :].rearrange("p (i n) -> p i n", i=4))
                exp_done[n, "m"] = V(ins)

            def out_products():
                pe.wait_ge(s_dve.h, s_dve.now())
                for i in range(4):
                    c = slice(i * P, (i + 1) * P)
                    pe.matmul(PS[:, 4, c], SC[:, i, 0:P], VV[:, 0, c], start=True, stop=True)
                    pe.matmul(PS[:, 5, c], SC[:, i, P:2 * P], VV[:, 0, c], start=True, stop=False)
                    mm = pe.matmul(PS[:, 5, c], SC[:, i, 2 * P:3 * P], VV[:, 1, c], start=False, stop=True)
                T(mm)

            qff = QF.rearrange("p h n -> p (h n)")

            def out_squares():
                act.wait_ge(s_pe.h, s_pe.now())
                A(act.activation(EE[1], PS[:, 4:6, :].rearrange("p a n -> p (a n)"), ACT.Square))
                act.wait_ge(ld[2].h, ld[2].now())
                A(act.activation(EE[0], qff, ACT.Sigmoid))

            def out_norm():
                dve.wait_ge(s_act.h, s_act.now())
                dve.wait_ge(ld[2].h, ld[2].now())
                dve.tensor_reduce(HS, EE[1].rearrange("p (i n) -> p i n", i=8), AX.X, ALU.add)
                dve.tensor_tensor(EE[0], EE[0], qff, ALU.mult)
                dve.drain()
                rstd(HS, HR, HV, P, 8)

            def out_gate():
                e8 = EE[0].rearrange("p (i n) -> p i n", i=8)
                dve.tensor_tensor(e8, e8, HR.unsqueeze(2).to_broadcast([P, 8, P]), ALU.mult)
                dve.drain()
                dve.tensor_tensor(e8, e8, HG.unsqueeze(1).to_broadcast([P, 8, P]), ALU.mult)
                dve.drain()
                dve.tensor_tensor(HO[:, :, :], PS[:, 4:6, :], EE[0].rearrange("p (h n) -> p h n", h=2), ALU.mult)
                V(dve.drain())

            def out_T():
                pe.wait_ge(s_dve.h, s_dve.now())
                bank_free[:] = [s_lo.now()] * 4
                transpose_split(HO, 4, g * 4 + 8, banks=(6, 7))

            def exps_of(n):
                exponents(n)
                exp_done[n] = s_act.now()

            steps = {1: [transposes], 3: [forget], 4: [log_sum], 6: [lambda: exps_of(0)]}
            for n in range(len(levels)):
                k = 7 + 2 * n
                steps[k] = [lambda n=n: masked(n - 1)] if n else []
                if n + 1 < len(levels):
                    steps[k].append(lambda n=n: exps_of(n + 1))
                steps[k].append(lambda n=n: factors(n))
                steps[k + 1] = [lambda n=n: products(n)]
            last = 8 + 2 * len(levels)
            steps[last - 1] = [lambda: masked(len(levels) - 1)]
            steps[last] = [out_products]
            steps[last + 1] = [out_squares]
            steps[last + 2] = [out_norm]
            steps[last + 3] = [out_gate]
            steps[last + 5] = [out_T]
            loads()
            s = Stage(g)
            for u in range(4):
                hooks = {k - 8 * u: (lambda v=v: [f() for f in v]) for k, v in steps.items() if 8 * u <= k < 8 * u + 8}
                store(u % 2, s.gemm(8, 16, u % 2, hooks=hooks), u % 2, cols_of(XKV, g * D + u * 512))
        s.end()
        fence()
        bank_free[:] = [s_lo.now()] * 4
        project_add()

        all_stored()
        MQ = work("mq", 2048, 1024, 2)
        MK = work("mk", 3072, 1024, 2)
        MV = work("mv", 4096, 1024, 2)
        MQT = work("mqt", 5120, 1024, 4)
        MKT = work("mkt", 6144, 1024, 4)
        MP = work("mp", 7168, 512, 2)
        MPT = work("mpt", 7680, 512, 2)
        MO = work("mo", 8192, 1024, 2)
        M1, M2, M3 = SMALL[:, 0:2], SMALL[:, 2:4], SMALL[:, 4:6]
        XD = float(W512) ** -0.5

        def cross(g):
            def loads():
                act.wait_ge(s_pe.h, s_pe.now())
                for i in range(2):
                    act.wait_ge(st[i].h, st[i].now())
                for dst, src, c in ((MQ, XQ, 0), (MK, XKV, 0), (MV, XKV, D)):
                    ld[1].inc(act.dma_start(dst, cols_of(src, g * 512 + c)), 16)

            def transposes():
                pe.wait_ge(ld[1].h, ld[1].now())
                pe.wait_ge(s_dve.h, s_dve.now())
                pe.wait_ge(s_lo.h, s_lo.now())
                for src, bank in ((MQ, 4), (MK, 6)):
                    for i in range(4):
                        for h in range(NH):
                            pe.transpose(PS[:, bank + i // 2, (i % 2) * S + h * P:(i % 2) * S + h * P + P],
                                         src[:, h, i * P:(i + 1) * P], IDENT[:, :])
                t = T(pe.drain())
                act.wait_ge(s_pe.h, t)
                dve.wait_ge(s_pe.h, t)
                A(act.activation(MQT.rearrange("p i n -> p (i n)"), PS[:, 4:6, :].rearrange("p a n -> p (a n)"), ACT.Copy))
                V(dve.tensor_copy(MKT.rearrange("p i n -> p (i n)"), PS[:, 6:8, :].rearrange("p a n -> p (a n)")))

            def scores():
                pe_after_both()
                for h in range(NH):
                    for k in range(4):
                        mm = pe.matmul(PS[:, 4 + h, 0:S], MQT[:, k, h * P:(h + 1) * P], MKT[:, k, :], start=k == 0, stop=k == 3)
                dve.wait_ge(s_pe.h, T(mm))
                dve.tensor_reduce(M1, PS[:, 4:6, 0:S], AX.X, ALU.max)
                dve.drain()
                V(dve.tensor_scalar(M1, M1, -XD, None, ALU.mult))

            def softmax():
                act.wait_ge(s_dve.h, s_dve.now())
                for h in range(NH):
                    act.activation(MP[:, h, :], PS[:, 4 + h, 0:S], ACT.Exp, scale=XD, bias=M1[:, h:h + 1], accum_out=M2[:, h:h + 1])
                A(act.drain())

            def probs_T():
                pe.wait_ge(s_act.h, s_act.now())
                dve.wait_ge(s_act.h, s_act.now())
                dve.reciprocal(M3, M2)
                V(dve.drain())
                for k in range(2):
                    for h in range(NH):
                        mm = pe.transpose(PS[:, 6, k * S + h * P:k * S + h * P + P], MP[:, h, k * P:(k + 1) * P], IDENT[:, :])
                act.wait_ge(s_pe.h, T(mm))
                A(act.activation(MPT.rearrange("p k n -> p (k n)"), PS[:, 6, :], ACT.Copy))

            def values():
                pe.wait_ge(s_act.h, s_act.now())
                for h in range(NH):
                    for k in range(2):
                        mm = pe.matmul(PS[:, 4 + h, :], MPT[:, k, h * P:(h + 1) * P], MV[:, k, :], start=k == 0, stop=k == 1)
                dve.wait_ge(s_pe.h, T(mm))
                for h in range(NH):
                    dve.tensor_scalar(MO[:, h, :], PS[:, 4 + h, :], M3[:, h:h + 1], None, ALU.mult)
                V(dve.drain())

            def result():
                pe.wait_ge(s_dve.h, s_dve.now())
                bank_free[:] = [s_lo.now()] * 4
                state["hidden"] = transpose_split(MO, 4, 16, banks=(6, 7))
                V(dve.drain())

            return loads, {1: transposes, 2: scores, 3: softmax, 4: probs_T, 5: values}, result

        def add_head(s, hooks={}):
            pe.wait_ge(s_lo.h, state["hidden"])
            for c in range(4):
                hk = {k - 2 * c: f for k, f in hooks.items() if 2 * c <= k < 2 * c + 2}
                add_to_x(c % 2, s.gemm(2, 16, c % 2, hooks=hk), slice(c * 512, (c + 1) * 512))

        first = norm_first(GAIN[:, 3, :])
        for u in range(4):
            extra = dict(first) if u == 0 else {}
            result = None
            if u == 3:
                loads, hooks, result = cross(0)
                loads()
                extra = dict(hooks=hooks)
            s = Stage()
            store(u % 2, s.gemm(8, 0, u % 2, **extra), u % 2, cols_of(XQ, u * 512))
            s.end()
        result()
        with loop(3, {"ld1": 48, "s_pe": 4, "s_act": 3, "s_dve": 5, "ev0": 2, "ev1": 2, "s_tp": 2, "s_hi": 2, "s_lo": 2}) as it:
            s = Stage(it)
            state["hidden"] = s_lo.now()
            loads, hooks, result = cross(it + 1)
            loads()
            add_head(s, hooks)
            act.wait_ge(pe_done, s.it * s.per + (s.base + s.k + HL_SLOTS))
            result()
        s.end()
        state["hidden"] = s_lo.now()
        s = Stage()
        add_head(s)
        s.end()
        bank_free[:] = [s_lo.now()] * 4

        small_load([a["router_group_2"][0], a["router_expert_2"][0]], 20)
        fence()
        normalize(X, Y3)
        pe_after_both()
        pe.wait_ge(s_lo.h, transpose_split(Y3, DK, 0, GAIN[:, 5, :]))
        t = small_gemm(20)
        COMB = GATE[:, :, 0:16]
        act.wait_ge(s_pe.h, t)
        LGT = SMALL[:, 0:40].rearrange("p (h n) -> p h n", h=2)
        t = A(act.activation(SMALL[:, 0:40], PS[:, 7, 0:40], ACT.Copy))
        RANK = SMALL[:, 40:44]
        l = ld[0].inc(act.dma_start(RANK, a["rank"][0].partition_broadcast(P)), 16)
        dve.wait_ge(s_act.h, t)
        dve.wait_ge(ld[0].h, l)
        rank2 = RANK.unsqueeze(1).to_broadcast([P, 2, 4])
        R1 = SMALL[:, 48:50]
        E4, OHG, SEL, O1, O2, WG = (SMALL[:, 56 + 8 * i:64 + 8 * i].rearrange("p (h n) -> p h n", h=2) for i in range(6))
        T1, T2, PG, WB = (SMALL[:, 112 + 2 * i:114 + 2 * i] for i in range(4))
        BIG = SMALL[:, 128:160].rearrange("p (h n) -> p h n", h=2)

        def b4(v):
            return v.unsqueeze(2).to_broadcast([P, 2, 4])

        def first_max(x, top, onehot):
            dve.tensor_reduce(top, x, AX.X, ALU.max)
            dve.drain()
            dve.tensor_tensor(onehot, x, b4(top), ALU.is_equal)
            dve.drain()
            dve.tensor_tensor(onehot, onehot, rank2, ALU.mult)
            dve.drain()
            dve.tensor_reduce(R1, onehot, AX.X, ALU.max)
            dve.drain()
            dve.tensor_tensor(onehot, onehot, b4(R1), ALU.is_equal)
            dve.drain()

        grp = LGT[:, :, 0:4]
        first_max(grp, T1, OHG)
        t = V(dve.tensor_tensor(E4, grp, b4(T1), ALU.subtract))
        act.wait_ge(s_dve.h, t)
        t = A(act.activation(E4, E4, ACT.Exp))
        dve.wait_ge(s_act.h, t)
        dve.tensor_reduce(PG, E4, AX.X, ALU.add)
        dve.drain()
        dve.reciprocal(PG, PG)
        for j in range(4):
            o = OHG[:, :, j:j + 1].to_broadcast([P, 2, 4])
            x = LGT[:, :, 4 + 4 * j:8 + 4 * j]
            dve.tensor_tensor(E4 if j else SEL, x, o, ALU.mult)
            dve.drain()
            if j:
                dve.tensor_tensor(SEL, SEL, E4, ALU.add)
                dve.drain()
        first_max(SEL, T1, O1)
        dve.scalar_tensor_tensor(out=E4, in0=O1, scalar=-3e38, in1=SEL, op0=ALU.mult, op1=ALU.add)
        dve.drain()
        first_max(E4, T2, O2)
        t = V(dve.tensor_tensor(WB, T2, T1, ALU.subtract))
        act.wait_ge(s_dve.h, t)
        t = A(act.activation(WB, WB, ACT.Exp))
        dve.wait_ge(s_act.h, t)
        dve.tensor_scalar(T1, WB, 1.0, None, ALU.add)
        dve.drain()
        dve.reciprocal(T1, T1)
        dve.drain()
        dve.tensor_tensor(T2, WB, T1, ALU.mult)
        dve.drain()
        dve.tensor_tensor(O1, O1, b4(T1), ALU.mult)
        dve.tensor_tensor(O2, O2, b4(T2), ALU.mult)
        dve.drain()
        dve.tensor_tensor(O1, O1, O2, ALU.add)
        dve.drain()
        dve.tensor_tensor(O1, O1, b4(PG), ALU.mult)
        dve.drain()
        for j in range(4):
            o = OHG[:, :, j:j + 1].to_broadcast([P, 2, 4])
            dve.tensor_tensor(COMB[:, :, 4 * j:4 * j + 4], O1, o, ALU.mult)
        dve.drain()

        def expert_hidden(e, r):
            act.wait_ge(pe_done, r[0])
            act.wait_ge(s_dve.h, s_dve.now())
            t = A(act.activation(SG, pair_ap(0).rearrange("p h n -> p (h n)"), ACT.Sigmoid))
            dve.wait_ge(s_act.h, t)
            sg3 = SG.rearrange("p (h n) -> p h n", h=2)
            ev[0].inc(dve.tensor_tensor(sg3, sg3, pair_ap(0), ALU.mult))
            dve.drain()
            dve.wait_ge(pe_done, r[1])
            dve.wait_ge(s_tp.h, s_tp.now())
            for h in range(NH):
                ins = dve.scalar_tensor_tensor(out=HB[:, h, :], in0=pair_ap(1)[:, h, :], scalar=COMB[:, h, bass.ds(e, 1)],
                                               in1=sg3[:, h, :], op0=ALU.mult, op1=ALU.mult)
            ev[1].inc(ins)
            return V(dve.drain())

        def expert_T(t):
            pe.wait_ge(s_dve.h, t)
            bank_free[2] = bank_free[3] = s_lo.now()
            act.wait_ge(pe_done, down_done())
            state["hidden"] = transpose_split(HB, 4, 16, banks=(6, 7))

        fence()
        s = Stage()
        r = (s.gemm(8, 0, 0), s.gemm(8, 0, 1))
        expert_hidden(0, r)
        s.end()
        with loop(N_EXP - 1, {"ev0": 2, "ev1": 2, "ev2": 2, "s_act": 1, "s_dve": 1, "s_tp": 2, "s_hi": 2, "s_lo": 2}) as it:
            s = Stage(it)
            state["down"] = it * s.per + (s.base + HL_SLOTS)
            before = s_dve.now()
            r0 = s.gemm(8, 0, 0)
            r1 = s.gemm(8, 0, 1, hooks={0: lambda: expert_T(before)})
            expert_hidden(it + 1, (r0, r1))
            down(s, (2, 0, 1, 2))
        s.end()
        state["down"] = at["b"] + HL_SLOTS
        expert_T(s_dve.now())
        s = Stage()
        down(s, (2, 0, 1, 2))
        s.end()
        assert at["b"] == total and at["stage"] == len(plan)

        fence()
        norm_in_place(a["norm_final_2"])
        t = V(dve.drain())
        act.wait_ge(s_dve.h, t)
        st[0].inc(act.dma_start(out[0].rearrange("(h p) n -> p h n", p=P), X[:, :, :]), 16)
        act.wait_ge(st[0].h, st[0].now())
        act.wait_ge(st[1].h, st[1].now())


def make_plan(a):
    plan = []

    def rows(w, r0, kt, c, n):
        return w[r0:r0 + kt * P, bass.ds(c, n)].rearrange("(k p) n -> p k n", p=P)

    def unit(w, per, c0, r0=0, blocks=8):
        return [lambda it, j=j: rows(w, r0 + j * 2 * P, 2, it * per + c0, 512) for j in range(blocks)]

    w_in = a["w_in"][0]
    for passes, c0 in ((1, 0), (2, 512), (3, 2584)):
        n = 1 if passes == 1 else 2
        plan.append((passes, sum((unit(w_in, 1024, c0 + 512 * u) for u in range(n)), [])))
    merge = [(1, unit(w_in, 0, 5656 + 512 * u)) for u in range(4)] + [(2, unit(w_in, 512, 5656 + 2048 + 1024 * u)) for u in range(4)]
    plan.append(merge[0])
    for w in range(2):
        w1 = a["cmp_w1"][0, w]
        plan.append((1, [lambda it, w1=w1, j=j: rows(w1, j * 4 * P, 4, 0, 256) for j in range(8)]))
    plan += merge[1:]
    plan.append((2, sum((unit(a["w_branch"][0, m], 1024, 512 * u, 0, 4) for u in range(2) for m in range(3)), [])))

    def square(w):
        plan.append((1, unit(w, 0, 0) + unit(w, 0, 512)))
        plan.append((1, unit(w, 0, 1024) + unit(w, 0, 1536)))

    def down_blocks(w, row):
        return [lambda it, c=c, j=j: w(it)[bass.ds(row(it) + j * 2 * P, 2 * P), c * 512:(c + 1) * 512]
                .rearrange("(k p) n -> p k n", p=P) for c in range(4) for j in range(2)]

    square(a["w_out"][0])
    w1, w2 = a["w_mlp_in"][0], a["w_mlp_out"][0]
    plan.append((1, unit(w1, 0, 0)))
    plan.append((15, unit(w1, 512, 512) + down_blocks(lambda it: w2, lambda it: it * 512)))
    plan.append((1, down_blocks(lambda it: w2, lambda it: 15 * 512)))
    w = a["w_in_2"][0]
    plan.append((1, unit(w, 0, 0) + unit(w, 0, 512)))
    plan.append((4, unit(w, 1024, 1024) + unit(w, 1024, 1536)))
    wkv = a["xattn_wkv"]
    plan.append((2, sum((unit(wkv, D, 512 * u) for u in range(4)), [])))
    square(a["w_out_2"][0])
    w, wo = a["xattn_wq_2"][0], a["xattn_wo_2"][0]
    plan.append((1, unit(w, 0, 0)))
    plan.append((1, unit(w, 0, 512)))
    plan.append((1, unit(w, 0, 1024)))
    plan.append((1, unit(w, 0, 1536)))
    plan.append((3, down_blocks(lambda it: wo, lambda it: it * 512)))
    plan.append((1, down_blocks(lambda it: wo, lambda it: 3 * 512)))

    wg, wu = (a[n][0].rearrange("e k n -> (e k) n") for n in ("w_gate_2", "w_up_2"))
    wd = a["w_down_2"][0].rearrange("e k n -> (e k) n")

    def expert(w, e0):
        return [lambda it, j=j: w[bass.ds(it * D + (e0 * D + j * 2 * P), 2 * P), :].rearrange("(k p) n -> p k n", p=P)
                for j in range(8)]

    plan.append((1, expert(wg, 0) + expert(wu, 0)))
    plan.append((N_EXP - 1, expert(wg, 1) + expert(wu, 1) + down_blocks(lambda it: wd, lambda it: it * 512)))
    plan.append((1, down_blocks(lambda it: wd, lambda it: (N_EXP - 1) * 512)))
    return plan


def constants():
    dist = np.arange(512) - 256
    n = np.maximum(dist, 0)
    ratio = np.log(np.maximum(n, 1).astype(np.float32) / np.float32(16)) / np.float32(math.log(128 / 16))
    large = np.minimum(16 + (ratio * 16).astype(np.int32), 31)
    bucket = np.where(n < 16, n, large)
    onehot = np.zeros((34, 512), np.float32)
    onehot[bucket, np.arange(512)] = 1.0
    onehot[:32, dist < 0] = 0.0
    onehot[32] = dist < 0
    onehot[33] = dist >= 128
    onehot = np.ascontiguousarray(onehot[:, ::-1])
    maskrows = np.zeros((2, 24), np.float32)
    maskrows[0] = NEG
    maskrows[1, 8:16] = NEG
    t, s = np.arange(S)[None, :], np.arange(S)[:, None]
    band = np.stack([((t - s >= 0) & (t - s < w)) / np.minimum(t + 1, w) - (t == s) for w in (2, 4, 8, 16)]).astype(np.float32)
    q, k = np.arange(P)[None, :], np.arange(P)[:, None]
    levels = [(q // (2 * h) == k // (2 * h)) & (k % (2 * h) < h) & (q % (2 * h) >= h) for h in (64, 32, 16, 8, 4, 2, 1)]
    levels = np.stack(levels + [q == k]).astype(np.float32)
    return {"ident": np.eye(P, dtype=np.float32), "onehot": onehot, "maskrows": maskrows, "band": band,
            "levels": levels, "rank": np.array([[4, 3, 2, 1]], np.float32)}


def by_feature(v):
    v = np.asarray(v)
    return v.reshape(-1, P).T


LAYOUT = {g: by_feature for g in ("norm_mix", "norm_mlp", "norm_mix_2", "norm_xattn_2", "norm_mem_2", "norm_ffn_2",
                                  "pool_scale_2", "hgrn_lb_logits_2")}
LAYOUT["cmp_pos"] = lambda v: np.asarray(v)[0].transpose(0, 2, 1)


def kernel(**inputs):
    from concourse import bacc
    from concourse.bass_utils import run_bass_kernel_spmd

    nc = bacc.Bacc("TRN2", target_bir_lowering=False, num_devices=1)
    arrays, aps = {}, {}
    inputs["xattn_wkv"] = np.concatenate([np.asarray(inputs.pop(n))[0] for n in ("xattn_wk_2", "xattn_wv_2")], axis=1)
    for name, value in {**inputs, **constants()}.items():
        v = np.ascontiguousarray(LAYOUT.get(name, np.asarray)(value))
        arrays[f"in_{name}"] = v
        aps[name] = nc.dram_tensor(f"in_{name}", v.shape, mybir.dt.from_np(v.dtype), kind="ExternalInput").ap()
    out = nc.dram_tensor("out", (1, S, D), F32, kind="ExternalOutput").ap()
    build(nc, aps, out)
    r = run_bass_kernel_spmd(nc, [arrays], core_ids=[0])
    return r.results[0]["out"]
```

```python
from contextlib import ExitStack, contextmanager
import math

import numpy as np
import concourse.bass as bass
from concourse import mybir
from concourse.alu_op_type import AluOpType as ALU

F32 = mybir.dt.float32
F32R = mybir.dt.float32r
U32 = mybir.dt.uint32
I32 = mybir.dt.int32
ACT = mybir.ActivationFunctionType
AX = mybir.AxisListType
ENG = mybir.EngineType

P = 128
D = 2048
S = 256
NH = S // P
DK = D // P
HD = 128
HEADS = 8
KVH = 2
GRP = HEADS // KVH
W512 = 512
EPS = 1e-6
NEG = -1e30
TINY = 1e-30
N_CMP = (S - 32) // 16 + 1
CMP_LEN = 32
N_EXP = 16
RAW_SLOTS = 8
HL_SLOTS = 4
LEAD = 3
HOLD = 2
BLK = 1024
BRANCH = 1024


class Count:

    loop = None

    def __init__(self, ctx, nc, name, start=1):
        self.h, self.name, self.n, self.used = ctx.enter_context(nc.semaphore(name)), name, start, 0
        if start:
            nc.gpsimd.sem_inc(self.h, start)

    def now(self):
        if Count.loop and Count.loop[1].get(self.name):
            it, per = Count.loop
            return it * per[self.name] + (self.n + self.used)
        return self.n + self.used

    def inc(self, instruction, by=1):
        instruction.then_inc(self.h, by)
        if Count.loop:
            assert self.name in Count.loop[1], self.name
            self.used += by
        else:
            self.n += by
        return self.now()


def build(nc, a, out):
    ctx = ExitStack()
    with ctx:
        def sb(name, shape, dt=F32):
            return ctx.enter_context(nc.sbuf_tensor(name, shape, dt))

        def count(name, start=1):
            c = Count(ctx, nc, name, start)
            counts.append(c)
            return c

        counts = []
        pe, act, dve, pool, sp = nc.tensor, nc.scalar, nc.vector, nc.gpsimd, nc.sync
        MAIN = [ENG.PE, ENG.Activation, ENG.DVE, ENG.Pool]

        RAW = sb("RAW", [P, RAW_SLOTS, BLK])
        HI = sb("HI", [P, HL_SLOTS, BLK], F32R)
        LO = sb("LO", [P, HL_SLOTS, BLK], F32R)
        XH = sb("XH", [P, 32, S], F32R)
        XL = sb("XL", [P, 32, S], F32R)
        X = sb("X", [P, NH, D])
        Y = sb("Y", [P, NH * D])
        IDENT = sb("IDENT", [P, P])
        SWH = sb("SWH", [P, DK * 24], F32R)
        SWL = sb("SWL", [P, DK * 24], F32R)
        GATE = sb("GATE", [P, NH, 24])
        GAIN = sb("GAIN", [P, 6, DK])
        SMALL = sb("SMALL", [P, 512])
        FULL = sb("FULL", [P, 1], I32)
        work_memory = ctx.enter_context(ExitStack())
        WORK = work_memory.enter_context(nc.sbuf_tensor("WORK", [P, 10240], F32))
        PS = ctx.enter_context(nc.psum_tensor("PS", [P, 8, 512], F32))
        Y3 = Y[:, :].rearrange("p (h n) -> p h n", h=NH)

        def work(name, at, n, *dims):
            assert at + n <= WORK.shape[1], name
            v = WORK[:, at:at + n]
            return v.rearrange("p (a b) -> p a b", a=dims[0]) if dims else v

        def dram(name, cols):
            return nc.dram_tensor(name, (NH, P, cols), F32, kind="Internal").ap()

        BROUT = dram("branches", 3072)
        BTAB = nc.dram_tensor("btab", (24, 384), F32, kind="Internal").ap()
        BROWS = nc.dram_tensor("brows", (P, 24, 384), F32, kind="Internal").ap()
        PROJ, SGATE, PROJ2 = dram("proj", 5632), dram("sgate", 3 * D), dram("proj2", 5120)
        XQ, XKV = dram("xq", D), dram("xkv", 2 * D)

        raw_in = [ctx.enter_context(nc.semaphore(f"raw_in{k}")) for k in range(RAW_SLOTS // 2)]
        hi_done = ctx.enter_context(nc.semaphore("hi_done"))
        lo_done = ctx.enter_context(nc.semaphore("lo_done"))
        pe_done = ctx.enter_context(nc.semaphore("pe_done"))
        ld = [count(f"ld{i}") for i in range(6)]
        ev = [count(f"ev{i}") for i in range(4)]
        st = [count(f"st{i}") for i in range(2)]
        s_stage = count("s_stage")
        sw = [count(f"sw{i}", 0) for i in range(3)]
        s_act = count("s_act")
        s_dve = count("s_dve")
        s_pool = count("s_pool")
        s_pe = count("s_pe")
        s_tp = count("s_tp")
        s_hi = count("s_hi")
        s_lo = count("s_lo")

        @contextmanager
        def loop(n, per):
            names = {c.name: c for c in counts}
            before = {c.name: c.n for c in counts}
            with nc.Fori(0, n, engines=MAIN) as it:
                Count.loop = (it, per)
                yield it
                Count.loop = None
            bad = {c.name: c.used for c in counts if c.used != per.get(c.name, 0)}
            assert not bad, bad
            for c in counts:
                c.n = before[c.name] + n * c.used
                c.used = 0

        def A(i):
            return s_act.inc(i)

        def V(i):
            return s_dve.inc(i)

        def T(i):
            return s_pe.inc(i)

        def stream_load(plan):
            b = 0
            for passes, tiles in plan:
                def body(it, base, n=2 * len(tiles)):
                    for k, (w, index) in enumerate(tiles):
                        first = base + 2 * k
                        slot = first % RAW_SLOTS
                        sp.wait_ge(lo_done, it * n + (first + 2))
                        src = w[bass.ds(index(it), 1)].rearrange("t p n -> p (t n)")
                        sp.dma_start(RAW[:, slot:slot + 2, :].rearrange("p s n -> p (s n)"), src).then_inc(raw_in[slot // 2], 16)
                assert 2 * len(tiles) % RAW_SLOTS == 0
                if passes == 1:
                    body(0, b)
                else:
                    with nc.Fori(0, passes, engines=[ENG.SP]) as it:
                        body(it, b)
                b += passes * 2 * len(tiles)
            assert b == total

        plan = make_plan(a)
        total = sum(2 * p * len(tiles) for p, tiles in plan)
        at = {"b": 0, "stage": 0}
        held = []

        def split(b, it=0, per=0):
            if isinstance(it, int) and b >= total:
                return
            raw, hl = b % RAW_SLOTS, b % HL_SLOTS
            act.wait_ge(raw_in[raw // 2], it * (16 * per // RAW_SLOTS) + 16 * (b // RAW_SLOTS + 1))
            act.wait_ge(pe_done, it * per + (b + 1))
            act.activation(HI[:, hl, :], RAW[:, raw, :], ACT.Copy).then_inc(hi_done, 1)
            dve.wait_ge(hi_done, it * per + (b + 1))
            dve.tensor_tensor(LO[:, hl, :], RAW[:, raw, :], HI[:, hl, :].bitcast(F32), ALU.subtract).then_inc(lo_done, 1)

        class Stage:

            def __init__(self, it=0):
                self.passes, tiles = plan[at["stage"]]
                self.per = 2 * len(tiles) if self.passes > 1 else 0
                self.base, self.k, self.n, self.it = at["b"], 0, 2 * len(tiles), it

            def end(self):
                assert self.k == self.n, (self.k, self.n)
                at["b"] += self.passes * self.n
                at["stage"] += 1

            def gemm(self, blocks, kt0, pair, cols=W512, m=P, lhs=None, hooks={}, ready=None, bank=None, hold=0):
                ktb = BLK // cols
                halves = NH if lhs is None else 1
                for j in range(blocks):
                    b = self.base + self.k
                    if j < blocks - hold:
                        split(b + LEAD, self.it, self.per)
                    else:
                        held.append((b + LEAD, self.it, self.per))
                    pe.wait_ge(lo_done, self.it * self.per + (b + 1 + RAW_SLOTS))
                    if ready is not None:
                        pe.wait_ge(s_lo.h, ready[j])
                    if j == 0:
                        pe.wait_ge(ev[pair].h, ev[pair].now())
                    for q in range(ktb):
                        kt = j * ktb + q
                        for h in range(halves):
                            o = PS[0:m, 2 * pair + h if bank is None else bank, 0:cols]
                            if lhs is None:
                                xh, xl = (t[:, kt0 + kt, h * P:h * P + P] for t in (XH, XL))
                            else:
                                xh, xl = lhs(kt)
                            wh, wl = (t[:, b % HL_SLOTS, q * cols:(q + 1) * cols] for t in (HI, LO))
                            pe.matmul(o, xh, wh, start=kt == 0, stop=False)
                            pe.matmul(o, xh, wl, start=False, stop=False)
                            mm = pe.matmul(o, xl, wh, start=False, stop=kt == blocks * ktb - 1)
                    mm.then_inc(pe_done, 1)
                    self.k += 1
                    if j in hooks:
                        hooks[j]()
                return self.it * self.per + (self.base + self.k + HL_SLOTS)

        def release():
            for x in held:
                split(*x)
            held.clear()

        def pair_ap(pair):
            return PS[:, 2 * pair:2 * pair + 2, :]

        bank_free = [1, 1, 1, 1]

        def transpose_split(src, nk, kt0, gain=None, banks=(4, 5, 6, 7), j0=0):
            for j in range(j0, nk, 2):
                i = banks[(j // 2) % len(banks)]
                if bank_free[i - 4] is not None:
                    pe.wait_ge(s_lo.h, bank_free[i - 4])
                for q in range(2):
                    for h in range(NH):
                        mm = pe.transpose(PS[:, i, q * S + h * P:q * S + h * P + P],
                                          src[:, h, (j + q) * P:(j + q + 1) * P], IDENT[:, :])
                t = s_tp.inc(mm)
                act.wait_ge(s_tp.h, t)
                dve.wait_ge(s_tp.h, t)
                if gain is None:
                    dh, dl = (v[:, bass.ds(kt0 + j, 2), :].rearrange("p a b -> p (a b)") for v in (XH, XL))
                    hi = s_hi.inc(act.activation(dh, PS[:, i, :], ACT.Copy))
                    dve.wait_ge(s_hi.h, hi)
                    lo = s_lo.inc(dve.tensor_tensor(dl, PS[:, i, :], dh.bitcast(F32), ALU.subtract))
                else:
                    for q in range(2):
                        g = gain[:, j + q:j + q + 1]
                        ins = act.activation(XH[:, kt0 + j + q, :], PS[:, i, q * S:(q + 1) * S], ACT.Copy, scale=g)
                    dve.wait_ge(s_hi.h, s_hi.inc(ins))
                    for q in range(2):
                        g = gain[:, j + q:j + q + 1]
                        ins = dve.scalar_tensor_tensor(
                            out=XL[:, kt0 + j + q, :], in0=PS[:, i, q * S:(q + 1) * S], scalar=g,
                            in1=XH[:, kt0 + j + q, :].bitcast(F32), op0=ALU.mult, op1=ALU.subtract)
                    lo = s_lo.inc(ins)
                bank_free[i - 4] = lo
            return lo

        def first_unit(gain, kt0=0, then={}, scaled=None):
            ready, marks = {}, {}

            def group(j):
                if scaled:
                    for x, t in marks[j // 2]:
                        pe.wait_ge(x, t)
                ready[j] = transpose_split(Y3, 2 * j + 2, kt0, gain, j0=2 * j)

            def lead():
                if scaled:
                    marks.update({q: scale(q, *scaled) for q in range(2)})
                for j in range(4):
                    group(j)
                    if j == 0:
                        release()
                    if scaled and j in (1, 3):
                        marks[j // 2 + 2] = scale(j // 2 + 2, *scaled)

            def hook(j):
                if j < 4:
                    group(j + 4)
                if j in then:
                    then[j]()

            return lead, {j: (lambda j=j: hook(j)) for j in range(8)}, ready

        def scale(q, src, r):
            c = slice(q * 512, (q + 1) * 512)
            a_ = A(act.activation(Y3[:, 0, c], src[:, 0, c], ACT.Copy, scale=r[:, 0:1]))
            v_ = V(dve.tensor_scalar(Y3[:, 1, c], src[:, 1, c], r[:, 1:2], None, ALU.mult))
            return (s_act.h, a_), (s_dve.h, v_)

        def rstd(sums, out_, v, n, width):
            dve.tensor_scalar(v, sums, 1.0 / n, EPS, ALU.mult, ALU.add)
            dve.drain()
            rsqrt(out_, v, width)

        def rsqrt(out_, v, width):
            t = V(dve.reciprocal(out_, v))
            act.wait_ge(s_dve.h, t)
            t = A(act.activation(out_, out_, ACT.Sqrt))
            dve.wait_ge(s_act.h, t)
            sq = SMALL[:, 480:480 + width]
            dve.tensor_tensor(sq, out_, out_, ALU.mult)
            dve.drain()
            dve.tensor_tensor(sq, sq, v, ALU.mult)
            dve.drain()
            dve.tensor_scalar(sq, sq, -0.5, 1.5, ALU.mult, ALU.add)
            dve.drain()
            dve.tensor_tensor(out_, out_, sq, ALU.mult)
            dve.drain()

        R1ST, R2ND = SMALL[:, 468:470], SMALL[:, 470:472]

        def square_sums(src, ready=None):
            ss = SMALL[:, 464:466]
            t = V(dve.drain())
            act.wait_ge(s_dve.h, t)
            if ready:
                for e in (act, dve):
                    e.wait_ge(*ready)
            t = A(act.activation(Y3[:, 0, :], src[:, 0, :], ACT.Square, accum_out=ss[:, 0:1]))
            dve.tensor_tensor_reduce(Y3[:, 1, :], src[:, 1, :], src[:, 1, :], 1.0, 0.0, ALU.mult, ALU.add, ss[:, 1:2])
            dve.drain()
            dve.wait_ge(s_act.h, t)
            rstd(ss, R1ST, SMALL[:, 466:468], D, 2)
            act.wait_ge(s_dve.h, V(dve.drain()))

        def normalize(src, ready=None):
            square_sums(src, ready)
            for q in range(4):
                scale(q, src, R1ST)

        SUMS = SMALL[:, 448:464].rearrange("p (w h c) -> p w h c", w=2, h=2)

        def column_sums(c, gain=None):
            cols = slice(c * 512, (c + 1) * 512)
            marks = [V(dve.drain())]
            if gain is not None:
                dve.tensor_tensor(Y3[:, :, cols], X[:, :, cols], gain[:, cols].unsqueeze(1).to_broadcast([P, 2, 512]), ALU.mult)
                marks.append(V(dve.drain()))
            if c == 0:
                act.activation(SMALL[:, 500:501], IDENT[:, 0:1], ACT.Sqrt)
                act.wait_ge(s_lo.h, s_lo.now())
            for w, (src, t) in enumerate(zip((X, Y3), marks)):
                act.wait_ge(s_dve.h, t)
                act.drain()
                for h in range(NH):
                    ins = act.activation(PS[:, 6 + h, :], src[:, h, cols], ACT.Square, accum_out=SUMS[:, w, h, c:c + 1])
                A(ins)

        def factors_of_x(twice=False):
            n = 4 if twice else 2
            ss, v = SMALL[:, 464:464 + n], SMALL[:, 472:472 + n]
            dve.wait_ge(s_act.h, s_act.now())
            dve.tensor_reduce(ss, SMALL[:, 448:448 + 4 * n].rearrange("p (w c) -> p w c", c=4), AX.X, ALU.add)
            dve.drain()
            dve.tensor_scalar(v[:, 0:2], ss[:, 0:2], 1.0 / D, EPS, ALU.mult, ALU.add)
            dve.drain()
            if twice:
                dve.reciprocal(v[:, 2:4], v[:, 0:2])
                dve.drain()
                dve.tensor_tensor(v[:, 2:4], v[:, 2:4], ss[:, 2:4], ALU.mult)
                dve.drain()
                dve.tensor_scalar(v[:, 2:4], v[:, 2:4], 1.0 / D, EPS, ALU.mult, ALU.add)
                dve.drain()
            rsqrt(SMALL[:, 468:468 + n], v, n)
            if twice:
                dve.tensor_tensor(R2ND, R2ND, R1ST, ALU.mult)
            act.wait_ge(s_dve.h, V(dve.drain()))

        def pe_after_both():
            pe.wait_ge(s_dve.h, s_dve.now())
            pe.wait_ge(s_act.h, s_act.now())

        STAGE = work("stage", 0, 2048, 2)

        def store(pair, ready, slot, dst, func=ACT.Copy):
            act.wait_ge(pe_done, ready)
            act.wait_ge(st[slot].h, st[slot].now())
            t = ev[pair].inc(act.activation(STAGE[:, slot, :], pair_ap(pair).rearrange("p h n -> p (h n)"), func))
            act.wait_ge(ev[pair].h, t)
            st[slot].inc(act.dma_start(dst, STAGE[:, slot, :].rearrange("p (h n) -> p h n", h=NH)), 16)

        def add_to_x(pair, ready, cols):
            dve.wait_ge(pe_done, ready)
            ev[pair].inc(dve.tensor_tensor(X[:, :, cols], pair_ap(pair), X[:, :, cols], ALU.add))

        def cols_of(t, c, n=W512):
            return t[:, :, bass.ds(c, n)].rearrange("h p n -> p h n")

        def all_stored():
            for s in st:
                act.wait_ge(s.h, s.now())

        SW = work("sw", 9856, DK * 24)

        def small_load(srcs, n):
            for x in (s_act, s_dve, s_pe):
                pool.wait_ge(x.h, x.now())
            c = 0
            for x in srcs:
                w = x.shape[1]
                sw[2].inc(pool.dma_start(SW[:, 0:DK * n].rearrange("p (k n) -> p k n", n=n)[:, :, c:c + w],
                                         x.rearrange("(k p) n -> p k n", p=P)), 16)
                c += w

        def small_split(n):
            act.wait_ge(sw[2].h, sw[2].now())
            act.wait_ge(s_pe.h, s_pe.now())
            t = A(act.activation(SWH[:, 0:DK * n], SW[:, 0:DK * n], ACT.Copy))
            dve.wait_ge(s_act.h, t)
            return V(dve.tensor_tensor(SWL[:, 0:DK * n], SW[:, 0:DK * n], SWH[:, 0:DK * n].bitcast(F32), ALU.subtract))

        def small_gemm(n, t, kt0=0):
            pe.wait_ge(s_dve.h, t)
            for i in range(4):
                pe.wait_ge(s_lo.h, bank_free[i])
            for k in range(DK):
                wh, wl = (s[:, k * n:(k + 1) * n] for s in (SWH, SWL))
                xh, xl = (s[:, kt0 + k, :] for s in (XH, XL))
                pe.matmul(PS[0:n, 7, 0:S], wh, xh, start=k == 0, stop=False)
                pe.matmul(PS[0:n, 7, 0:S], wl, xh, start=False, stop=False)
                mm = pe.matmul(PS[0:n, 7, 0:S], wh, xl, start=False, stop=k == DK - 1)
            act.wait_ge(s_pe.h, T(mm))
            pe.wait_ge(s_act.h, A(act.activation(SMALL[0:n, 192:448], PS[0:n, 7, 0:S], ACT.Copy)))
            for h in range(NH):
                mm = pe.transpose(PS[:, 7, h * n:(h + 1) * n], SMALL[0:n, 192 + h * P:192 + (h + 1) * P], IDENT[0:n, 0:n])
            return T(mm)

        def fence():
            marks = [A(act.drain()), V(dve.drain()), T(pe.drain())]
            for e in (act, dve, pe):
                for s, t in zip((s_act, s_dve, s_pe), marks):
                    e.wait_ge(s.h, t)

        small_load([a["w_in_gates"]], 24)
        for h in range(NH):
            sp.dma_start(X[:, h, :], a["x"][0, h * P:(h + 1) * P, :]).then_inc(ld[1].h, 16)
            ld[1].n += 16
        dve.sem_inc(lo_done, RAW_SLOTS)
        pe.sem_inc(pe_done, HL_SLOTS)
        stream_load(plan)
        ld[2].inc(act.dma_start(IDENT[:, :], a["ident"]), 16)
        ld[2].inc(act.dma_start(GAIN[:, :, :].rearrange("p g k -> p (g k)"), a["gains"]), 16)
        square_sums(X, (ld[1].h, ld[1].now()))
        for e in (act, dve, pe):
            e.wait_ge(ld[2].h, ld[2].now())
        OH, REL = WORK[0:34, 8192:8704], WORK[0:34, 8704:8728]
        BIAS = work("bias", 2048, 24 * 256, 24)
        sw[0].inc(pool.dma_start(OH, a["onehot"]), 16)
        sw[0].inc(pool.dma_start(REL[0:32, :], a["rel_bias"]), 16)
        sw[0].inc(pool.dma_start(REL[32:34, :], a["maskrows"]), 16)

        def bias_table():
            pe.wait_ge(sw[0].h, sw[0].now())
            t = T(pe.matmul(PS[0:24, 3, :], REL, OH, start=True, stop=True))
            dve.wait_ge(s_pe.h, t)
            t = V(dve.tensor_copy(WORK[0:24, 8960:9344], PS[0:24, 3, 0:384]))
            pool.wait_ge(s_dve.h, t)
            sw[1].inc(pool.dma_start(BTAB, WORK[0:24, 8960:9344]), 16)
            pool.wait_ge(sw[1].h, sw[1].now())
            sw[1].inc(pool.dma_start(BROWS, BTAB.partition_broadcast(P)), 16)
            pool.wait_ge(sw[1].h, sw[1].now())
            sw[1].inc(pool.dma_start(BIAS, bass.AP(BROWS.tensor, 127, [[24 * 384 - 1, P], [384, 24], [1, 256]])), 16)

        lead, hooks1, ready1 = first_unit(GAIN[:, 0, :], then={5: bias_table}, scaled=(X, R1ST))
        lead()
        for b in range(LEAD):
            split(b)

        s = Stage()
        store(0, s.gemm(8, 0, 0, hooks=hooks1, ready=ready1), 0, cols_of(PROJ, 0))
        s.end()
        t = small_gemm(24, small_split(24))
        act.wait_ge(s_pe.h, t)
        A(act.activation(GATE[:, :, :].rearrange("p h n -> p (h n)"), PS[:, 7, 0:48], ACT.Sigmoid))
        for passes, c0 in ((2, 512), (3, 2560)):
            with loop(passes, {"ev0": 1, "ev1": 1, "st0": 16, "st1": 16}) as it:
                s = Stage(it)
                for u in range(2):
                    store(u, s.gemm(8, 0, u), u, cols_of(PROJ, it * 1024 + (c0 + u * 512)))
            s.end()
        all_stored()

        KT = work("kT", 8192, 256)
        AQ = work("aq", 8448, 1024, 2)
        AK = work("ak", 9472, 256, 2)
        AV = work("av", 9728, 256, 2)
        OA = AQ
        LG = Y[:, 0:1536].rearrange("p (i n) -> p i n", i=4)
        PT = Y[:, 1536:3072].rearrange("p (i n) -> p i n", i=4)
        QT = Y[:, 3072:4096].rearrange("p (i n) -> p i n", i=4)
        SINK, MX, NM, RS, RI, ES = (SMALL[:, 8 * i:8 * i + 8] for i in range(6))
        ld[0].inc(act.dma_start(SINK, a["swa_sinks"].rearrange("a n -> (a n)").partition_broadcast(P)), 16)
        dve.wait_ge(ld[0].h, ld[0].now())
        dve.wait_ge(sw[1].h, sw[1].now())
        gate_cols = [0]

        def gate_unit(pair, hooks, base=0, it=None):
            s = Stage(0 if it is None else it)
            r = s.gemm(8, 0, pair, hooks=hooks)
            store(pair, r, pair, cols_of(SGATE, gate_cols[0] if it is None else it * 512 + gate_cols[0]), ACT.Sigmoid)
            return s

        POS = Y[:, 0:64].rearrange("p (w l) -> p w l", w=2)
        W2 = Y[:, 64:576].rearrange("p (w k n) -> p w k n", w=2, k=2)
        KC = Y[:, 576:576 + 32].rearrange("p (g c) -> p g c", g=2)
        VC = Y[:, 608:608 + 256].rearrange("p (g d) -> p g d", g=2)
        HC = Y[:, 864:864 + 256]
        HCT = Y[:, 1120:1120 + 64].rearrange("p (k c) -> p k c", k=2)
        KTC = work("ktc", 8192, 256 + 256)
        NC2 = 2 * N_CMP
        pe_done_of = {}
        act.wait_ge(s_dve.h, s_dve.now())
        for w in range(2):
            ld[4].inc(act.dma_start(POS[:, w, :], a["cmp_pos"][w]), 16)
            ld[4].inc(act.dma_start(W2[:, w, :, :], a["cmp_w2"][0, w].rearrange("(k p) n -> p k n", p=P)), 16)
        CIN = Y[:, 2048:3072].rearrange("p (w h n) -> p w h n", w=2, h=2)
        for w in range(2):
            ld[1].inc(act.dma_start(CIN[:, w, :, :], cols_of(PROJ, 1024 + 256 * w, 256)), 16)
        ld_c = ld[1].now()

        def xc_parts(w):
            return (v[:, 24 + 4 * w:28 + 4 * w, :].rearrange("p a b -> p (a b)")[:, 0:960] for v in (XH, XL))

        def compress_in(w):
            pe.wait_ge(ld[1].h, ld_c)
            for g in range(KVH):
                for h in range(NH):
                    mm = pe.transpose(PS[:, 6 + w, g * S + h * P:g * S + h * P + P], CIN[:, w, h, g * P:g * P + P], IDENT[:, :])
            t = T(mm)
            dve.wait_ge(s_pe.h, t)
            dve.tensor_copy(KTC, PS[:, 6 + w, :])
            dve.drain()
            dve.wait_ge(ld[4].h, ld[4].now())
            xc = Y[:, 3072:4032].rearrange("p (l c) -> p l c", l=32)
            for g in range(KVH):
                for q in range(2):
                    src = KTC[:, g * S + 16 * q:g * S + 16 * q + 240].rearrange("p (c r) -> p r c", r=16)
                    dve.tensor_tensor(xc[:, 16 * q:16 * q + 16, g * N_CMP:(g + 1) * N_CMP], src,
                                      POS[:, w, 16 * q:16 * q + 16].unsqueeze(2).to_broadcast([P, 16, N_CMP]), ALU.add)
            t = V(dve.drain())
            xcf = Y[:, 3072:4032]
            xch, xcl = xc_parts(w)
            act.wait_ge(s_dve.h, t)
            t = A(act.activation(xch, xcf, ACT.Copy))
            dve.wait_ge(s_act.h, t)
            V(dve.tensor_tensor(xcl, xcf, xch.bitcast(F32), ALU.subtract))
            dve.drain()

        s = gate_unit(0, {1: lambda: compress_in(0), 4: lambda: compress_in(1)})
        s.end()
        gate_cols[0] += 512
        pe.wait_ge(s_dve.h, s_dve.now())
        for w in range(2):
            s = Stage()
            xch, xcl = xc_parts(w)
            pe_done_of[w] = s.gemm(8, 0, 2 + w - 1, cols=256, m=NC2,
                                   lhs=lambda kt: (xch[:, kt * NC2:(kt + 1) * NC2], xcl[:, kt * NC2:(kt + 1) * NC2]))
            s.end()
            act.wait_ge(pe_done, pe_done_of[w])
            ev[1 + w].inc(act.activation(HC[0:NC2, :] if w == 0 else Y[0:NC2, 1792:2048], PS[0:NC2, 2 + 2 * w, 0:256],
                                         ACT.Gelu_apprx_tanh))

        def compress_T(w):
            pe.wait_ge(ev[1 + w].h, ev[1 + w].now())
            hc = HC if w == 0 else Y[:, 1792:2048]
            for k in range(2):
                mm = pe.transpose(PS[:, 7, k * 32:k * 32 + NC2], hc[0:NC2, k * P:(k + 1) * P], IDENT[0:NC2, 0:NC2])
            t = T(mm)
            dve.wait_ge(s_pe.h, t)
            V(dve.tensor_copy(HCT[:, :, 0:NC2], PS[:, 7, 0:64].rearrange("p (k c) -> p k c", k=2)[:, :, 0:NC2]))

        def compress_out(w):
            pe.wait_ge(s_dve.h, s_dve.now())
            if w == 0:
                for k in range(2):
                    mm = pe.matmul(PS[:, 6, 0:NC2], W2[:, 0, k, :], HCT[:, k, 0:NC2], start=k == 0, stop=k == 1)
                t = T(mm)
                dve.wait_ge(s_pe.h, t)
                V(dve.tensor_copy(KC[:, :, 0:N_CMP], PS[:, 6, 0:NC2].rearrange("p (g c) -> p g c", g=2)))
            else:
                for g in range(KVH):
                    for k in range(2):
                        mm = pe.matmul(PS[0:N_CMP, 6, g * P:(g + 1) * P], HCT[:, k, g * N_CMP:(g + 1) * N_CMP],
                                       W2[:, 1, k, :], start=k == 0, stop=k == 1)
                t = T(mm)
                dve.wait_ge(s_pe.h, t)
                V(dve.tensor_copy(VC[0:N_CMP, :, :], PS[0:N_CMP, 6, 0:256].rearrange("p (g c) -> p g c", g=2)))

        CQT = Y[:, 2048:4096].rearrange("p (i n) -> p i n", i=8)
        CL = Y[:, 1184:1184 + 240]
        CM = Y[:, 1424:1424 + 240]
        CPT = work("cpt", 9472, 512, 2)
        CR = SMALL[:, 304:320]
        cl4, cm4, cb4 = (v.rearrange("p (h i c) -> p h i c", h=2, i=8) for v in (CL, CM, SMALL[:, 64:304]))
        cl3, cm3 = (v.rearrange("p (i c) -> p i c", i=16) for v in (CL, CM))

        def cmp_bias():
            dve.memset(SMALL[:, 64:304], NEG)
            dve.drain()
            n0 = 7
            dve.tensor_copy(cb4[:, 0, :, 0:n0], BIAS[:, 0:HEADS, P + 31:P + 31 + 16 * (n0 - 1) + 1:16])
            dve.tensor_copy(cb4[:, 1, :, :], BIAS[:, 0:HEADS, 31:31 + 16 * (N_CMP - 1) + 1:16])
            dve.drain()
            dve.tensor_scalar(CM, SMALL[:, 64:304], NEG / 2, None, ALU.is_gt)
            V(dve.drain())

        def cmp_load(g):
            act.wait_ge(s_pe.h, s_pe.now())
            ld[1].inc(act.dma_start(AQ, cols_of(PROJ, 512 * g)), 16)

        def cmp_q(g):
            pe.wait_ge(ld[1].h, ld[1].now())
            pe.wait_ge(s_act.h, s_act.now())
            for i in range(4):
                for h in range(NH):
                    mm = pe.transpose(PS[:, 4 + i // 2, (i % 2) * S + h * P:(i % 2) * S + h * P + P],
                                      AQ[:, h, i * P:(i + 1) * P], IDENT[:, :])
            t = T(mm)
            act.wait_ge(s_pe.h, t)
            A(act.activation(CQT[:, 4 * g:4 * g + 4, :].rearrange("p i n -> p (i n)"),
                             PS[:, 4:6, :].rearrange("p a n -> p (a n)"), ACT.Copy))

        def cmp_logits():
            pe.wait_ge(s_act.h, s_act.now())
            pe.wait_ge(s_dve.h, s_dve.now())
            for h in range(NH):
                for i in range(HEADS):
                    o = (h * HEADS + i) * N_CMP
                    mm = pe.matmul(PS[:, 6, o:o + N_CMP], CQT[:, i, h * P:h * P + P], KC[:, i // GRP, 0:N_CMP],
                                   start=True, stop=True)
            t = T(mm)
            dve.wait_ge(s_pe.h, t)
            for h in range(NH):
                dve.scalar_tensor_tensor(out=cl4[:, h], in0=PS[:, 6, h * 120:h * 120 + 120].rearrange("p (i c) -> p i c", i=8),
                                         scalar=HD ** -0.5, in1=cb4[:, h], op0=ALU.mult, op1=ALU.add)
            dve.drain()
            dve.tensor_reduce(CR, cl3, AX.X, ALU.max)
            dve.drain()
            V(dve.tensor_tensor(cl3, cl3, CR.unsqueeze(2).to_broadcast([P, 16, N_CMP]), ALU.subtract))

        def cmp_softmax():
            act.wait_ge(s_dve.h, s_dve.now())
            t = A(act.activation(CL, CL, ACT.Exp))
            dve.wait_ge(s_act.h, t)
            dve.tensor_tensor(CL, CL, CM, ALU.mult)
            dve.drain()
            dve.tensor_reduce(CR, cl3, AX.X, ALU.add)
            dve.drain()
            dve.tensor_scalar(CR, CR, TINY, None, ALU.max)
            dve.drain()
            dve.reciprocal(CR, CR)
            dve.drain()
            gates = GATE[:, :, :].rearrange("p h (i b) -> p h i b", b=3)
            dve.tensor_tensor(CR.rearrange("p (h i) -> p h i", h=2), CR.rearrange("p (h i) -> p h i", h=2), gates[:, :, :, 0], ALU.mult)
            dve.drain()
            V(dve.tensor_tensor(cl3, cl3, CR.unsqueeze(2).to_broadcast([P, 16, N_CMP]), ALU.mult))

        def cmp_pT(i0):
            pe.wait_ge(s_dve.h, s_dve.now())
            pe.wait_ge(s_act.h, s_act.now())
            for i in range(2):
                for h in range(NH):
                    o = (h * HEADS + i0 + i) * N_CMP
                    mm = pe.transpose(PS[0:N_CMP, 6, (i * 2 + h) * P:(i * 2 + h + 1) * P], CL[:, o:o + N_CMP], IDENT[:, :])
            t = T(mm)
            act.wait_ge(s_pe.h, t)
            A(act.activation(CPT[0:N_CMP, :, :].rearrange("p i n -> p (i n)"), PS[0:N_CMP, 6, :], ACT.Copy))

        def cmp_pv(i0):
            pe.wait_ge(s_act.h, s_act.now())
            for i in range(2):
                for h in range(NH):
                    c = (i0 + i) % GRP
                    mm = pe.matmul(PS[:, 4 + h, c * P:c * P + P], CPT[0:N_CMP, i, h * P:h * P + P],
                                   VC[0:N_CMP, i0 // GRP, :], start=True, stop=True)
            t = T(mm)
            if i0 % GRP == 2:
                dve.wait_ge(s_pe.h, t)
                t = V(dve.tensor_copy(OA[:, :, :], PS[:, 4:6, :]))
                act.wait_ge(s_dve.h, t)
                ld[2].inc(act.dma_start(cols_of(BROUT, 512 * (i0 // GRP)), OA), 16)
                act.wait_ge(ld[2].h, ld[2].now())

        hk = {0: [lambda: compress_T(0), lambda: cmp_load(0)], 1: [lambda: compress_out(0), cmp_bias], 2: [lambda: compress_T(1)],
              3: [lambda: compress_out(1), lambda: cmp_q(0)], 4: [lambda: cmp_load(1)], 6: [lambda: cmp_q(1)], 7: [cmp_logits]}
        def both(hk):
            return {k: (lambda v=v: [f() for f in v]) for k, v in hk.items()}
        gate_unit(0, both(hk)).end()
        gate_cols[0] += 512
        hk = {0: [cmp_softmax], 2: [lambda: cmp_pT(0)], 3: [lambda: cmp_pv(0)], 4: [lambda: cmp_pT(2)], 5: [lambda: cmp_pv(2)],
              6: [lambda: cmp_pT(4)], 7: [lambda: cmp_pv(4)]}
        gate_unit(1, both(hk)).end()
        gate_cols[0] += 512
        hk = {0: [lambda: cmp_pT(6)], 1: [lambda: cmp_pv(6)]}
        gate_unit(0, both(hk)).end()
        gate_cols[0] += 512

        def attention(q0, k0, v0, head0, sink, gate, out0, accumulate, slot):
            per = {"ld1": 48, "s_pe": 4, "s_act": 4, "s_dve": 5, "ev0": 1, "st0": 16, "ld2": 16 * (accumulate + (slot is None))}
            if slot is not None:
                per.update(s_tp=2, s_hi=2, s_lo=2)
            with loop(KVH, per) as g:
                def loads():
                    act.wait_ge(s_pe.h, s_pe.now())
                    act.wait_ge(s_dve.h, s_dve.now())
                    if slot is not None:
                        act.wait_ge(s_tp.h, s_tp.now())
                    act.wait_ge(ld[2].h, ld[2].now())
                    ld[1].inc(act.dma_start(AQ, cols_of(PROJ, g * 512 + q0)), 16)
                    ld[1].inc(act.dma_start(AK, cols_of(PROJ, g * P + k0, P)), 16)
                    ld[1].inc(act.dma_start(AV, cols_of(PROJ, g * P + v0, P)), 16)

                def transposes():
                    pe.wait_ge(s_dve.h, s_dve.now())
                    pe.wait_ge(ld[1].h, ld[1].now())
                    if slot is not None:
                        pe.wait_ge(s_lo.h, s_lo.now())
                    for i in range(GRP):
                        for h in range(NH):
                            pe.transpose(PS[:, 4 + i // 2, (i % 2) * S + h * P:(i % 2) * S + h * P + P],
                                         AQ[:, h, i * P:(i + 1) * P], IDENT[:, :])
                    for h in range(NH):
                        mm = pe.transpose(PS[:, 6, h * P:h * P + P], AK[:, h, :], IDENT[:, :])
                    t = T(mm)
                    act.wait_ge(s_pe.h, t)
                    dve.wait_ge(s_pe.h, t)
                    A(act.activation(QT.rearrange("p i n -> p (i n)"), PS[:, 4:6, :].rearrange("p a n -> p (a n)"), ACT.Copy))
                    V(dve.tensor_copy(KT[:, 0:S], PS[:, 6, 0:S]))
                    if accumulate:
                        ld[2].inc(act.dma_start(OA, cols_of(BROUT, g * 512 + out0)), 16)

                def logits():
                    pe.wait_ge(s_act.h, s_act.now())
                    pe.wait_ge(s_dve.h, s_dve.now())
                    for i in range(GRP):
                        pe.matmul(PS[:, 4 + i, 0:P], QT[:, i, 0:P], KT[:, 0:P], start=True, stop=True)
                        mm = pe.matmul(PS[:, 4 + i, P:3 * P], QT[:, i, P:S], KT[:, 0:S], start=True, stop=True)
                    t = T(mm)
                    dve.wait_ge(s_pe.h, t)
                    hb = BIAS[:, bass.ds(g * GRP + head0, GRP), :]
                    dve.scalar_tensor_tensor(out=LG[:, :, P:3 * P], in0=PS[:, 4:8, P:3 * P], scalar=HD ** -0.5,
                                             in1=hb, op0=ALU.mult, op1=ALU.add)
                    dve.scalar_tensor_tensor(out=LG[:, :, 0:P], in0=PS[:, 4:8, 0:P], scalar=HD ** -0.5,
                                             in1=hb[:, :, P:S], op0=ALU.mult, op1=ALU.add)
                    dve.drain()
                    dve.tensor_reduce(MX[:, 4:8], LG[:, :, P:3 * P], AX.X, ALU.max)
                    dve.tensor_reduce(MX[:, 0:4], LG[:, :, 0:P], AX.X, ALU.max)
                    dve.drain()
                    if sink:
                        sk = SINK[:, bass.ds(g * GRP, GRP)].unsqueeze(1).to_broadcast([P, 2, 4])
                        mx2, es2 = (v.rearrange("p (h i) -> p h i", h=2) for v in (MX, ES))
                        dve.tensor_tensor(mx2, mx2, sk, ALU.max)
                        dve.drain()
                        dve.tensor_tensor(es2, sk, mx2, ALU.subtract)
                    V(dve.tensor_scalar(NM, MX, -1.0, None, ALU.mult))

                def exps(h):
                    act.wait_ge(s_dve.h, s_dve.now())
                    for i in range(GRP):
                        v = LG[:, i, 0:P] if h == 0 else LG[:, i, P:3 * P]
                        c = h * GRP + i
                        act.activation(v, v, ACT.Exp, bias=NM[:, c:c + 1], accum_out=RS[:, c:c + 1])
                    if h == 0:
                        return
                    if sink:
                        act.activation(ES, ES, ACT.Exp)
                    A(act.drain())

                def probs_T():
                    pe.wait_ge(s_act.h, s_act.now())
                    dve.wait_ge(s_act.h, s_act.now())
                    for i in range(GRP):
                        for j in range(3):
                            mm = pe.transpose(PS[:, 4 + i, j * P:(j + 1) * P], LG[:, i, j * P:(j + 1) * P], IDENT[:, :])
                    t = T(mm)
                    if sink:
                        dve.tensor_tensor(RS, RS, ES, ALU.add)
                        dve.drain()
                    dve.tensor_scalar(RS, RS, TINY, None, ALU.max)
                    dve.drain()
                    dve.reciprocal(RI, RS)
                    dve.drain()
                    ri2 = RI.rearrange("p (h i) -> p h i", h=2)
                    if gate:
                        dve.tensor_tensor(ri2, ri2, GATE[:, :, :].rearrange("p h (i b) -> p h i b", b=3)[:, :, bass.ds(g * GRP, GRP), gate], ALU.mult)
                        dve.drain()
                    act.wait_ge(s_pe.h, t)
                    dve.wait_ge(s_pe.h, t)
                    A(act.activation(PT[:, 0:2, :], PS[:, 4:6, 0:3 * P], ACT.Copy))
                    V(dve.tensor_copy(PT[:, 2:4, :], PS[:, 6:8, 0:3 * P]))

                def values():
                    pe.wait_ge(s_act.h, s_act.now())
                    pe.wait_ge(s_dve.h, s_dve.now())
                    for i in range(GRP):
                        c = slice(i * P, (i + 1) * P)
                        pe.matmul(PS[:, 4, c], PT[:, i, 0:P], AV[:, 0, :], start=True, stop=True)
                        pe.matmul(PS[:, 5, c], PT[:, i, P:2 * P], AV[:, 0, :], start=True, stop=False)
                        mm = pe.matmul(PS[:, 5, c], PT[:, i, 2 * P:3 * P], AV[:, 1, :], start=False, stop=True)
                    t = T(mm)
                    dve.wait_ge(s_pe.h, t)
                    if accumulate:
                        dve.wait_ge(ld[2].h, ld[2].now())
                    for h in range(NH):
                        dst = OA[:, h, :].rearrange("p (i n) -> p i n", i=GRP)
                        src = PS[:, 4 + h, :].rearrange("p (i n) -> p i n", i=GRP)
                        r = RI[:, h * GRP:h * GRP + GRP].unsqueeze(2).to_broadcast([P, GRP, P])
                        if accumulate:
                            lg = Y[:, h * 512:h * 512 + 512].rearrange("p (i n) -> p i n", i=GRP)
                            dve.tensor_tensor(lg, src, r, ALU.mult)
                            dve.drain()
                            dve.tensor_tensor(dst, dst, lg, ALU.add)
                        else:
                            dve.tensor_tensor(dst, src, r, ALU.mult)
                    V(dve.drain())

                def result():
                    if slot is None:
                        act.wait_ge(s_dve.h, s_dve.now())
                        ld[2].inc(act.dma_start(cols_of(BROUT, g * 512 + out0), OA), 16)
                        A(act.drain())
                        V(dve.drain())
                        return
                    pe.wait_ge(s_dve.h, s_dve.now())
                    bank_free[:] = [s_lo.now()] * 4
                    transpose_split(OA, 4, g * 4 + slot, banks=(6, 7))
                    V(dve.drain())
                    A(act.drain())

                loads()
                s = gate_unit(0, {1: transposes, 2: logits, 4: lambda: exps(0), 5: lambda: exps(1), 6: probs_T, 7: values}, it=g)
                result()
            s.end()
            gate_cols[0] += 1024
            bank_free[:] = [s_lo.now()] * 4

        attention(0, 1536, 1792, 0, False, 1, 0, True, None)
        attention(0, 2048, 2304, 0, False, 2, 0, True, 16)
        attention(2560, 3584, 3840, 8, True, 0, 1024, False, 24)
        attention(4096, 5120, 5376, 16, False, 0, 2048, False, None)
        for e in (act, dve):
            for x in (s_act, s_dve, s_pe):
                e.wait_ge(x.h, x.now())
        act.wait_ge(ld[2].h, ld[2].now())
        all_stored()
        OB = work("ob", 6144, 2048, 2)
        ld[1].inc(act.dma_start(OB, cols_of(BROUT, 2048, 1024)), 16)

        def third_branch():
            pe.wait_ge(ld[1].h, ld[1].now())
            pe.wait_ge(s_dve.h, s_dve.now())
            bank_free[:] = [s_lo.now()] * 4
            for e in (act, dve):
                e.wait_ge(pe_done, h_read)
            state["third"] = transpose_split(OB, 8, 0, banks=(6, 7))

        GS = work("gs", 0, 3072, 3)
        TM = work("tm", 3072, 3072, 3)
        state = {}
        h_read = at["b"] + HL_SLOTS
        for it in range(2):
            s = Stage()
            for cc in range(2):
                act.wait_ge(s_dve.h, s_dve.now())
                for m in range(3):
                    ld[2].inc(act.dma_start(GS[:, m, :].rearrange("p (h n) -> p h n", h=2),
                                            cols_of(SGATE, it * 1024 + (m * D + cc * 512))), 16)
                gl = ld[2].now()
                for m in range(3):
                    if it + cc == 0 and m == 2:
                        pe.wait_ge(s_lo.h, state["third"])
                    r = s.gemm(4, (16, 24, 0)[m], m, hooks={0: third_branch} if it + cc + m == 0 else {})
                    dve.wait_ge(pe_done, r)
                    dve.wait_ge(ld[2].h, gl)
                    y = Y3[:, :, it * 1024 + cc * 512:it * 1024 + cc * 512 + 512]
                    g3, t3 = (v[:, m, :].rearrange("p (h n) -> p h n", h=2) for v in (GS, TM))
                    if m == 0:
                        ev[m].inc(dve.tensor_tensor(y, pair_ap(m), g3, ALU.mult))
                        dve.drain()
                    else:
                        ev[m].inc(dve.tensor_tensor(t3, pair_ap(m), g3, ALU.mult))
                        dve.drain()
                        dve.tensor_tensor(y, y, t3, ALU.add)
                    V(dve.drain())
            s.end()

        def project_add(of_y=False):
            s = Stage()
            hooks, ready = {}, None
            if of_y:
                lead, hooks, ready = first_unit(None)
                lead()
            for c in range(4):
                if c == 2:
                    s.end()
                    s = Stage()
                pair = (1, 0, 1, 0)[c]
                add_to_x(pair, s.gemm(8, 0, pair, hooks=hooks if c == 0 else {}, ready=ready if c == 0 else None,
                                      hold=HOLD * (c == 3)),
                         slice(c * 512, (c + 1) * 512))
                column_sums(c)
            s.end()

        fence()
        project_add(True)

        def down(s, pairs=(1, 2, 1, 2), kt0=16, after=None):
            pe.wait_ge(s_lo.h, state["hidden"])
            for c in range(4):
                hold = HOLD if after and c == 3 else 0
                add_to_x(pairs[c], s.gemm(2, kt0, pairs[c], hold=hold), slice(c * 512, (c + 1) * 512))
                if after:
                    after(c)

        HB = work("hb", 0, 1024, 2)
        SG = work("sg", 1024, 1024)

        def relu_square(r):
            act.wait_ge(pe_done, r)
            act.wait_ge(s_tp.h, s_tp.now())
            t = ev[0].inc(act.activation(SG, pair_ap(0).rearrange("p h n -> p (h n)"), ACT.Relu))
            act.wait_ge(ev[0].h, t)
            return A(act.activation(HB[:, :, :].rearrange("p h n -> p (h n)"), SG, ACT.Square))

        def hidden_T(t):
            pe.wait_ge(s_act.h, t)
            bank_free[2] = bank_free[3] = s_lo.now()
            act.wait_ge(pe_done, down_done())
            state["hidden"] = transpose_split(HB, 4, 16, banks=(6, 7))

        def down_done():
            return state["down"]

        def norm_first(gain, src=None, then={}):
            fence()
            factors_of_x(src is not None)
            lead, hooks, ready = first_unit(gain, scaled=(X, R1ST) if src is None else (src, R2ND), then=then)
            lead()
            return dict(hooks=hooks, ready=ready)

        FG = work("fg", 8192, 2048)
        first = norm_first(GAIN[:, 1, :])
        ld[0].inc(act.dma_start(FG, a["norm_final"].partition_broadcast(P)), 16)
        s = Stage()
        relu_square(s.gemm(8, 0, 0, **first))
        s.end()
        with loop(15, {"ev0": 1, "ev1": 2, "ev2": 2, "s_act": 1, "s_tp": 2, "s_hi": 2, "s_lo": 2}) as it:
            s = Stage(it)
            state["down"] = it * s.per + (s.base + HL_SLOTS)
            before = s_act.now()
            r = s.gemm(8, 0, 0, hooks={2: lambda: hidden_T(before)})
            relu_square(r)
            down(s)
        s.end()
        state["down"] = at["b"] + HL_SLOTS
        hidden_T(s_act.now())
        dve.wait_ge(ld[0].h, ld[0].now())
        s = Stage()
        down(s, after=lambda c: column_sums(c, FG))
        s.end()

        MEM = work("mem", 2048, 4096, 2)
        def x_normed(q):
            c = slice(q * 256, (q + 1) * 256)
            for h in range(NH):
                ins = dve.scalar_tensor_tensor(out=X[:, h, c], in0=X[:, h, c], scalar=R1ST[:, h:h + 1], in1=FG[:, c],
                                               op0=ALU.mult, op1=ALU.mult)
            V(ins)

        def mem_load():
            act.wait_ge(s_dve.h, s_dve.now())
            ld[1].inc(act.dma_start(MEM, a["mem_2"][0].rearrange("(h p) n -> p h n", p=P)), 16)

        def mem_norm():
            for e in (act, dve):
                e.wait_ge(s_tp.h, s_tp.now())
            normalize(MEM, (ld[1].h, ld[1].now()))

        def mem_T(j):
            if j == 0:
                pe_after_both()
            transpose_split(Y3, 4 * j + 4, 16, GAIN[:, 4, :], j0=4 * j)

        mem_load()
        beside = {q: (lambda q=q: x_normed(q)) for q in range(7)}
        beside[7] = lambda: (x_normed(7), mem_norm())
        first = norm_first(GAIN[:, 2, :], Y3, beside)
        s = Stage()
        store(0, s.gemm(8, 0, 0, **first), 0, cols_of(PROJ2, 0))
        store(1, s.gemm(8, 0, 1, hooks={2 + j: (lambda j=j: mem_T(j)) for j in range(4)}), 1, cols_of(PROJ2, 512))
        s.end()
        PU = Y[:, 0:2048].rearrange("p (h n) -> p h n", h=2)
        PO = Y[:, 2048:4096].rearrange("p (c n) -> p c n", c=8)
        PW = work("pw", 2048, 2048).rearrange("p (g k n) -> p g k n", g=4, k=2)
        PP = work("pp", 4096, 2048, 8)
        MASK = work("mask", 6656, 1024, 8)
        BAND = work("band", 8192, 2048).rearrange("p (g h n) -> p g h n", g=4, h=2)
        PSC = SMALL[:, 0:8]
        HG = SMALL[:, 32:160]
        L2 = SMALL[:, 160:176]
        for x in (*st, s_tp, s_act, s_dve, s_lo):
            pool.wait_ge(x.h, x.now())
        for dst, src in ((PU, cols_of(PROJ2, 0, 1024)), (BAND, a["band"].rearrange("g (h p) n -> p g h n", p=P)),
                         (PW, a["pool_w_2"][0].rearrange("g (k p) n -> p g k n", p=P)), (PSC, a["pool_scale_2"]),
                         (MASK, a["levels"].rearrange("l p n -> p l n")), (L2, a["hgrn_lb_logits_2"]),
                         (HG, a["hgrn_norm_2"][0].partition_broadcast(P))):
            sw[0].inc(pool.dma_start(dst, src), 16)
        with loop(3, {"ev0": 1, "ev1": 1, "st0": 16, "st1": 16}) as it:
            s = Stage(it)
            for u in range(2):
                store(u, s.gemm(8, 0, u), u, cols_of(PROJ2, it * 1024 + (1024 + u * 512)))
        s.end()

        ONE = work("one", 7680, 256)
        LB, LB1 = SMALL[:, 16:24], SMALL[:, 24:32]

        def pool_mean(c):
            if c == 0:
                for e in (pe, act, dve):
                    e.wait_ge(sw[0].h, sw[0].now())
                dve.memset(ONE, 1.0)
                dve.drain()
                dve.memset(ONE.rearrange("p (c t) -> p c t", t=64)[:, :, 0:1], 0.0)
                V(dve.tensor_tensor(L2[:, 0:8], L2[:, 0:8], L2[:, 8:16], ALU.subtract))
            pe.wait_ge(s_act.h, s_act.now())
            for h in range(NH):
                mm = pe.matmul(PS[:, 4 + c % 2, 0:S], PU[:, h, c * P:(c + 1) * P], BAND[:, c // 2, h, :], start=h == 0, stop=h == 1)
            act.wait_ge(s_pe.h, T(mm))
            A(act.activation(PP[:, c, :], PS[:, 4 + c % 2, 0:S], ACT.Copy))

        def pool_mix(c):
            pe.wait_ge(s_act.h, s_act.now())
            for j in range(2):
                mm = pe.matmul(PS[:, 6 + c % 2, 0:S], PW[:, c // 2, j, (c % 2) * P:(c % 2 + 1) * P], PP[:, c // 2 * 2 + j, :],
                               start=j == 0, stop=j == 1)
            act.wait_ge(s_pe.h, T(mm))
            A(act.activation(PO[:, c, :], PS[:, 6 + c % 2, 0:S], ACT.Copy, scale=PSC[:, c:c + 1]))

        s = Stage()
        store(0, s.gemm(8, 0, 0, hooks={c: (lambda c=c: pool_mean(c)) for c in range(8)}), 0, cols_of(PROJ2, 4096))
        r = s.gemm(8, 0, 1, hooks={c: (lambda c=c: pool_mix(c)) for c in range(8)})
        store(1, r, 1, cols_of(PROJ2, 4608))
        s.end()
        act.wait_ge(s_dve.h, s_dve.now())
        A(act.activation(LB, L2[:, 0:8], ACT.Sigmoid))
        A(act.activation(LB1, L2[:, 0:8], ACT.Sigmoid, scale=-1.0))
        pooled = A(act.activation(XH[:, 0:8, :].rearrange("p a b -> p (a b)"), Y[:, 2048:4096], ACT.Copy))
        dve.wait_ge(s_act.h, pooled)
        dve.wait_ge(pe_done, r)
        V(dve.tensor_tensor(XL[:, 0:8, :].rearrange("p a b -> p (a b)"), Y[:, 2048:4096],
                            XH[:, 0:8, :].rearrange("p a b -> p (a b)").bitcast(F32), ALU.subtract))
        for e in (act, dve):
            e.wait_ge(s_pe.h, s_pe.now())
        act.wait_ge(s_dve.h, s_dve.now())
        all_stored()

        QF = Y[:, 0:1024].rearrange("p (h n) -> p h n", h=2)
        FF = Y[:, 1024:2048].rearrange("p (h n) -> p h n", h=2)
        AA = Y[:, 2048:3072]
        EE = [Y[:, 3072:4096], Y[:, 1024:2048]]
        VV = work("vv", 2048, 1024, 2)
        QQ = work("qq", 3072, 1024)
        KK = work("kk", 4096, 1024)
        SC = work("sc", 5120, 1536, 4)
        HO = work("ho", 7936, 1024, 2)
        HS, HV, HR = SMALL[:, 176:184], SMALL[:, 184:192], SMALL[:, 192:200]
        dve.memset(WORK[:, 5120:6656], 0.0)
        V(dve.drain())
        levels = [32, 16, 8, 4, 2, 1, 0, 64, 128]
        per = {"ld1": 48, "ld2": 16, "s_pe": 11, "s_act": 15, "s_dve": 30, "ev0": 2, "ev1": 2, "st0": 32, "st1": 32,
               "s_tp": 2, "s_hi": 2, "s_lo": 2}
        with loop(2, per) as g:
            q_ps, f_ps = (PS[:, b:b + 2, :].rearrange("p a n -> p (a n)") for b in (4, 6))

            def loads():
                act.wait_ge(s_pe.h, s_pe.now())
                act.wait_ge(s_dve.h, s_dve.now())
                ld[1].inc(act.dma_start(QF, cols_of(PROJ2, g * 512 + 1024)), 16)
                ld[1].inc(act.dma_start(FF, cols_of(PROJ2, g * 512 + 2048)), 16)
                ld[1].inc(act.dma_start(VV, cols_of(PROJ2, g * 512 + 3072)), 16)

            def transposes():
                pe.wait_ge(ld[1].h, ld[1].now())
                pe.wait_ge(s_dve.h, s_dve.now())
                pe.wait_ge(s_lo.h, s_lo.now())
                for src, bank in ((QF, 4), (FF, 6)):
                    for i in range(4):
                        for h in range(NH):
                            mm = pe.transpose(PS[:, bank + i // 2, (i % 2) * S + h * P:(i % 2) * S + h * P + P],
                                              src[:, h, i * P:(i + 1) * P], IDENT[:, :])
                act.wait_ge(s_pe.h, T(mm))
                ld[2].inc(act.dma_start(QF, cols_of(PROJ2, g * 512 + 4096)), 16)
                A(act.activation(EE[0], q_ps, ACT.Sigmoid))
                A(act.activation(KK, f_ps, ACT.Sigmoid, scale=-1.0))
                A(act.activation(AA, f_ps, ACT.Sigmoid))

            def forget():
                dve.wait_ge(s_act.h, s_act.now())
                V(dve.tensor_tensor(QQ, q_ps, EE[0], ALU.mult))
                for i in range(4):
                    c = slice(i * S, (i + 1) * S)
                    lb, lb1 = (v[:, bass.ds(g * 4 + i, 1)] for v in (LB, LB1))
                    dve.tensor_scalar(KK[:, c], KK[:, c], lb1, None, ALU.mult)
                    dve.tensor_scalar(AA[:, c], AA[:, c], lb1, lb, ALU.mult, ALU.add)
                dve.drain()
                V(dve.tensor_scalar(AA, AA, 1e-19, None, ALU.max))

            def log_sum():
                act.wait_ge(s_dve.h, s_dve.now())
                dve.wait_ge(s_act.h, A(act.activation(EE[0], AA, ACT.Ln)))
                for i in range(4):
                    c = slice(i * S, (i + 1) * S)
                    dve.tensor_tensor_scan(AA[:, c], ONE, EE[0][:, c], 0.0, ALU.mult, ALU.add)
                V(dve.drain())

            def blocks_of(H, *v):
                return [x.rearrange("p (b n) -> p b n", n=2 * H) for x in v]

            def exponents(n):
                H = levels[n]
                if not H:
                    return
                e = EE[n % 2]
                av, ev_ = blocks_of(H, AA, e)
                nb = 1024 // (2 * H)
                if H >= 64:
                    dve.tensor_tensor(av[:, :, H:2 * H], av[:, :, H:2 * H],
                                      av[:, :, H - 1:H].to_broadcast([P, nb, H]), ALU.add)
                    dve.drain()
                ref = av[:, :, H - 1:H].to_broadcast([P, nb, H])
                dve.wait_ge(s_pe.h, s_pe.now())
                dve.tensor_tensor(ev_[:, :, H:2 * H], av[:, :, H:2 * H], ref, ALU.subtract)
                act.wait_ge(s_dve.h, V(dve.tensor_tensor(ev_[:, :, 0:H], ref, av[:, :, 0:H], ALU.subtract)))
                A(act.activation(e, e, ACT.Exp))

            exp_done = {}

            def factors(n):
                H = levels[n]
                if not H:
                    return
                ev_, qv, kv = blocks_of(H, EE[n % 2], QQ, KK)
                dve.wait_ge(s_act.h, exp_done[n])
                dve.tensor_tensor(ev_[:, :, H:2 * H], ev_[:, :, H:2 * H], qv[:, :, H:2 * H], ALU.mult)
                exp_done[n, "f"] = V(dve.tensor_tensor(ev_[:, :, 0:H], ev_[:, :, 0:H], kv[:, :, 0:H], ALU.mult))

            def products(n):
                H = levels[n]
                lft, rgt = (EE[n % 2], EE[n % 2]) if H else (KK, QQ)
                if H:
                    pe.wait_ge(s_dve.h, exp_done[n, "f"])
                b = 4 if n % 2 == 0 else 6
                if n >= 2:
                    pe.wait_ge(s_dve.h, exp_done[n - 2, "m"])
                if H == 128:
                    for i in range(4):
                        mm = pe.matmul(PS[:, b, i * P:(i + 1) * P], lft[:, i * S:i * S + P], rgt[:, i * S + P:(i + 1) * S],
                                       start=True, stop=True)
                else:
                    for i in range(4):
                        for h in range(NH):
                            c = slice(i * S + h * P, i * S + h * P + P)
                            mm = pe.matmul(PS[:, b + h, i * P:(i + 1) * P], lft[:, c], rgt[:, c], start=True, stop=True)
                exp_done[n, "p"] = T(mm)

            def masked(n):
                H = levels[n]
                b = 4 if n % 2 == 0 else 6
                dve.wait_ge(s_pe.h, exp_done[n, "p"])
                if H == 128:
                    exp_done[n, "m"] = V(dve.tensor_copy(SC[:, :, P:2 * P], PS[:, b, :].rearrange("p (i n) -> p i n", i=4)))
                    return
                mk = MASK[:, {64: 0, 32: 1, 16: 2, 8: 3, 4: 4, 2: 5, 1: 6, 0: 7}[H], :].bitcast(U32).unsqueeze(1).to_broadcast([P, 4, P])
                dve.memset(SMALL[:, 500:501], 0.0)
                for h in range(NH):
                    ins = dve.copy_predicated(SC[:, :, 2 * h * P:(2 * h + 1) * P], mk,
                                              PS[:, b + h, :].rearrange("p (i n) -> p i n", i=4))
                exp_done[n, "m"] = V(ins)

            def out_products():
                pe.wait_ge(s_dve.h, s_dve.now())
                for i in range(4):
                    c = slice(i * P, (i + 1) * P)
                    pe.matmul(PS[:, 4, c], SC[:, i, 0:P], VV[:, 0, c], start=True, stop=True)
                    pe.matmul(PS[:, 5, c], SC[:, i, P:2 * P], VV[:, 0, c], start=True, stop=False)
                    mm = pe.matmul(PS[:, 5, c], SC[:, i, 2 * P:3 * P], VV[:, 1, c], start=False, stop=True)
                T(mm)

            qff = QF.rearrange("p h n -> p (h n)")

            def out_squares():
                act.wait_ge(s_pe.h, s_pe.now())
                A(act.activation(EE[1], PS[:, 4:6, :].rearrange("p a n -> p (a n)"), ACT.Square))
                act.wait_ge(ld[2].h, ld[2].now())
                A(act.activation(EE[0], qff, ACT.Sigmoid))

            def out_norm():
                dve.wait_ge(s_act.h, s_act.now())
                dve.wait_ge(ld[2].h, ld[2].now())
                dve.tensor_reduce(HS, EE[1].rearrange("p (i n) -> p i n", i=8), AX.X, ALU.add)
                dve.tensor_tensor(EE[0], EE[0], qff, ALU.mult)
                dve.drain()
                rstd(HS, HR, HV, P, 8)

            def out_gate():
                e8 = EE[0].rearrange("p (i n) -> p i n", i=8)
                dve.tensor_tensor(e8, e8, HR.unsqueeze(2).to_broadcast([P, 8, P]), ALU.mult)
                dve.drain()
                dve.tensor_tensor(e8, e8, HG.unsqueeze(1).to_broadcast([P, 8, P]), ALU.mult)
                dve.drain()
                dve.tensor_tensor(HO[:, :, :], PS[:, 4:6, :], EE[0].rearrange("p (h n) -> p h n", h=2), ALU.mult)
                V(dve.drain())

            def out_T():
                pe.wait_ge(s_dve.h, s_dve.now())
                bank_free[:] = [s_lo.now()] * 4
                transpose_split(HO, 4, g * 4 + 8, banks=(6, 7))

            def exps_of(n):
                exponents(n)
                exp_done[n] = s_act.now()

            steps = {0: [loads], 2: [transposes], 3: [forget], 4: [log_sum], 6: [lambda: exps_of(0)]}
            for n in range(len(levels)):
                k = 7 + 2 * n
                steps[k] = [lambda n=n: masked(n - 1)] if n else []
                if n + 1 < len(levels):
                    steps[k].append(lambda n=n: exps_of(n + 1))
                steps[k].append(lambda n=n: factors(n))
                steps[k + 1] = [lambda n=n: products(n)]
            last = 8 + 2 * len(levels)
            steps[last - 1] = [lambda: masked(len(levels) - 1)]
            steps[last] = [out_products]
            steps[last + 1] = [out_squares]
            steps[last + 2] = [out_norm]
            steps[last + 3] = [out_gate]
            steps[last + 5] = [out_T]
            s = Stage(g)
            for u in range(4):
                hooks = {k - 8 * u: (lambda v=v: [f() for f in v]) for k, v in steps.items() if 8 * u <= k < 8 * u + 8}
                store(u % 2, s.gemm(8, 16, u % 2, hooks=hooks), u % 2, cols_of(XKV, g * D + u * 512))
        s.end()
        fence()
        bank_free[:] = [s_lo.now()] * 4
        project_add()

        all_stored()
        MQ = work("mq", 2048, 1024, 2)
        MK = work("mk", 3072, 1024, 2)
        MV = work("mv", 4096, 1024, 2)
        MQT = work("mqt", 5120, 1024, 4)
        MKT = work("mkt", 6144, 1024, 4)
        MP = work("mp", 7168, 512, 2)
        MPT = work("mpt", 7680, 512, 2)
        MO = work("mo", 8192, 1024, 2)
        M1, M2, M3 = SMALL[:, 0:2], SMALL[:, 2:4], SMALL[:, 4:6]
        XD = float(W512) ** -0.5

        small_load([a["router_group_2"][0], a["router_expert_2"][0]], 20)

        def cross(g):
            def loads():
                act.wait_ge(s_pe.h, s_pe.now())
                for i in range(2):
                    act.wait_ge(st[i].h, st[i].now())
                for dst, src, c in ((MQ, XQ, 0), (MK, XKV, 0), (MV, XKV, D)):
                    ld[1].inc(act.dma_start(dst, cols_of(src, g * 512 + c)), 16)

            def transposes():
                pe.wait_ge(ld[1].h, ld[1].now())
                pe.wait_ge(s_dve.h, s_dve.now())
                pe.wait_ge(s_lo.h, s_lo.now())
                for src, bank in ((MQ, 4), (MK, 6)):
                    for i in range(4):
                        for h in range(NH):
                            pe.transpose(PS[:, bank + i // 2, (i % 2) * S + h * P:(i % 2) * S + h * P + P],
                                         src[:, h, i * P:(i + 1) * P], IDENT[:, :])
                t = T(pe.drain())
                act.wait_ge(s_pe.h, t)
                dve.wait_ge(s_pe.h, t)
                A(act.activation(MQT.rearrange("p i n -> p (i n)"), PS[:, 4:6, :].rearrange("p a n -> p (a n)"), ACT.Copy))
                V(dve.tensor_copy(MKT.rearrange("p i n -> p (i n)"), PS[:, 6:8, :].rearrange("p a n -> p (a n)")))

            def scores():
                pe_after_both()
                for h in range(NH):
                    for k in range(4):
                        mm = pe.matmul(PS[:, 4 + h, 0:S], MQT[:, k, h * P:(h + 1) * P], MKT[:, k, :], start=k == 0, stop=k == 3)
                dve.wait_ge(s_pe.h, T(mm))
                dve.tensor_reduce(M1, PS[:, 4:6, 0:S], AX.X, ALU.max)
                dve.drain()
                V(dve.tensor_scalar(M1, M1, -XD, None, ALU.mult))

            def softmax():
                act.wait_ge(s_dve.h, s_dve.now())
                for h in range(NH):
                    act.activation(MP[:, h, :], PS[:, 4 + h, 0:S], ACT.Exp, scale=XD, bias=M1[:, h:h + 1], accum_out=M2[:, h:h + 1])
                A(act.drain())

            def probs_T():
                pe.wait_ge(s_act.h, s_act.now())
                dve.wait_ge(s_act.h, s_act.now())
                dve.reciprocal(M3, M2)
                V(dve.drain())
                for k in range(2):
                    for h in range(NH):
                        mm = pe.transpose(PS[:, 6, k * S + h * P:k * S + h * P + P], MP[:, h, k * P:(k + 1) * P], IDENT[:, :])
                act.wait_ge(s_pe.h, T(mm))
                A(act.activation(MPT.rearrange("p k n -> p (k n)"), PS[:, 6, :], ACT.Copy))

            def values():
                pe.wait_ge(s_act.h, s_act.now())
                for h in range(NH):
                    for k in range(2):
                        mm = pe.matmul(PS[:, 4 + h, :], MPT[:, k, h * P:(h + 1) * P], MV[:, k, :], start=k == 0, stop=k == 1)
                dve.wait_ge(s_pe.h, T(mm))
                for h in range(NH):
                    dve.tensor_scalar(MO[:, h, :], PS[:, 4 + h, :], M3[:, h:h + 1], None, ALU.mult)
                V(dve.drain())

            def result():
                pe.wait_ge(s_dve.h, s_dve.now())
                bank_free[:] = [s_lo.now()] * 4
                state["hidden"] = transpose_split(MO, 4, 16, banks=(6, 7))
                V(dve.drain())

            return loads, {1: transposes, 2: scores, 3: softmax, 4: probs_T, 5: values}, result

        def add_head(s, hooks={}, after=None):
            pe.wait_ge(s_lo.h, state["hidden"])
            for c in range(4):
                hk = {k - 2 * c: f for k, f in hooks.items() if 2 * c <= k < 2 * c + 2}
                hold = HOLD if after and c == 3 else 0
                add_to_x(c % 2, s.gemm(2, 16, c % 2, hooks=hk, hold=hold), slice(c * 512, (c + 1) * 512))
                if after:
                    after(c)

        first = norm_first(GAIN[:, 3, :])
        for u in range(4):
            extra = dict(first) if u == 0 else {}
            result = None
            if u == 3:
                loads, hooks, result = cross(0)
                extra = dict(hooks={0: loads, **{k + 1: f for k, f in hooks.items()}})
            s = Stage()
            store(u % 2, s.gemm(8, 0, u % 2, **extra), u % 2, cols_of(XQ, u * 512))
            s.end()
        result()
        with loop(3, {"ld1": 48, "s_pe": 4, "s_act": 3, "s_dve": 5, "ev0": 2, "ev1": 2, "s_tp": 2, "s_hi": 2, "s_lo": 2}) as it:
            s = Stage(it)
            state["hidden"] = s_lo.now()
            loads, hooks, result = cross(it + 1)
            loads()
            add_head(s, hooks)
            act.wait_ge(pe_done, s.it * s.per + (s.base + s.k + HL_SLOTS))
            result()
        s.end()
        state["hidden"] = s_lo.now()
        router = small_split(20)
        s = Stage()
        add_head(s, after=column_sums)
        s.end()
        bank_free[:] = [s_lo.now()] * 4

        fence()
        work_memory.close()
        WORK = sb("WORK_MOE", [P, 5120])
        ROUNDED = sb("ROUNDED", [P, 3840], F32R)
        HB, SG, FG = work("hb", 0, 1024, 2), work("sg", 1024, 1024), work("fg", 2048, 2048)
        TRI, ONES, IOTA = work("tri", 4096, P), work("ones", 4224, P), work("iota", 4352, P)
        RANK = SMALL[:, 40:44]
        l = ld[0].inc(act.dma_start(RANK, a["rank"][0].partition_broadcast(P)), 16)
        ld[3].inc(act.dma_start(FG, a["norm_ffn_row"][0].partition_broadcast(P)), 16)
        ld[5].inc(act.dma_start(TRI, a["tri"]), 16)
        ld[5].inc(act.dma_start(IOTA, a["iota"][0].partition_broadcast(P)), 16)
        factors_of_x()
        lead, hooks, ready = first_unit(GAIN[:, 5, :], 16, scaled=(X, R1ST))
        lead()
        for j in range(4):
            hooks[j]()
        pe.wait_ge(s_lo.h, ready[7])
        HTOK = [v[:, 0:DK, :].rearrange("p a b -> p (a b)").rearrange("p (h n) -> p h n", h=2) for v in (XH, XL)]
        pool.wait_ge(s_tp.h, s_tp.now())
        pool.wait_ge(ld[3].h, ld[3].now())
        pool.wait_ge(s_dve.h, s_dve.now())
        pool.wait_ge(s_act.h, s_act.now())
        for q in range(4):
            y = Y3[:, :, q * 512:(q + 1) * 512]
            s_pool.inc(pool.tensor_tensor(y, y, FG[:, q * 512:(q + 1) * 512].unsqueeze(1).to_broadcast([P, 2, 512]), ALU.mult))
        t = small_gemm(20, router, 16)
        COMB = GATE[:, :, 0:16]
        act.wait_ge(s_pe.h, t)
        LGT = SMALL[:, 0:40].rearrange("p (h n) -> p h n", h=2)
        t = A(act.activation(SMALL[:, 0:40], PS[:, 7, 0:40], ACT.Copy))
        for q in range(4):
            act.wait_ge(s_pool.h, s_pool.now() - 3 + q)
            A(act.activation(HTOK[0][:, :, q * 512:(q + 1) * 512], Y3[:, :, q * 512:(q + 1) * 512], ACT.Copy))
        htok_hi = s_act.now()
        dve.wait_ge(s_act.h, t)
        dve.wait_ge(ld[0].h, l)
        rank2 = RANK.unsqueeze(1).to_broadcast([P, 2, 4])
        R1 = SMALL[:, 48:50]
        E4, OHG, SEL, O1, O2, WG = (SMALL[:, 56 + 8 * i:64 + 8 * i].rearrange("p (h n) -> p h n", h=2) for i in range(6))
        T1, T2, PG, WB, TG = (SMALL[:, 112 + 2 * i:114 + 2 * i] for i in range(5))
        CHOSEN = SMALL[:, 128:160].rearrange("p (h n) -> p h n", h=2)
        dve.memset(ONES, 1.0)

        def b4(v):
            return v.unsqueeze(2).to_broadcast([P, 2, 4])

        def first_max(x, top, onehot):
            dve.tensor_reduce(top, x, AX.X, ALU.max)
            dve.drain()
            dve.tensor_tensor(onehot, x, b4(top), ALU.is_equal)
            dve.drain()
            dve.tensor_tensor(onehot, onehot, rank2, ALU.mult)
            dve.drain()
            dve.tensor_reduce(R1, onehot, AX.X, ALU.max)
            dve.drain()
            dve.tensor_tensor(onehot, onehot, b4(R1), ALU.is_equal)
            dve.drain()

        grp = LGT[:, :, 0:4]
        first_max(grp, TG, OHG)
        for j in range(4):
            o = OHG[:, :, j:j + 1].to_broadcast([P, 2, 4])
            x = LGT[:, :, 4 + 4 * j:8 + 4 * j]
            dve.tensor_tensor(E4 if j else SEL, x, o, ALU.mult)
            dve.drain()
            if j:
                dve.tensor_tensor(SEL, SEL, E4, ALU.add)
                dve.drain()
        first_max(SEL, T1, O1)
        dve.scalar_tensor_tensor(out=E4, in0=O1, scalar=-3e38, in1=SEL, op0=ALU.mult, op1=ALU.add)
        dve.drain()
        first_max(E4, T2, O2)
        dve.tensor_tensor(E4, O1, O2, ALU.add)
        dve.drain()
        for j in range(4):
            o = OHG[:, :, j:j + 1].to_broadcast([P, 2, 4])
            dve.tensor_tensor(CHOSEN[:, :, 4 * j:4 * j + 4], E4, o, ALU.mult)

        def weights():
            dve.drain()
            dve.tensor_tensor(E4, grp, b4(TG), ALU.subtract)
            t = V(dve.tensor_tensor(WB, T2, T1, ALU.subtract))
            act.wait_ge(s_dve.h, t)
            A(act.activation(E4, E4, ACT.Exp))
            t = A(act.activation(WB, WB, ACT.Exp))
            dve.wait_ge(s_act.h, t)
            dve.tensor_reduce(PG, E4, AX.X, ALU.add)
            dve.tensor_scalar(T1, WB, 1.0, None, ALU.add)
            dve.drain()
            dve.reciprocal(PG, PG)
            dve.reciprocal(T1, T1)
            dve.drain()
            dve.tensor_tensor(T2, WB, T1, ALU.mult)
            dve.drain()
            dve.tensor_tensor(O1, O1, b4(T1), ALU.mult)
            dve.tensor_tensor(O2, O2, b4(T2), ALU.mult)
            dve.drain()
            dve.tensor_tensor(O1, O1, O2, ALU.add)
            dve.drain()
            dve.tensor_tensor(O1, O1, b4(PG), ALU.mult)
            dve.drain()
            for j in range(4):
                o = OHG[:, :, j:j + 1].to_broadcast([P, 2, 4])
                dve.tensor_tensor(COMB[:, :, 4 * j:4 * j + 4], O1, o, ALU.mult)
            V(dve.drain())

        SLOT = SMALL[:, 160:192].rearrange("p (h n) -> p h n", h=2)
        for e in (pe, dve):
            e.wait_ge(ld[5].h, ld[5].now())
        pe.wait_ge(s_dve.h, V(dve.drain()))
        pe.matmul(PS[:, 6, 0:16], TRI, CHOSEN[:, 0, :], start=True, stop=True)
        pe.matmul(PS[:, 6, 16:32], TRI, CHOSEN[:, 1, :], start=True, stop=False)
        pe.matmul(PS[:, 6, 16:32], ONES, CHOSEN[:, 0, :], start=False, stop=True)
        pe.matmul(PS[:, 6, 32:48], ONES, CHOSEN[:, 0, :], start=True, stop=False)
        t = T(pe.matmul(PS[:, 6, 32:48], ONES, CHOSEN[:, 1, :], start=False, stop=True))
        dve.wait_ge(s_pe.h, t)
        dve.tensor_tensor(SLOT, PS[:, 6, 0:32].rearrange("p (h n) -> p h n", h=2), CHOSEN, ALU.mult)
        dve.tensor_reduce(R1[:, 0:1], PS[:, 6, 32:48], AX.X, ALU.max)
        dve.drain()
        dve.tensor_scalar(SLOT, SLOT, -1.0, None, ALU.add)
        dve.tensor_scalar(FULL[:, :], R1[:, 0:1], P + 0.5, None, ALU.is_gt)
        fence()
        for e in (pool, sp):
            e.wait_ge(s_dve.h, s_dve.now())
        act.wait_ge(s_pool.h, s_pool.now())
        ld[3].inc(act.dma_start(FG, a["norm_final_2"].partition_broadcast(P)), 16)
        full = nc.values_load(FULL[0:1, 0:1], min_val=0, max_val=1)
        at_branch = {c.name: c.n for c in counts}, dict(at), list(bank_free)

        def end_branch():
            fence()
            for i in range(2):
                act.wait_ge(st[i].h, st[i].now())
            for c in counts:
                if c not in sw:
                    more = at_branch[0][c.name] + BRANCH - c.n
                    assert more > 0, c.name
                    dve.sem_inc(c.h, more)
                    c.n += more

        G1 = work("g1", 4480, 256, 2)
        GT = ROUNDED[:, 0:256]
        G2 = ROUNDED[:, 256:768].rearrange("p (h n) -> p h n", h=2)
        HTH, HTL = ROUNDED[:, 768:1280], ROUNDED[:, 1280:1792]
        YH, YL = (ROUNDED[:, c:c + 1024].rearrange("p (b n) -> p b n", b=2) for c in (1792, 2816))
        def token_lo(r):
            c = slice(r * 256, (r + 1) * 256)
            V(dve.tensor_tensor(HTOK[1][:, :, c], Y3[:, :, c], HTOK[0][:, :, c].bitcast(F32), ALU.subtract))

        def choose(e0):
            dve.wait_ge(s_tp.h, s_tp.now())
            for j in range(2):
                for h in range(NH):
                    ins = dve.tensor_scalar(G2[:, h, j * P:(j + 1) * P], IOTA, SLOT[:, h, bass.ds(e0 + j, 1)], None, ALU.is_equal)
            state["chosen"] = V(ins)

        def gather(r, chosen, free=None, bank=6, bank_read=None):
            pe.wait_ge(s_hi.h, s_hi.now() if bank_read is None else bank_read)
            pe.wait_ge(s_lo.h, s_lo.now())
            pe.wait_ge(s_dve.h, chosen)
            for k in range(2):
                c = slice((2 * r + k) * P, (2 * r + k + 1) * P)
                for part in range(2):
                    for h in range(NH):
                        mm = pe.matmul(PS[:, bank + part, k * 256:(k + 1) * 256], HTOK[part][:, h, c], G2[:, h, :],
                                       start=h == 0, stop=h == 1)
            act.wait_ge(s_tp.h, s_tp.inc(mm))
            if free is not None:
                act.wait_ge(pe_done, free)
            for part, dst in enumerate((XH, XL)):
                s_hi.inc(act.activation(dst[:, 16 + 2 * r:18 + 2 * r, :].rearrange("p a b -> p (a b)"), PS[:, bank + part, :], ACT.Copy))

        def slots_of(j):
            return lambda kt: tuple(v[:, 16 + kt, j * P:(j + 1) * P] for v in (XH, XL))

        def hidden_of(kt):
            return tuple(v[:, kt * P:(kt + 1) * P] for v in (HTH, HTL))

        def gate_up(s, j, hooks={}, gate_hooks={}):
            r0 = s.gemm(8, 0, 0, lhs=slots_of(j), bank=0, hooks=gate_hooks)
            act.wait_ge(pe_done, r0)
            act.wait_ge(s_dve.h, s_dve.now())
            t_gate = A(act.activation(SG[:, 0:512], PS[:, 0, :], ACT.Sigmoid))
            r1 = s.gemm(8, 0, 1, lhs=slots_of(j), bank=1, hooks=hooks)
            dve.wait_ge(s_act.h, t_gate)
            ev[0].inc(dve.tensor_tensor(SG[:, 0:512], SG[:, 0:512], PS[:, 0, :], ALU.mult))
            dve.drain()
            dve.wait_ge(pe_done, r1)
            dve.wait_ge(s_tp.h, s_tp.now())
            ev[1].inc(dve.tensor_tensor(HB[:, 0, :], SG[:, 0:512], PS[:, 1, :], ALU.mult))
            V(dve.drain())
            return r1

        def rows_of(e):
            dve.wait_ge(s_tp.h, s_tp.now())
            for h in range(NH):
                ins = dve.tensor_scalar(G1[:, h, :], IOTA, SLOT[:, h, bass.ds(e, 1)], None, ALU.is_equal)
            state["rows"] = V(ins)

        def rows_T():
            pe.wait_ge(s_hi.h, s_hi.now())
            pe.wait_ge(s_lo.h, s_lo.now())
            pe.wait_ge(s_dve.h, state["rows"])
            for h in range(NH):
                mm = pe.transpose(PS[:, 7, h * P:(h + 1) * P], G1[:, h, :], IDENT[:, :])
            act.wait_ge(s_tp.h, s_tp.inc(mm))
            s_hi.inc(act.activation(GT, PS[:, 7, 0:256], ACT.Copy))

        def slots_T():
            pe.wait_ge(s_lo.h, s_lo.now())
            pe.wait_ge(s_dve.h, state["hidden"])
            for k in range(4):
                mm = pe.transpose(PS[:, 6, k * P:(k + 1) * P], HB[:, 0, k * P:(k + 1) * P], IDENT[:, :])
            act.wait_ge(s_tp.h, s_tp.inc(mm))
            dve.wait_ge(s_hi.h, s_hi.inc(act.activation(HTH, PS[:, 6, :], ACT.Copy)))
            s_lo.inc(dve.tensor_tensor(HTL, PS[:, 6, :], HTH.bitcast(F32), ALU.subtract))

        def scatter(e, c, after=None):
            pe.wait_ge(ev[2 + c % 2].h, state["y", c])
            pe.wait_ge(s_dve.h, state["added"])
            for h in range(NH):
                for part, y in enumerate((YH, YL)):
                    mm = pe.matmul(PS[:, 4 + h, :], GT[:, h * P:(h + 1) * P], y[:, c % 2, :], start=part == 0, stop=part == 1)
            dve.wait_ge(s_pe.h, T(mm))
            for h in range(NH):
                x = X[:, h, c * 512:(c + 1) * 512]
                ins = dve.scalar_tensor_tensor(out=x, in0=PS[:, 4 + h, :], scalar=COMB[:, h, bass.ds(e, 1)], in1=x,
                                               op0=ALU.mult, op1=ALU.add)
            state["added"] = V(ins)
            if after:
                after(c)

        def down_slots(s, e, extra={}, after=None):
            pe.wait_ge(s_hi.h, s_hi.now())
            pe.wait_ge(s_lo.h, s_lo.now())
            state["added"] = s_dve.now()
            for c in range(4):
                def last(c=c):
                    if c:
                        scatter(e, c - 1, after)
                    extra.get(2 * c + 1, nothing)()
                r = s.gemm(2, 0, 2 + c % 2, lhs=hidden_of, bank=2 + c % 2, hooks={0: extra.get(2 * c, nothing), 1: last})
                act.wait_ge(pe_done, r)
                act.wait_ge(s_pe.h, s_pe.now())
                t = A(act.activation(YH[:, c % 2, :], PS[:, 2 + c % 2, :], ACT.Copy))
                dve.wait_ge(s_act.h, t)
                state["y", c] = ev[2 + c % 2].inc(dve.tensor_tensor(
                    YL[:, c % 2, :], PS[:, 2 + c % 2, :], YH[:, c % 2, :].bitcast(F32), ALU.subtract))
            extra.get(8, nothing)()

        def nothing():
            pass

        def pair_step(s, e, first, single=False):
            left = s_dve.now()
            y_left = ev[3].now()

            def leftover():
                if not first:
                    state["y", 3], state["added"] = y_left, left
                    scatter(e - 2, 3)

            state["hidden"] = left
            hk = {0: slots_T, 2: lambda: rows_of(e - 1), 4: rows_T}
            if not single:
                hk[5] = lambda: choose(e + 1)
            r = gate_up(s, 1, hk, {2: leftover})
            if single:
                down_slots(s, e - 1)
                scatter(e - 1, 3)
                return
            chosen = state["chosen"]
            down_slots(s, e - 1, {k: (lambda k=k: gather(k, chosen, r)) for k in range(8)})
            pe.wait_ge(s_hi.h, s_hi.now())
            state["hidden"] = s_dve.now()
            gate_up(s, 0, {0: slots_T, 2: lambda: rows_of(e), 4: rows_T}, {1: lambda: scatter(e - 1, 3)})
            down_slots(s, e)

        with nc.If(full == 0):
            choose(0)
            dve.wait_ge(s_act.h, htok_hi)
            read = [s_hi.now()] * 2
            for r in range(8):
                token_lo(r)
                gather(r, s_dve.now(), bank=4 + 2 * (r % 2), bank_read=read[r % 2])
                read[r % 2] = s_hi.now()
            weights()
            pe.wait_ge(s_hi.h, s_hi.now())
            s = Stage()
            gate_up(s, 0)
            s.end()
            s = Stage()
            pair_step(s, 1, True)
            s.end()
            per = {"ev0": 2, "ev1": 2, "ev2": 4, "ev3": 4, "s_act": 10, "s_dve": 13, "s_pe": 8, "s_tp": 12, "s_hi": 20, "s_lo": 2}
            with loop(6, per) as it:
                s = Stage(it)
                pair_step(s, it * 2 + 3, False)
            s.end()
            s = Stage()
            pair_step(s, N_EXP - 1, False, single=True)
            s.end()
            s = Stage()
            state["hidden"] = s_dve.now()
            slots_T()
            rows_of(N_EXP - 1)
            rows_T()
            down_slots(s, N_EXP - 1, after=column_sums)
            scatter(N_EXP - 1, 3, column_sums)
            s.end()
            end_branch()
            after = dict(at)

        def expert_hidden(e, r):
            act.wait_ge(pe_done, r[0])
            act.wait_ge(s_dve.h, s_dve.now())
            t = A(act.activation(SG, pair_ap(0).rearrange("p h n -> p (h n)"), ACT.Sigmoid))
            dve.wait_ge(s_act.h, t)
            sg3 = SG.rearrange("p (h n) -> p h n", h=2)
            ev[0].inc(dve.tensor_tensor(sg3, sg3, pair_ap(0), ALU.mult))
            dve.drain()
            dve.wait_ge(pe_done, r[1])
            dve.wait_ge(s_tp.h, s_tp.now())
            for h in range(NH):
                ins = dve.scalar_tensor_tensor(out=HB[:, h, :], in0=pair_ap(1)[:, h, :], scalar=COMB[:, h, bass.ds(e, 1)],
                                               in1=sg3[:, h, :], op0=ALU.mult, op1=ALU.mult)
            ev[1].inc(ins)
            return V(dve.drain())

        def expert_T(t):
            pe.wait_ge(s_dve.h, t)
            bank_free[2] = bank_free[3] = s_lo.now()
            act.wait_ge(pe_done, down_done())
            state["hidden"] = transpose_split(HB, 4, 0, banks=(6, 7))

        def dense_step(s, e, it=0):
            state["down"] = it * s.per + (s.base + s.k + HL_SLOTS)
            before = s_dve.now()
            r0 = s.gemm(8, 16, 0)
            r1 = s.gemm(8, 16, 1, hooks={0: lambda: expert_T(before)})
            expert_hidden(e, (r0, r1))
            down(s, (2, 0, 1, 2), 0)

        with nc.Else():
            for c in counts:
                c.n = at_branch[0][c.name]
            at.update(at_branch[1])
            bank_free[:] = at_branch[2]
            weights()
            s = Stage()
            r = (s.gemm(8, 16, 0), s.gemm(8, 16, 1))
            expert_hidden(0, r)
            s.end()
            s = Stage()
            dense_step(s, 1)
            dense_step(s, 2)
            s.end()
            with loop(6, {"ev0": 4, "ev1": 4, "ev2": 4, "s_act": 2, "s_dve": 2, "s_tp": 4, "s_hi": 4, "s_lo": 4}) as it:
                s = Stage(it)
                dense_step(s, it * 2 + 3, it)
                dense_step(s, it * 2 + 4, it)
            s.end()
            s = Stage()
            dense_step(s, N_EXP - 1)
            s.end()
            state["down"] = at["b"] + HL_SLOTS
            expert_T(s_dve.now())
            s = Stage()
            down(s, (2, 0, 1, 2), 0, column_sums)
            s.end()
            end_branch()
        assert at == after
        assert at["b"] == total and at["stage"] == len(plan)

        fence()
        factors_of_x()
        dve.wait_ge(ld[3].h, ld[3].now())
        for q in range(4):
            c = slice(q * 512, (q + 1) * 512)
            for h in range(NH):
                ins = dve.scalar_tensor_tensor(out=X[:, h, c], in0=X[:, h, c], scalar=R1ST[:, h:h + 1], in1=FG[:, c],
                                               op0=ALU.mult, op1=ALU.mult)
            act.wait_ge(s_dve.h, V(ins))
            st[0].inc(act.dma_start(out[0, :, c].rearrange("(h p) n -> p h n", p=P), X[:, :, c]), 16)
        act.wait_ge(st[0].h, st[0].now())
        act.wait_ge(st[1].h, st[1].now())


def make_plan(a):
    plan = []

    def unit(w, group, per=0, tall=D // W512, at=0):
        return [(a[w], lambda it, j=j: it * (per * tall) + (at + group * tall + j)) for j in range(tall)]

    def rows(w, r0, tall, per=1):
        return [(a[w], lambda it, c=c: it * per + (c * tall + r0)) for c in range(4)]

    plan.append((1, unit("w_in", 0)))
    plan.append((2, unit("w_in", 1, 2) + unit("w_in", 2, 2)))
    plan.append((3, unit("w_in", 5, 2) + unit("w_in", 6, 2)))
    merge = [(1, unit("w_in", 11 + u)) for u in range(4)] + [(2, unit("w_in", 15 + 2 * u, 1)) for u in range(4)]
    plan.append(merge[0])
    plan += [(1, [(a["cmp_w1"], lambda it, n=4 * w + j: n) for j in range(4)]) for w in range(2)]
    plan += merge[1:]
    for group in (0, 2):
        plan.append((1, sum((unit("w_branch", group + u, 0, 2, 8 * m) for u in range(2) for m in range(3)), [])))

    def square(w):
        plan.append((1, unit(w, 0) + unit(w, 1)))
        plan.append((1, unit(w, 2) + unit(w, 3)))

    square("w_out")
    plan.append((1, unit("w_mlp_in", 0)))
    plan.append((15, unit("w_mlp_in", 1, 1) + rows("w_mlp_out", 0, 16)))
    plan.append((1, rows("w_mlp_out", 15, 16)))
    plan.append((1, unit("w_in_2", 0) + unit("w_in_2", 1)))
    plan.append((3, unit("w_in_2", 2, 2) + unit("w_in_2", 3, 2)))
    plan.append((1, unit("w_in_2", 8) + unit("w_in_2", 9)))
    plan.append((2, sum((unit("xattn_wkv", u, 4) for u in range(4)), [])))
    square("w_out_2")
    for u in range(4):
        plan.append((1, unit("xattn_wq_2", u)))
    plan.append((3, rows("xattn_wo_2", 0, 4)))
    plan.append((1, rows("xattn_wo_2", 3, 4)))

    def expert_step(e, per=0):
        down = [(a["w_down_2"], lambda it, c=c: it * per * 4 + (4 * (e - 1) + c)) for c in range(4)]
        return unit("w_gate_2", e, per) + unit("w_up_2", e, per) + (down if e else [])

    plan.append((1, expert_step(0)))
    plan.append((1, expert_step(1) + expert_step(2)))
    plan.append((N_EXP // 2 - 2, expert_step(3, 2) + expert_step(4, 2)))
    plan.append((1, expert_step(N_EXP - 1)))
    plan.append((1, [(a["w_down_2"], lambda it, c=c: 4 * (N_EXP - 1) + c) for c in range(4)]))
    return plan


def constants():
    dist = np.arange(512) - 256
    n = np.maximum(dist, 0)
    ratio = np.log(np.maximum(n, 1).astype(np.float32) / np.float32(16)) / np.float32(math.log(128 / 16))
    large = np.minimum(16 + (ratio * 16).astype(np.int32), 31)
    bucket = np.where(n < 16, n, large)
    onehot = np.zeros((34, 512), np.float32)
    onehot[bucket, np.arange(512)] = 1.0
    onehot[:32, dist < 0] = 0.0
    onehot[32] = dist < 0
    onehot[33] = dist >= 128
    onehot = np.ascontiguousarray(onehot[:, ::-1])
    maskrows = np.zeros((2, 24), np.float32)
    maskrows[0] = NEG
    maskrows[1, 8:16] = NEG
    t, s = np.arange(S)[None, :], np.arange(S)[:, None]
    band = np.stack([((t - s >= 0) & (t - s < w)) / np.minimum(t + 1, w) - (t == s) for w in (2, 4, 8, 16)]).astype(np.float32)
    q, k = np.arange(P)[None, :], np.arange(P)[:, None]
    levels = [(q // (2 * h) == k // (2 * h)) & (k % (2 * h) < h) & (q % (2 * h) >= h) for h in (64, 32, 16, 8, 4, 2, 1)]
    levels = np.stack(levels + [q == k]).astype(np.float32)
    return {"ident": np.eye(P, dtype=np.float32), "onehot": onehot, "maskrows": maskrows, "band": band,
            "levels": levels, "rank": np.array([[4, 3, 2, 1]], np.float32),
            "tri": (k <= q).astype(np.float32), "iota": np.arange(P, dtype=np.float32)[None]}


def by_feature(v):
    v = np.asarray(v)
    return v.reshape(-1, P).T


def tiled(w, rows=W512, cols=W512):
    w = np.asarray(w)
    w = w.reshape(-1, w.shape[-2] // rows, rows // P, P, w.shape[-1] // cols, cols)
    return w.transpose(0, 4, 1, 3, 2, 5).reshape(-1, P, rows // P * cols)


LAYOUT = {g: by_feature for g in ("pool_scale_2", "hgrn_lb_logits_2")}
LAYOUT.update({w: tiled for w in ("w_in", "w_branch", "w_out", "w_mlp_in", "w_mlp_out", "w_in_2", "xattn_wkv", "w_out_2",
                                  "xattn_wq_2", "xattn_wo_2", "w_gate_2", "w_up_2", "w_down_2")})
LAYOUT["cmp_w1"] = lambda w: tiled(w, 1024, 256)
LAYOUT["cmp_pos"] = lambda v: np.asarray(v)[0].transpose(0, 2, 1)


def kernel(**inputs):
    from concourse import bacc
    from concourse.bass_utils import run_bass_kernel_spmd

    nc = bacc.Bacc("TRN2", target_bir_lowering=False, num_devices=1)
    arrays, aps = {}, {}
    inputs["xattn_wkv"] = np.concatenate([np.asarray(inputs.pop(n))[0] for n in ("xattn_wk_2", "xattn_wv_2")], axis=1)
    w_in = np.asarray(inputs["w_in"])[0]
    inputs["w_in_gates"] = w_in[:, 2560:2584]
    inputs["w_in"] = np.concatenate([w_in[:, :2560], w_in[:, 2584:]], axis=1)
    inputs["norm_ffn_row"] = np.asarray(inputs["norm_ffn_2"])
    inputs["gains"] = np.concatenate([by_feature(inputs.pop(g)) for g in (
        "norm_mix", "norm_mlp", "norm_mix_2", "norm_xattn_2", "norm_mem_2", "norm_ffn_2")], axis=1)
    for name, value in {**inputs, **constants()}.items():
        v = np.ascontiguousarray(LAYOUT.get(name, np.asarray)(value))
        arrays[f"in_{name}"] = v
        aps[name] = nc.dram_tensor(f"in_{name}", v.shape, mybir.dt.from_np(v.dtype), kind="ExternalInput").ap()
    out = nc.dram_tensor("out", (1, S, D), F32, kind="ExternalOutput").ap()
    build(nc, aps, out)
    r = run_bass_kernel_spmd(nc, [arrays], core_ids=[0])
    return r.results[0]["out"]
```
